# Optimizing a Trainium2 kernel written in Bass

```python
import jax, jax.numpy as jnp
from jax import lax
import numpy as np

D_MODEL = 1024
BATCH = 1
SEQ = 1024
DEPTH = 1
DEC_BATCH = 8
DEC_SEQ = 8
PAST_LEN = 1024
PAGE_SIZE = 128

HEAD_DIM = 64
RWKV_HEADS = 4
RWKV_W = RWKV_HEADS * HEAD_DIM
W_LORA = 32
A_LORA = 32
G_LORA = 64
RWKV_PROJ = 3 * RWKV_W + W_LORA + A_LORA + G_LORA
GN_EPS = 64e-5
GMLP_GROUPS = 4
GMLP_W = GMLP_GROUPS * HEAD_DIM
CHUNK = 128
LN_EPS = 1e-5
SB_HEADS = 8
SB_W = SB_HEADS * HEAD_DIM
Q_BLOCK = 128
SB_BIAS_INIT = -6.0
D_MIX = RWKV_W + GMLP_W + SB_W
P_TOTAL = RWKV_PROJ + 2 * GMLP_W + 3 * SB_W
N_GROUPS = 4
EXPERTS_PER_GROUP = 4
N_EXPERTS = N_GROUPS * EXPERTS_PER_GROUP
TOP_K = 2
D_EXPERT = 256
N_MOD = 6
RMS_EPS = 1e-6

kernel_name = "hymba_rwkv7_gmlp_stickbreak_hmoe_step"

def rms_norm(x, g):
    x32 = x.astype(jnp.float32)
    y = x32 * lax.rsqrt(jnp.mean(x32 * x32, axis=-1, keepdims=True) + RMS_EPS)
    return (y * g.astype(jnp.float32)).astype(x.dtype)

def rwkv_step(S, inp):
    r, dec, k, v, a_vec, b_vec = inp
    Sa = jnp.einsum('bhij,bhj->bhi', S, a_vec)
    S = S * dec[:, :, None, :] + Sa[..., None] * b_vec[:, :, None, :] + v[..., None] * k[:, :, None, :]
    y = jnp.einsum('bhij,bhj->bhi', S, r)
    return S, y

def rwkv_mix(p, p_prev, S0, mu, w0, w_up, a0, a_up, g_up, k_k, k_a, r_k, ln_g, ln_b):
    B, T, _ = p.shape
    f32 = jnp.float32
    prev = jnp.concatenate([p_prev[:, None, :].astype(p.dtype), p[:, :-1]], axis=1)
    ps = p + mu * (prev - p)
    o = 3 * RWKV_W
    r = ps[..., 0:RWKV_W]
    k = ps[..., RWKV_W:2 * RWKV_W]
    v = ps[..., 2 * RWKV_W:o]
    wd = ps[..., o:o + W_LORA]
    ad = ps[..., o + W_LORA:o + W_LORA + A_LORA]
    gd = ps[..., o + W_LORA + A_LORA:]
    w = -jax.nn.softplus(-(w0 + jnp.tanh(wd) @ w_up).astype(f32)) - 0.5
    decay = jnp.exp(-jnp.exp(w))
    a = jax.nn.sigmoid((a0 + ad @ a_up).astype(f32))
    g = jax.nn.sigmoid(gd) @ g_up

    def heads(t):
        return t.astype(f32).reshape(B, T, RWKV_HEADS, HEAD_DIM)

    kk = heads(k * k_k)
    kk = kk * lax.rsqrt(jnp.maximum(jnp.sum(kk * kk, axis=-1, keepdims=True), 1e-24))
    ah = heads(a)
    kh = heads(k) * (1.0 + (ah - 1.0) * k_a.reshape(RWKV_HEADS, HEAD_DIM).astype(f32))
    rh, vh, dh = heads(r), heads(v), heads(decay)
    a_vec = -kk
    b_vec = kk * ah
    xs = tuple(jnp.swapaxes(t, 0, 1) for t in (rh, dh, kh, vh, a_vec, b_vec))
    S, y = lax.scan(rwkv_step, S0.astype(f32), xs)
    y = jnp.swapaxes(y, 0, 1)
    mean = jnp.mean(y, axis=-1, keepdims=True)
    var = jnp.mean(jnp.square(y - mean), axis=-1, keepdims=True)
    y = (y - mean) * lax.rsqrt(var + GN_EPS)
    y = y * ln_g.reshape(RWKV_HEADS, HEAD_DIM).astype(f32) + ln_b.reshape(RWKV_HEADS, HEAD_DIM).astype(f32)
    bonus = jnp.sum(rh * kh * r_k.astype(f32), axis=-1, keepdims=True) * vh
    out = ((y + bonus).reshape(B, T, RWKV_W) * g.astype(f32)).astype(p.dtype)
    return out, S.astype(S0.dtype), p[:, -1]

def gmlp_mix(u, v, ln_g, ln_b, ws, bs):
    B, T, _ = u.shape
    f32 = jnp.float32
    u = jax.nn.gelu(u)
    v = jax.nn.gelu(v).astype(f32).reshape(B, T, GMLP_GROUPS, HEAD_DIM)
    mean = jnp.mean(v, axis=-1, keepdims=True)
    var = jnp.mean(jnp.square(v - mean), axis=-1, keepdims=True)
    v = (v - mean) * lax.rsqrt(var + LN_EPS)
    v = v * ln_g.reshape(GMLP_GROUPS, HEAD_DIM).astype(f32) + ln_b.reshape(GMLP_GROUPS, HEAD_DIM).astype(f32)
    n_chunks = -(-T // CHUNK)
    pad = n_chunks * CHUNK - T
    vp = jnp.pad(v, ((0, 0), (0, pad), (0, 0), (0, 0))).reshape(B, n_chunks, CHUNK, GMLP_GROUPS, HEAD_DIM)
    wm = ws.astype(f32) * jnp.tril(jnp.ones((CHUNK, CHUNK), f32))
    mixed = jnp.einsum('gts,bnsgc->bntgc', wm, vp) + jnp.swapaxes(bs.astype(f32), 0, 1)[None, None, :, :, None]
    mixed = mixed.reshape(B, n_chunks * CHUNK, GMLP_W)[:, :T]
    y = (u.astype(f32) * mixed).astype(u.dtype)
    return y, v.reshape(B, T, GMLP_W).astype(u.dtype)

def sb_block(q, k, v, q_pos, k_pos, bias):
    f32 = jnp.float32
    z = jnp.einsum('bqhd,bkhd->bhqk', q.astype(f32), k.astype(f32)) * (HEAD_DIM ** -0.5)
    z = z + bias.astype(f32)[None, :, None, None]
    mask = k_pos[None, :] < q_pos[:, None]
    log_not = jnp.where(mask, jax.nn.log_sigmoid(-z), 0.0)
    shifted = jnp.concatenate([log_not[..., 1:], jnp.zeros_like(log_not[..., :1])], axis=-1)
    tail = lax.cumsum(shifted, axis=3, reverse=True)
    A = jnp.where(mask, jnp.exp(jax.nn.log_sigmoid(z) + tail), 0.0)
    return jnp.einsum('bhqk,bkhd->bqhd', A, v.astype(f32)).astype(q.dtype)

def sb_sweep(q, k_all, v_all, q_offset, bias):
    Tq = q.shape[1]
    outs = []
    for s0 in range(0, Tq, Q_BLOCK):
        s1 = min(s0 + Q_BLOCK, Tq)
        kend = q_offset + s1
        q_pos = q_offset + jnp.arange(s0, s1)
        k_pos = jnp.arange(kend)
        outs.append(sb_block(q[:, s0:s1], k_all[:, :kend], v_all[:, :kend], q_pos, k_pos, bias))
    return jnp.concatenate(outs, axis=1)

def hier_moe(h, rg_w, rg_b, re_w, re_b, wg, wu, wd):
    f32 = jnp.float32
    N = h.shape[0]
    pg = jax.nn.softmax((h @ rg_w + rg_b).astype(f32), axis=-1)
    pg_top, g_idx = lax.top_k(pg, 1)
    el = (h @ re_w + re_b).astype(f32).reshape(N, N_GROUPS, EXPERTS_PER_GROUP)
    el = jnp.take_along_axis(el, g_idx[:, :, None], axis=1)[:, 0]
    pe = jax.nn.softmax(el, axis=-1)
    pe_top, e_idx = lax.top_k(pe, TOP_K)
    pe_top = pe_top / jnp.sum(pe_top, axis=-1, keepdims=True)
    gate = pg_top * pe_top
    ids = g_idx * EXPERTS_PER_GROUP + e_idx
    dense_w = jnp.sum(jax.nn.one_hot(ids, N_EXPERTS, dtype=f32) * gate[..., None], axis=1)
    hid = jax.nn.silu(jnp.einsum('nd,edf->nef', h, wg)) * jnp.einsum('nd,edf->nef', h, wu)
    hid = hid * dense_w[:, :, None].astype(h.dtype)
    return jnp.einsum('nef,efd->nd', hid, wd)

def trunk_layer(x, c, lw, rwkv_S0, rwkv_shift0, past_k, past_v):
    B, T, _ = x.shape
    mod = (jax.nn.silu(c) @ lw['w_mod'] + lw['b_mod']).reshape(B, N_MOD, 1, D_MODEL)
    shift1, scale1, gate1, shift2, scale2, gate2 = (mod[:, i] for i in range(N_MOD))
    h = rms_norm(x, lw['norm1_g']) * (1.0 + scale1) + shift1
    p = h @ lw['w_in']
    o = RWKV_PROJ
    p_rwkv = p[..., :o]
    g_u = p[..., o:o + GMLP_W]
    g_v = p[..., o + GMLP_W:o + 2 * GMLP_W]
    o = o + 2 * GMLP_W
    q = p[..., o:o + SB_W].reshape(B, T, SB_HEADS, HEAD_DIM)
    k = p[..., o + SB_W:o + 2 * SB_W].reshape(B, T, SB_HEADS, HEAD_DIM)
    v = p[..., o + 2 * SB_W:o + 3 * SB_W].reshape(B, T, SB_HEADS, HEAD_DIM)

    y_rwkv, S_new, shift_new = rwkv_mix(p_rwkv, rwkv_shift0, rwkv_S0, lw['rwkv_mu'], lw['rwkv_w0'], lw['rwkv_w_up'],
                                        lw['rwkv_a0'], lw['rwkv_a_up'], lw['rwkv_g_up'], lw['rwkv_k_k'],
                                        lw['rwkv_k_a'], lw['rwkv_r_k'], lw['rwkv_ln_g'], lw['rwkv_ln_b'])
    y_gmlp, v_rows = gmlp_mix(g_u, g_v, lw['gmlp_ln_g'], lw['gmlp_ln_b'], lw['gmlp_ws'], lw['gmlp_bs'])
    if past_k is None:
        k_all, v_all, q_off = k, v, 0
    else:
        k_all = jnp.concatenate([past_k.astype(k.dtype), k], axis=1)
        v_all = jnp.concatenate([past_v.astype(v.dtype), v], axis=1)
        q_off = past_k.shape[1]
    y_sb = sb_sweep(q, k_all, v_all, q_off, lw['sb_bias']).reshape(B, T, SB_W)

    mixed = jnp.concatenate([y_rwkv, y_gmlp, y_sb], axis=-1) @ lw['w_out']
    x = x + gate1 * mixed
    h2 = rms_norm(x, lw['norm2_g']) * (1.0 + scale2) + shift2
    moe = hier_moe(h2.reshape(B * T, D_MODEL), lw['router_g_w'], lw['router_g_b'], lw['router_e_w'],
                   lw['router_e_b'], lw['exp_wg'], lw['exp_wu'], lw['exp_wd']).reshape(B, T, D_MODEL)
    x = x + gate2 * moe
    return x, S_new, shift_new, k, v, v_rows

def setup_inputs(seed: int = 0) -> dict:
    key = jax.random.key(seed)
    ks = iter(jax.random.split(key, 64))
    f32 = jnp.float32

    def nrm(shape, scale=1.0):
        return scale * jax.random.normal(next(ks), shape, f32)

    n_pages = PAST_LEN // PAGE_SIZE
    n_pool = (DEC_BATCH * n_pages * 5) // 4
    x_prompt = nrm((BATCH, SEQ, D_MODEL))
    x_sample = nrm((DEC_BATCH, DEC_SEQ, D_MODEL))
    cache_k = nrm((DEPTH, n_pool, PAGE_SIZE, SB_HEADS, HEAD_DIM))
    cache_v = nrm((DEPTH, n_pool, PAGE_SIZE, SB_HEADS, HEAD_DIM))
    page_table = jax.random.permutation(next(ks), n_pool)[:DEC_BATCH * n_pages].reshape(DEC_BATCH, n_pages).astype(jnp.int32)
    state_rwkv = nrm((DEPTH, DEC_BATCH, RWKV_HEADS, HEAD_DIM, HEAD_DIM), 0.1)
    state_rwkv_shift = nrm((DEPTH, DEC_BATCH, RWKV_PROJ))
    c_prompt = nrm((BATCH, D_MODEL))
    c_sample = nrm((DEC_BATCH, D_MODEL))
    b_mod = nrm((DEPTH, N_MOD, D_MODEL), 0.02).at[:, 2].add(1.0).at[:, 5].add(1.0).reshape(DEPTH, N_MOD * D_MODEL)
    return {
        'x_prompt': x_prompt,
        'x_sample': x_sample,
        'cache_k': cache_k,
        'cache_v': cache_v,
        'page_table': page_table,
        'state_rwkv': state_rwkv,
        'state_rwkv_shift': state_rwkv_shift,
        'c_prompt': c_prompt,
        'c_sample': c_sample,
        'norm1_g': 1.0 + nrm((DEPTH, D_MODEL), 0.02),
        'norm2_g': 1.0 + nrm((DEPTH, D_MODEL), 0.02),
        'w_mod': nrm((DEPTH, D_MODEL, N_MOD * D_MODEL), 0.1 * D_MODEL ** -0.5),
        'b_mod': b_mod,
        'w_in': nrm((DEPTH, D_MODEL, P_TOTAL), D_MODEL ** -0.5),
        'rwkv_mu': jax.random.uniform(next(ks), (DEPTH, RWKV_PROJ), f32),
        'rwkv_w0': jax.random.uniform(next(ks), (DEPTH, RWKV_W), f32, -6.5, -1.5),
        'rwkv_w_up': nrm((DEPTH, W_LORA, RWKV_W), 0.1),
        'rwkv_a0': nrm((DEPTH, RWKV_W), 0.1),
        'rwkv_a_up': nrm((DEPTH, A_LORA, RWKV_W), 0.1),
        'rwkv_g_up': nrm((DEPTH, G_LORA, RWKV_W), G_LORA ** -0.5),
        'rwkv_k_k': 0.85 + nrm((DEPTH, RWKV_W), 0.02),
        'rwkv_k_a': 1.0 + nrm((DEPTH, RWKV_W), 0.02),
        'rwkv_r_k': nrm((DEPTH, RWKV_HEADS, HEAD_DIM), 0.1),
        'rwkv_ln_g': 1.0 + nrm((DEPTH, RWKV_W), 0.02),
        'rwkv_ln_b': nrm((DEPTH, RWKV_W), 0.01),
        'gmlp_ln_g': 1.0 + nrm((DEPTH, GMLP_W), 0.02),
        'gmlp_ln_b': nrm((DEPTH, GMLP_W), 0.01),
        'gmlp_ws': nrm((DEPTH, GMLP_GROUPS, CHUNK, CHUNK), CHUNK ** -0.5),
        'gmlp_bs': 1.0 + nrm((DEPTH, GMLP_GROUPS, CHUNK), 0.02),
        'sb_bias': SB_BIAS_INIT + nrm((DEPTH, SB_HEADS), 0.3),
        'w_out': nrm((DEPTH, D_MIX, D_MODEL), D_MIX ** -0.5),
        'router_g_w': nrm((DEPTH, D_MODEL, N_GROUPS), D_MODEL ** -0.5),
        'router_g_b': nrm((DEPTH, N_GROUPS), 0.01),
        'router_e_w': nrm((DEPTH, D_MODEL, N_EXPERTS), D_MODEL ** -0.5),
        'router_e_b': nrm((DEPTH, N_EXPERTS), 0.01),
        'exp_wg': nrm((DEPTH, N_EXPERTS, D_MODEL, D_EXPERT), D_MODEL ** -0.5),
        'exp_wu': nrm((DEPTH, N_EXPERTS, D_MODEL, D_EXPERT), D_MODEL ** -0.5),
        'exp_wd': nrm((DEPTH, N_EXPERTS, D_EXPERT, D_MODEL), D_EXPERT ** -0.5),
        'final_g': 1.0 + nrm((D_MODEL,), 0.02),
    }

def reference(x_prompt, x_sample, cache_k, cache_v, page_table, state_rwkv, state_rwkv_shift, c_prompt, c_sample,
              norm1_g, norm2_g, w_mod, b_mod, w_in, rwkv_mu, rwkv_w0, rwkv_w_up, rwkv_a0, rwkv_a_up, rwkv_g_up,
              rwkv_k_k, rwkv_k_a, rwkv_r_k, rwkv_ln_g, rwkv_ln_b, gmlp_ln_g, gmlp_ln_b, gmlp_ws, gmlp_bs, sb_bias,
              w_out, router_g_w, router_g_b, router_e_w, router_e_b, exp_wg, exp_wu, exp_wd, final_g):
    B = x_prompt.shape[0]
    DB = x_sample.shape[0]
    n_pages = page_table.shape[1]
    xp, xs = x_prompt, x_sample
    kp_l, vp_l, ks_l, vs_l = [], [], [], []
    Sp_l, shp_l, Ss_l, shs_l, gv_l = [], [], [], [], []
    for l in range(DEPTH):
        lw = dict(norm1_g=norm1_g[l], norm2_g=norm2_g[l], w_mod=w_mod[l], b_mod=b_mod[l], w_in=w_in[l],
                  rwkv_mu=rwkv_mu[l], rwkv_w0=rwkv_w0[l], rwkv_w_up=rwkv_w_up[l], rwkv_a0=rwkv_a0[l],
                  rwkv_a_up=rwkv_a_up[l], rwkv_g_up=rwkv_g_up[l], rwkv_k_k=rwkv_k_k[l], rwkv_k_a=rwkv_k_a[l],
                  rwkv_r_k=rwkv_r_k[l], rwkv_ln_g=rwkv_ln_g[l], rwkv_ln_b=rwkv_ln_b[l], gmlp_ln_g=gmlp_ln_g[l],
                  gmlp_ln_b=gmlp_ln_b[l], gmlp_ws=gmlp_ws[l], gmlp_bs=gmlp_bs[l], sb_bias=sb_bias[l],
                  w_out=w_out[l], router_g_w=router_g_w[l], router_g_b=router_g_b[l], router_e_w=router_e_w[l],
                  router_e_b=router_e_b[l], exp_wg=exp_wg[l], exp_wu=exp_wu[l], exp_wd=exp_wd[l])
        S0 = jnp.zeros((B, RWKV_HEADS, HEAD_DIM, HEAD_DIM), xp.dtype)
        sh0 = jnp.zeros((B, RWKV_PROJ), xp.dtype)
        xp, Sp, shp, kp, vp, _ = trunk_layer(xp, c_prompt, lw, S0, sh0, None, None)
        past_k = cache_k[l][page_table].reshape(DB, n_pages * PAGE_SIZE, SB_HEADS, HEAD_DIM)
        past_v = cache_v[l][page_table].reshape(DB, n_pages * PAGE_SIZE, SB_HEADS, HEAD_DIM)
        xs, Ss, shs, ksm, vsm, gv = trunk_layer(xs, c_sample, lw, state_rwkv[l], state_rwkv_shift[l], past_k, past_v)
        kp_l.append(kp); vp_l.append(vp); ks_l.append(ksm); vs_l.append(vsm)
        Sp_l.append(Sp); shp_l.append(shp); Ss_l.append(Ss); shs_l.append(shs); gv_l.append(gv)
    y_prompt = rms_norm(xp, final_g)
    y_sample = rms_norm(xs, final_g)
    return (y_prompt, y_sample, jnp.stack(kp_l), jnp.stack(vp_l), jnp.stack(ks_l), jnp.stack(vs_l),
            jnp.stack(Sp_l), jnp.stack(shp_l), jnp.stack(Ss_l), jnp.stack(shs_l), jnp.stack(gv_l))


_drawn_inputs = setup_inputs


def setup_inputs(seed=0):
    import zlib

    import numpy as np

    out = dict(_drawn_inputs(seed))
    spreads = {}
    factors = {'rwkv_k_a': 2.732,
     'rwkv_ln_g': 13.311,
     'rwkv_ln_b': 28.096,
     'gmlp_ln_g': 9.445,
     'gmlp_ln_b': 18.769,
     'gmlp_bs': 15.047,
     'router_g_b': 29.675,
     'router_e_b': 18.908,
     'final_g': 23.597,
     'norm2_g': 4.328,
     'sb_bias': 30.856,
     'cache_k': 8.0,
     'cache_v': 8.0}
    for name, (base, spread) in spreads.items():
        noise = np.random.default_rng([zlib.crc32(name.encode()), seed]).standard_normal(out[name].shape)
        drawn = base * np.exp(spread * noise) if base else spread * noise
        out[name] = __import__('jax').numpy.asarray(drawn.astype(out[name].dtype))
    for name, factor in factors.items():
        out[name] = (out[name] * factor).astype(out[name].dtype)
    return out
```

```python
from contextlib import ExitStack

import numpy as np

import concourse.bass as bass
from concourse import mybir

F32 = mybir.dt.float32
I32 = mybir.dt.int32
U32 = mybir.dt.uint32
ALU = mybir.AluOpType
ACT = mybir.ActivationFunctionType
AXX = mybir.AxisListType.X

P = 128
D = 1024
KT = D // P
SEQ, SB, ST = 1024, 8, 8
NS = SB * ST
TOK = SEQ + NS
NT = SEQ // P
COLS = ((0, 512), (512, 1024), (1024, TOK))
HD = 64
RW, RH = 256, 4
RPROJ = 896
RF = RPROJ // P
GW, GG = 256, 4
SBW, SH = 512, 8
OG = RPROJ
OQ = OG + 2 * GW
PAGE, NPAGE = 128, 8
NE, DE, NGR = 16, 256, 4
ET = (2 * TOK + NE * (P - 1)) // P
C = 64
NC = SEQ // C
RMS_EPS, GN_EPS, LN_EPS = 1e-6, 64e-5, 1e-5
DECAY = float(np.exp(-0.5))


def each(eng, n, body, unroll=2):
    full = n // unroll
    if full > 1:
        with eng.Fori(0, full) as i:
            for u in range(unroll):
                body(i * unroll + u, u, i)
    else:
        for t in range(full * unroll):
            body(t, t % unroll, t // unroll)
    for t in range(full * unroll, n):
        body(t, t % unroll, t // unroll)


def ahead(eng, n, front, back, lead=1, back_first=False):
    looped = (n - 1 - lead) // 2 * 2
    for t in range(lead):
        front(t, t % 2, t // 2)

    def both(t, u, r):
        if back_first:
            back(t, u, r)
        front(t + lead, (u + lead) % 2, r + (u + lead) // 2)
        if not back_first:
            back(t, u, r)

    each(eng, looped, both)
    for t in range(looped, n - lead):
        both(t, t % 2, t // 2)
    for t in range(n - lead, n):
        back(t, t % 2, t // 2)


def wait_apart(eng, sem, value, passed):
    eng.wait_ge(sem, value)
    eng.sem_inc(passed, 1)


class Phase:

    def __init__(self, nc, name):
        self.nc, self.name, self.ctx = nc, name, ExitStack()
        self.semaphores = []

    def __enter__(self):
        return self

    def __exit__(self, *_):
        if self.semaphores:
            self.nc.clear_and_free_semaphores(self.semaphores)
            self.nc.all_engine_barrier()
        self.ctx.close()

    def sb(self, name, shape, dt=F32):
        return self.ctx.enter_context(self.nc.sbuf_tensor(f"{self.name}_{name}", shape, dt))

    def ps(self, name, shape, dt=F32):
        return self.ctx.enter_context(self.nc.psum_tensor(f"{self.name}_{name}", shape, dt))

    def sem(self, name):
        self.semaphores.append(self.nc.alloc_semaphore(name=f"{self.name}_{name}"))
        return self.semaphores[-1]


def bc(ap, axis, n):
    return ap.unsqueeze(axis).to_broadcast([*ap.shape[:axis], n, *ap.shape[axis:]])


def constants(nc, ph, keep):
    ident, head_ones, neg_from, neg_ones = (keep[k] for k in ("ident", "head_ones", "neg_from", "neg_ones"))
    built = ph.sem("const_built")

    def build(pool):
        def fill(ap, value):
            nc.gpsimd.memset(ap, value).then_inc(built, 1)

        for at, half in enumerate((0, HD)):
            fill(head_ones[half:half + HD, half:half + HD], 1.0)
            pool.wait_ge(built, 2 * at + 1)
            fill(head_ones[half:half + HD, HD - half:P - half], 0.0)
            pool.wait_ge(built, 2 * at + 2)
        fill(ident[:, :], 0.0)
        fill(neg_from[:, :], -1.0)
        fill(neg_ones[:, :], -1.0)
        pool.wait_ge(built, 7)
        nc.gpsimd.affine_select(out=ident[:, :], in_=ident[:, :], compare_op=ALU.not_equal, fill=1.0,
                                base=0, pattern=[[-1, P]], channel_multiplier=1).then_inc(built, 1)
        nc.gpsimd.affine_select(out=neg_from[:, :], in_=neg_from[:, :], compare_op=ALU.is_ge, fill=0.0,
                                base=0, pattern=[[-1, P]], channel_multiplier=1).then_inc(built, 1)
        pool.wait_ge(built, 9)

    return build, built


def modulation(nc, T, keep, mod_rows):
    W, NM, WC = 3, 6 * D, 512
    R = SB + 1
    w_view = T["w_mod"].rearrange("(k p) n -> p k n", p=P)
    with Phase(nc, "mod") as ph:
        c_in, c_act = ph.sb("c_in", [R, D]), ph.sb("c_act", [R, D])
        c_T = ph.sb("c_T", [P, KT, R])
        w = ph.sb("w", [P, W, KT, WC])
        bias, rows = ph.sb("bias", [R, NM]), ph.sb("sums", [R, NM])
        ps_T = ph.ps("ps_T", [P, KT, R])
        ps = ph.ps("ps", [P, W, WC])
        build, built = constants(nc, ph, keep)
        c_loaded, b_loaded, silu_done, cT_ready = (ph.sem(x) for x in ("c_loaded", "b_loaded", "silu_done", "cT_ready"))
        c_turned = ph.sem("c_turned")
        w_loaded = [ph.sem(f"w_loaded{u}") for u in range(W)]
        prod_done, row_done, stored = ph.sem("prod_done"), ph.sem("row_done"), ph.sem("stored")
        with nc.Block() as block:
            @block.gpsimd
            def _(pool):
                build(pool)

            @block.sync
            def _(sp):
                sp.dma_start(c_in[0:SB, :], T["c_sample"]).then_inc(c_loaded, 16)
                sp.dma_start(c_in[SB:R, :], T["c_prompt"]).then_inc(c_loaded, 16)
                sp.dma_start(bias[:, :], T["b_mod"].to_broadcast([R, NM])).then_inc(b_loaded, 16)

                def load(n, u, r):
                    sp.wait_ge(prod_done, n + 1)
                    sp.dma_start(w[:, u, :, :], w_view[:, :, bass.ds(n * WC, WC)]).then_inc(w_loaded[u], 16)

                each(sp, NM // WC, load, W)
                sp.wait_ge(row_done, NM // WC + W)
                sp.dma_start(mod_rows, rows[:, :]).then_inc(stored, 16)
                sp.wait_ge(stored, 16)

            @block.scalar
            def _(act):
                act.wait_ge(c_loaded, 32)
                nc.scalar.activation(c_act[:, :], c_in[:, :], ACT.Silu).then_inc(silu_done, 1)

            @block.tensor
            def _(pe):
                pe.sem_inc(prod_done, W)
                pe.wait_ge(built, 9)
                pe.wait_ge(silu_done, 1)
                for k in range(KT):
                    last = nc.tensor.transpose(ps_T[:, k, :], c_act[:, k * P:(k + 1) * P], keep["ident"][0:R, 0:R])
                last.then_inc(c_turned, 1)
                pe.wait_ge(cT_ready, 1)

                def product(n, u, r):
                    pe.wait_ge(w_loaded[u], r * 16 + 16)
                    pe.wait_ge(row_done, n + 1)
                    for k in range(KT):
                        last = nc.tensor.matmul(ps[0:R, u, :], c_T[:, k, :], w[:, u, k, :],
                                                start=(k == 0), stop=(k == KT - 1))
                    last.then_inc(prod_done, 1)

                each(pe, NM // WC, product, W)

            @block.vector
            def _(dve):
                dve.sem_inc(row_done, W)
                dve.wait_ge(c_turned, 1)
                nc.vector.tensor_copy(c_T[:, :, :], ps_T[:, :, :]).then_inc(cT_ready, 1)
                dve.wait_ge(b_loaded, 16)

                def add_bias(n, u, r):
                    dve.wait_ge(prod_done, W + n + 1)
                    nc.vector.tensor_tensor(rows[:, bass.ds(n * WC, WC)], ps[0:R, u, :],
                                            bias[:, bass.ds(n * WC, WC)], ALU.add).then_inc(row_done, 1)

                each(dve, NM // WC, add_bias, W)


def rows_of(n):
    return NS if isinstance(n, int) and n == NT else P


def load_mod(sp, dst_prompt, dst_sample, mod_rows, what, loaded):
    cols = slice(what * D, (what + 1) * D)
    sp.dma_start(dst_prompt, mod_rows[SB:SB + 1, cols].to_broadcast([P, D])).then_inc(loaded, 16)
    for b in range(SB):
        sp.dma_start(dst_sample[b * ST:(b + 1) * ST, :],
                     mod_rows[b:b + 1, cols].to_broadcast([ST, D])).then_inc(loaded, 16)


MOD_LOADS = 16 * (SB + 1)


def norm1(nc, T, keep, mod_rows):
    hT, v_sb, v_g = keep["hT"], keep["v_sb"], keep["v_g"]
    w_view = T["w_in"].rearrange("(k p) n -> p k n", p=P)
    x_tiles = T["x_prompt"].rearrange("(n p) d -> n p d", p=P)
    with Phase(nc, "n1") as ph:
        x, h = ph.sb("x", [P, 2, D]), ph.sb("h", [P, 2, D])
        squares = ph.sb("squares", [P, 2, D])
        ht = ph.sb("ht", [P, 2, KT, P])
        gain = {"p": ph.sb("gain_p", [P, D]), "s": ph.sb("gain_s", [NS, D])}
        shift = {"p": ph.sb("shift_p", [P, D]), "s": ph.sb("shift_s", [NS, D])}
        g = ph.sb("g", [P, D])
        wv = ph.sb("wv", [P, KT, GW + SBW])
        ss, ms, rt, rstd = (ph.sb(x_, [P, 2]) for x_ in ("ss", "ms", "rt", "rstd"))
        ps_h = ph.ps("ps_h", [P, 2, KT, P])
        ps_v = ph.ps("ps_v", [P, 2, 1024])
        (mod_loaded, wv_loaded, x_free, sq_done, ms_done, rt_done, rstd_done, scaled, h_done, turned, ht_ready,
         copied, v_done, v_kept, gains, stored) = (ph.sem(x_) for x_ in (
             "mod_loaded", "wv_loaded", "x_free", "sq_done", "ms_done", "rt_done", "rstd_done", "scaled", "h_done",
             "turned", "ht_ready", "copied", "v_done", "v_kept", "gains", "stored"))
        x_loaded = [ph.sem(f"x_loaded{u}") for u in range(2)]
        with nc.Block() as block:
            @block.sync
            def _(sp):
                sp.dma_start(g[:, :], T["norm1_g"].to_broadcast([P, D])).then_inc(mod_loaded, 16)
                load_mod(sp, gain["p"][:, :], gain["s"], mod_rows, 1, mod_loaded)
                load_mod(sp, shift["p"][:, :], shift["s"], mod_rows, 0, mod_loaded)

                def load(n, u, r):
                    sp.wait_ge(x_free, n + 1)
                    src = T["x_sample"] if rows_of(n) == NS else x_tiles[bass.ds(n, 1), :, :].squeeze(0)
                    sp.dma_start(x[0:rows_of(n), u, :], src).then_inc(x_loaded[u], 16)

                each(sp, NT + 1, load)
                sp.wait_ge(v_kept, 2 * (NT + 1) + 4)
                sp.dma_start(T["v_prompt"].rearrange("(n p) c -> p n c", p=P), v_sb[:, 0:NT, :]).then_inc(stored, 16)
                sp.dma_start(T["v_sample"], v_sb[0:NS, NT, :]).then_inc(stored, 16)
                sp.wait_ge(stored, 32)

            @block.scalar
            def _(act):
                act.dma_start(wv[:, :, 0:GW], w_view[:, :, OG + GW:OG + 2 * GW]).then_inc(wv_loaded, 16)
                act.dma_start(wv[:, :, GW:], w_view[:, :, OQ + 2 * SBW:OQ + 3 * SBW]).then_inc(wv_loaded, 16)

                act.sem_inc(ht_ready, 2)

                def stats(n, u, r):
                    m = rows_of(n)
                    act.wait_ge(x_loaded[u], r * 16 + 16)
                    nc.scalar.activation(squares[0:m, u, :], x[0:m, u, :], ACT.Square,
                                         accum_out=ss[0:m, u:u + 1]).then_inc(sq_done, 1)
                    act.wait_ge(ms_done, n + 1)
                    nc.scalar.activation(rt[0:m, u:u + 1], ms[0:m, u:u + 1], ACT.Sqrt).then_inc(rt_done, 1)

                def evacuate(n, u, r):
                    m = rows_of(n)
                    act.wait_ge(turned, n + 3)
                    act.wait_ge(copied, n + 1)
                    act.wait_ge(v_done, n + 1)
                    nc.scalar.activation(ht[:, u, :, 0:m], ps_h[:, u, :, 0:m], ACT.Copy).then_inc(ht_ready, 1)

                ahead(act, NT + 1, stats, evacuate)

            @block.gpsimd
            def _(pool):
                pool.sem_inc(copied, 2)

                def copy(n, u, r):
                    m = rows_of(n)
                    pool.wait_ge(ht_ready, n + 3)
                    nc.gpsimd.tensor_copy(hT[:, :, bass.ds(n * P, m)], ht[:, u, :, 0:m]).then_inc(copied, 1)

                each(pool, NT + 1, copy)

            @block.vector
            def _(dve):
                dve.sem_inc(x_free, 2)
                dve.sem_inc(v_kept, 4)
                dve.wait_ge(mod_loaded, 16 + 2 * MOD_LOADS)
                nc.vector.scalar_tensor_tensor(gain["p"][:, :], gain["p"][:, :], 1.0, g[:, :],
                                               ALU.add, ALU.mult).then_inc(gains, 1)
                nc.vector.scalar_tensor_tensor(gain["s"][:, :], gain["s"][:, :], 1.0, g[0:NS, :],
                                               ALU.add, ALU.mult).then_inc(gains, 1)
                dve.wait_ge(gains, 2)

                def norm(n, u, r):
                    m = rows_of(n)
                    group = "s" if m == NS else "p"
                    dve.wait_ge(sq_done, n + 1)
                    nc.vector.tensor_scalar(ms[0:m, u:u + 1], ss[0:m, u:u + 1], 1.0 / D, RMS_EPS,
                                            ALU.mult, ALU.add).then_inc(ms_done, 1)
                    dve.wait_ge(rt_done, n + 1)
                    nc.vector.reciprocal(rstd[0:m, u:u + 1], rt[0:m, u:u + 1]).then_inc(rstd_done, 1)
                    dve.wait_ge(rstd_done, n + 1)
                    dve.wait_ge(turned, n + 1)
                    nc.vector.scalar_tensor_tensor(h[0:m, u, :], x[0:m, u, :], rstd[0:m, u:u + 1], gain[group][0:m, :],
                                                   ALU.mult, ALU.mult).then_inc(x_free, 1)
                    dve.wait_ge(x_free, n + 3)
                    nc.vector.tensor_tensor(h[0:m, u, :], h[0:m, u, :], shift[group][0:m, :],
                                            ALU.add).then_inc(h_done, 1)

                def keep_v(n, u, r):
                    m = rows_of(n)
                    dve.wait_ge(v_done, n + 3)
                    nc.vector.tensor_copy(v_g[0:m, bass.ds(n, 1), :].squeeze(1), ps_v[0:m, u, 0:GW]).then_inc(v_kept, 1)
                    nc.vector.tensor_copy(v_sb[0:m, bass.ds(n, 1), :].squeeze(1),
                                          ps_v[0:m, u, 512:1024]).then_inc(v_kept, 1)

                ahead(dve, NT + 1, norm, keep_v, lead=2)

            @block.tensor
            def _(pe):
                pe.sem_inc(turned, 2)
                pe.sem_inc(v_done, 2)

                def turn(n, u, r):
                    m = rows_of(n)
                    pe.wait_ge(h_done, n + 1)
                    pe.wait_ge(ht_ready, n + 1)
                    for k in range(KT):
                        last = nc.tensor.transpose(ps_h[:, u, k, 0:m], h[0:m, u, k * P:(k + 1) * P],
                                                   keep["ident"][0:m, 0:m])
                    last.then_inc(turned, 1)

                def project(n, u, r):
                    m = rows_of(n)
                    pe.wait_ge(wv_loaded, 32)
                    pe.wait_ge(ht_ready, n + 3)
                    pe.wait_ge(v_kept, 2 * n + 2)
                    for col, lo, hi in ((0, 0, GW), (512, GW, GW + SBW)):
                        for k in range(KT):
                            last = nc.tensor.matmul(ps_v[0:m, u, col:col + hi - lo], ht[:, u, k, 0:m], wv[:, k, lo:hi],
                                                    start=(k == 0), stop=(k == KT - 1))
                    last.then_inc(v_done, 1)

                ahead(pe, NT + 1, turn, project)


BUILT = 2 * (2 * 4 + 1 + 4 + 1)
LN_STEPS = 20
CLIP = 20.0
STEPS = 21


def rwkv_project(nc, T, keep):
    hT, R = keep["hT"], keep["R"]
    w_view = T["w_in"].rearrange("(k p) n -> p k n", p=P)
    with Phase(nc, "rp") as ph:
        w = ph.sb("w", [P, 2, KT, P])
        p_at = ph.sb("p_at", [P, 2, 1 + TOK])
        diff = ph.sb("diff", [P, 2, TOK])
        mu = ph.sb("mu", [P, RF])
        carried, carried_T = ph.sb("carried", [SB, RPROJ]), ph.sb("carried_T", [P, RF, SB])
        lasts, last_rows = ph.sb("lasts", [P, RF, SB + 1]), ph.sb("last_rows", [SB + 1, RF, P])
        ps = ph.ps("ps", [P, 2, 1536])
        ps_c, ps_l = ph.ps("ps_c", [P, RF, SB]), ps[0:SB + 1, 1, :]
        (small_loaded, zeroed, carried_turned, carried_kept, projected, p_kept, diffed, fixed, mixed, lasts_kept,
         lasts_turned, rows_kept, stored) = (ph.sem(x_) for x_ in (
             "small_loaded", "zeroed", "carried_turned", "carried_kept", "projected", "p_kept", "diffed", "fixed",
             "mixed", "lasts_kept", "lasts_turned", "rows_kept", "stored"))
        w_loaded = [ph.sem(f"w_loaded{u}") for u in range(2)]
        with nc.Block() as block:
            @block.sync
            def _(sp):
                sp.dma_start(carried[:, :], T["state_rwkv_shift"]).then_inc(small_loaded, 16)
                with nc.allow_non_contiguous_dma(reason="one scalar per feature"):
                    sp.dma_start(mu[:, :], T["rwkv_mu"].rearrange("a (f p) -> p (a f)", p=P)).then_inc(small_loaded, 16)

                def load(n, u, r):
                    sp.wait_ge(projected, n + 1)
                    sp.dma_start(w[:, u, :, :], w_view[:, :, bass.ds(n * P, P)]).then_inc(w_loaded[u], 16)

                each(sp, RF, load)
                sp.wait_ge(rows_kept, 1)
                rows = last_rows[:, :, :].rearrange("b f p -> b (f p)")
                sp.dma_start(T["shift_prompt"], rows[0:1, :]).then_inc(stored, 16)
                sp.dma_start(T["shift_sample"], rows[1:SB + 1, :]).then_inc(stored, 16)
                sp.wait_ge(stored, 32)

            @block.tensor
            def _(pe):
                pe.sem_inc(projected, 2)
                pe.wait_ge(small_loaded, 32)
                for f in range(RF):
                    last = nc.tensor.transpose(ps_c[:, f, :], carried[:, f * P:(f + 1) * P], keep["ident"][0:SB, 0:SB])
                last.then_inc(carried_turned, 1)

                def project(n, u, r):
                    pe.wait_ge(w_loaded[u], r * 16 + 16)
                    pe.wait_ge(p_kept, n + 1)
                    for lo, hi in COLS:
                        for k in range(KT):
                            last = nc.tensor.matmul(ps[:, u, lo:hi], w[:, u, k, :], hT[:, k, lo:hi],
                                                    start=(k == 0), stop=(k == KT - 1))
                    last.then_inc(projected, 1)

                each(pe, RF, project)
                pe.wait_ge(lasts_kept, RF + 2)
                for f in range(RF):
                    last = nc.tensor.transpose(ps_l[:, f * P:(f + 1) * P], lasts[:, f, :], keep["ident"][:, :])
                last.then_inc(lasts_turned, 1)

            @block.scalar
            def _(act):
                act.sem_inc(p_kept, 2)
                act.wait_ge(carried_turned, 1)
                nc.scalar.activation(carried_T[:, :, :], ps_c[:, :, :], ACT.Copy).then_inc(carried_kept, 1)
                act.wait_ge(zeroed, 1)

                def evacuate(n, u, r):
                    act.wait_ge(projected, n + 3)
                    act.wait_ge(mixed, n + 1)
                    act.wait_ge(lasts_kept, n + 1)
                    nc.scalar.activation(p_at[:, u, 1:], ps[:, u, 0:TOK], ACT.Copy).then_inc(p_kept, 1)

                each(act, RF, evacuate)
                act.wait_ge(lasts_turned, 1)
                nc.scalar.activation(last_rows[:, :, :].rearrange("b f p -> b (f p)"), ps_l[:, 0:RPROJ],
                                     ACT.Copy).then_inc(rows_kept, 1)

            @block.gpsimd
            def _(pool):
                pool.sem_inc(lasts_kept, 2)

                def keep_last(n, u, r):
                    pool.wait_ge(p_kept, n + 3)
                    nc.gpsimd.tensor_copy(lasts[:, bass.ds(n, 1), :].squeeze(1),
                                          p_at[:, u, SEQ:1 + TOK:ST]).then_inc(lasts_kept, 1)

                each(pool, RF, keep_last)

            @block.vector
            def _(dve):
                dve.sem_inc(mixed, 2)
                nc.vector.memset(p_at[:, :, 0:1], 0.0).then_inc(zeroed, 1)
                dve.wait_ge(carried_kept, 1)

                def mix(n, u, r):
                    dve.wait_ge(p_kept, n + 3)
                    nc.vector.tensor_tensor(diff[:, u, :], p_at[:, u, 0:TOK], p_at[:, u, 1:],
                                            ALU.subtract).then_inc(diffed, 1)
                    dve.wait_ge(diffed, n + 1)
                    nc.vector.tensor_tensor(diff[:, u, SEQ::ST], carried_T[:, bass.ds(n, 1), :].squeeze(1),
                                            p_at[:, u, 1 + SEQ::ST], ALU.subtract).then_inc(fixed, 1)
                    dve.wait_ge(fixed, n + 1)
                    nc.vector.scalar_tensor_tensor(R[:, bass.ds(n, 1), :].squeeze(1), diff[:, u, :],
                                                   mu[:, bass.ds(n, 1)], p_at[:, u, 1:],
                                                   ALU.mult, ALU.add).then_inc(mixed, 1)

                each(dve, RF, mix)


def rwkv_prepare(nc, T, keep):
    R, B, mT, ends, head_ones = keep["R"], keep["B"], keep["mT"], keep["ends"], keep["head_ones"]
    with Phase(nc, "rq") as ph:
        t_w, t_a, t_l, t_k, t_e = (ph.sb(x_, [P, TOK]) for x_ in ("t_w", "t_a", "t_l", "t_k", "t_e"))
        t_x, t_y = mT[:, 6, :], mT[:, 7, :]
        inside = ph.sb("inside", [P, TOK])
        up = ph.sb("up", [P, RW])
        gd = ph.sb("gd", [P, TOK])
        cols = {x_: ph.sb(x_, [P, 2]) for x_ in ("w0", "a0", "k_k", "k_a", "r_k", "k_0")}
        ps_w, ps_a = ph.ps("ps_w", [P, 1536]), ph.ps("ps_a", [P, 1536])
        (loaded, masked, lora_in, w_up, a_up, g_up, w_sig, a_sig, g_kept, squared, sums, did) = (ph.sem(x_) for x_ in (
            "loaded", "masked", "lora_in", "w_up", "a_up", "g_up", "w_sig", "a_sig", "g_kept", "squared", "sums", "did"))
        rooted, exp_l, exp_nl, exp_p, ranked, bonus_sum, const = (ph.sem(x_) for x_ in (
            "rooted", "exp_l", "exp_nl", "exp_p", "ranked", "bonus_sum", "const"))
        with nc.Block() as block:
            @block.sync
            def _(sp):
                with nc.allow_non_contiguous_dma(reason="one scalar per feature"):
                    for x_, name in (("w0", "rwkv_w0"), ("a0", "rwkv_a0"), ("k_k", "rwkv_k_k"), ("k_a", "rwkv_k_a"),
                                     ("r_k", "rwkv_r_k")):
                        sp.dma_start(cols[x_][:, :], T[name].rearrange("a (f p) -> p (a f)", p=P)).then_inc(loaded, 16)
                sp.dma_start(up[0:32, :], T["rwkv_w_up"]).then_inc(loaded, 16)
                sp.dma_start(up[32:64, :], T["rwkv_a_up"]).then_inc(loaded, 16)
                sp.dma_start(up[64:P, :], T["rwkv_g_up"]).then_inc(loaded, 16)

            @block.tensor
            def _(pe):
                def up_project(ps, rows, f, done):
                    for lo, hi in COLS:
                        last = nc.tensor.matmul(ps[:, lo:hi], up[rows, f * P:(f + 1) * P], gd[rows, lo:hi],
                                                start=True, stop=True)
                    last.then_inc(done, 1)

                def head_sum(ps, of, done):
                    for lo, hi in COLS:
                        last = nc.tensor.matmul(ps[:, lo:hi], head_ones[:, :], of[:, lo:hi], start=True, stop=True)
                    last.then_inc(done, 1)

                pe.wait_ge(loaded, 16 * 8)
                pe.wait_ge(lora_in, 3)
                for f in range(2):
                    if f:
                        pe.wait_ge(did, STEPS)
                        pe.wait_ge(g_kept, 1)
                    up_project(ps_w, slice(0, 32), f, w_up)
                    up_project(ps_a, slice(32, 64), f, a_up)
                    pe.wait_ge(w_sig, f + 1)
                    pe.wait_ge(squared, f + 1)
                    head_sum(ps_w, t_k, sums)
                    pe.wait_ge(did, f * STEPS + 4)
                    pe.wait_ge(rooted, f + 1)
                    up_project(ps_w, slice(64, P), f, g_up)
                    pe.wait_ge(a_sig, f + 1)
                    pe.wait_ge(did, f * STEPS + 12)
                    head_sum(ps_a, t_x, bonus_sum)

            @block.scalar
            def _(act):
                act.wait_ge(loaded, 16 * 8)
                nc.scalar.activation(gd[0:32, :], R[0:32, 6, :], ACT.Tanh).then_inc(lora_in, 1)
                nc.scalar.activation(gd[64:P, :], R[64:P, 6, :], ACT.Sigmoid).then_inc(lora_in, 1)
                nc.scalar.activation(gd[32:64, :], R[32:64, 6, :], ACT.Copy).then_inc(lora_in, 1)
                for f in range(2):
                    if f:
                        act.wait_ge(did, STEPS)
                    act.wait_ge(w_up, f + 1)
                    nc.scalar.activation(t_w[:, :], ps_w[:, 0:TOK], ACT.Sigmoid, bias=cols["w0"][:, f:f + 1]).then_inc(w_sig, 1)
                    act.wait_ge(a_up, f + 1)
                    nc.scalar.activation(t_a[:, :], ps_a[:, 0:TOK], ACT.Sigmoid, bias=cols["a0"][:, f:f + 1]).then_inc(a_sig, 1)
                    nc.scalar.activation(t_k[:, :], R[:, 2 + f, :], ACT.Square, scale=cols["k_k"][:, f:f + 1]).then_inc(squared, 1)
                    act.wait_ge(did, f * STEPS + 4)
                    nc.scalar.activation(t_k[:, :], t_y, ACT.Sqrt).then_inc(rooted, 1)
                    act.wait_ge(did, f * STEPS + 6)
                    nc.scalar.activation(t_e[:, :], t_e[:, :], ACT.Exp, scale=-DECAY).then_inc(exp_p, 1)
                    nc.scalar.activation(t_w[:, :], t_l[:, :], ACT.Exp, scale=DECAY).then_inc(exp_nl, 1)
                    act.wait_ge(exp_nl, f + 1)
                    nc.scalar.activation(t_l[:, :], t_l[:, :], ACT.Exp, scale=-DECAY).then_inc(exp_l, 1)
                    act.wait_ge(g_up, f + 1)
                    nc.scalar.activation(mT[:, 2 + f, :], ps_w[:, 0:TOK], ACT.Copy).then_inc(g_kept, 1)

            @block.vector
            def _(dve):
                def of_ends(f):
                    return ((slice(0, SEQ), C, bc(ends[:, f, 0:NC], 2, C)),
                            (slice(SEQ, TOK), ST, bc(ends[:, f, NC:], 2, ST)))

                def step(ins):
                    count[0] += 1
                    ins.then_inc(did, 1)
                    dve.wait_ge(did, count[0])

                count = [0]
                nc.vector.memset(inside[:, :], 1.0).then_inc(const, 1)
                dve.wait_ge(const, 1)
                nc.vector.memset(inside[:, 0:SEQ:C], 0.0).then_inc(const, 1)
                nc.vector.memset(inside[:, SEQ::ST], 0.0).then_inc(const, 1)
                dve.wait_ge(loaded, 16 * 8)
                nc.vector.tensor_scalar(cols["k_0"][:, :], cols["k_a"][:, :], -1.0, 1.0, ALU.mult, ALU.add).then_inc(const, 1)
                dve.wait_ge(const, 4)
                for f in range(2):
                    r, k, v = R[:, f, :], R[:, 2 + f, :], R[:, 4 + f, :]
                    sc = {x_: c[:, f:f + 1] for x_, c in cols.items()}
                    if f:
                        dve.wait_ge(bonus_sum, 1)
                        dve.wait_ge(exp_l, 1)
                    dve.wait_ge(w_sig, f + 1)
                    step(nc.vector.tensor_tensor_scan(t_l[:, :], inside[:, :], t_w[:, :], 0.0, ALU.mult, ALU.add))
                    step(nc.vector.tensor_scalar(t_x, k, sc["k_k"], None, ALU.mult))
                    step(nc.vector.tensor_tensor(t_e[:, :], t_l[:, :], t_w[:, :], ALU.subtract))
                    dve.wait_ge(sums, f + 1)
                    step(nc.vector.tensor_scalar(t_y, ps_w[:, 0:TOK], 1e-24, None, ALU.max))
                    dve.wait_ge(rooted, f + 1)
                    step(nc.vector.reciprocal(t_y, t_k[:, :]))
                    step(nc.vector.tensor_tensor(t_x, t_x, t_y, ALU.mult))
                    dve.wait_ge(exp_p, f + 1)
                    nc.vector.scalar_tensor_tensor(B[:, 0, f, :], t_x, -1.0, t_e[:, :], ALU.mult, ALU.mult).then_inc(did, 1)
                    dve.wait_ge(a_sig, f + 1)
                    nc.vector.tensor_scalar(t_y, t_a[:, :], sc["k_a"], sc["k_0"], ALU.mult, ALU.add).then_inc(did, 1)
                    count[0] += 2
                    dve.wait_ge(did, count[0])
                    step(nc.vector.tensor_tensor(k, k, t_y, ALU.mult))
                    step(nc.vector.tensor_tensor(t_a[:, :], t_x, t_a[:, :], ALU.mult))
                    dve.wait_ge(exp_nl, f + 1)
                    step(nc.vector.tensor_tensor(B[:, 1, f, :], t_a[:, :], t_w[:, :], ALU.mult))
                    step(nc.vector.scalar_tensor_tensor(t_x, r, sc["r_k"], k, ALU.mult, ALU.mult))
                    dve.wait_ge(exp_l, f + 1)
                    step(nc.vector.tensor_copy(ends[:, f, 0:NC], t_l[:, C - 1:SEQ:C]))
                    step(nc.vector.tensor_copy(ends[:, f, NC:], t_l[:, SEQ + ST - 1::ST]))
                    step(nc.vector.tensor_tensor(r, r, t_l[:, :], ALU.mult))
                    step(nc.vector.tensor_tensor(k, k, t_w[:, :], ALU.mult))
                    for at, size, end in of_ends(f):
                        for dst, src in ((B[:, 2, f, at], B[:, 1, f, at]), (B[:, 3, f, at], k[:, at])):
                            step(nc.vector.tensor_tensor(dst.rearrange("p (c t) -> p c t", t=size),
                                                         src.rearrange("p (c t) -> p c t", t=size), end, ALU.mult))
                    dve.wait_ge(bonus_sum, f + 1)
                    step(nc.vector.tensor_tensor(mT[:, 4 + f, :], ps_a[:, 0:TOK], v, ALU.mult))
                assert count[0] == 2 * STEPS


def rwkv_chunks(nc, T, keep):
    R, B, mT, ends = keep["R"], keep["B"], keep["mT"], keep["ends"]
    ident = keep["ident"]
    LEVELS = 5
    TURNS = NT
    HALF = [slice(0, HD), slice(HD, P)]
    L_, N_ = 0, 1
    with Phase(nc, "rc") as ph:
        stR, stB = ph.sb("stR", [P, 2, 6, P]), ph.sb("stB", [P, 2, 8, P])
        RING = 4
        pw = ph.sb("pw", [P, RING, 2, 4, C])
        inv = ph.sb("inv", [P, 4, C])
        M = ph.sb("M", [P, 2, 4, C])
        LkT = ph.sb("LkT", [P, 4, C])
        tok = ph.sb("tok", [P, 4, 4, C])
        XW = ph.sb("XW", [P, 2, 4, C])
        U = ph.sb("U", [P, 2, C])
        S = ph.sb("S", [P, 2, 2, HD])
        masks = {"p": ph.sb("mask_p", [P, 3, C]), "s": ph.sb("mask_s", [P, 3, C])}
        own = ph.sb("own", [P, SB])
        I2 = ph.sb("I2", [P, C])
        Ss = ph.sb("Ss", [P, 2, SB, HD])
        UVm = ph.sb("UVm", [P, 2, SB, C])
        S_out, S_out_prompt = UVm, U
        bank = [ph.ps(f"bank{x_}", [P, 512]) for x_ in range(8)]

        def q4(b, half=0):
            return bank[b][:, half * 256:half * 256 + 256].rearrange("p (q c) -> p q c", c=C)

        names = ("staged pairs turned_tok lk_done m_done powers inverses xw_done u_done s_done y_done ln_kept inv_kept "
                 "tok_kept lk_kept m_kept x_kept u_kept s_kept y_kept built loaded S_turned S_ready parts masked_uv passed "
                 "out_turned out_kept stored")
        g = {x_: ph.sem(x_) for x_ in names.split()}
        with nc.Block() as block:
            @block.sync
            def _(sp):
                for h in range(2):
                    for f in range(2):
                        sp.dma_start(Ss[HALF[h], f, :, :],
                                     T["state_rwkv"][:, 2 * f + h, :, :].rearrange("b i j -> i b j")).then_inc(g["loaded"], 16)
                sp.wait_ge(g["out_kept"], 2)
                for h in range(2):
                    for f in range(2):
                        sp.dma_start(T["S_prompt"][2 * f + h, :, :], S_out_prompt[HALF[h], f, :]).then_inc(g["stored"], 16)
                        sp.dma_start(T["S_sample"][:, 2 * f + h, :, :].rearrange("b i j -> i b j"),
                                     S_out[HALF[h], f, :, :]).then_inc(g["stored"], 16)
                sp.wait_ge(g["stored"], 8 * 16)

            @block.gpsimd
            def _(pool):
                count = [0]

                def step(ins):
                    count[0] += 1
                    ins.then_inc(g["built"], 1)
                    pool.wait_ge(g["built"], count[0])

                def select(ap, op, base, pattern, mult):
                    step(nc.gpsimd.affine_select(out=ap, in_=ap, compare_op=op, fill=0.0, base=base, pattern=pattern,
                                                 channel_multiplier=mult))

                for h in range(2):
                    rows = HALF[h]
                    for m in masks.values():
                        step(nc.gpsimd.memset(m[rows, :, :], 1.0))
                        select(m[rows, 0, :], ALU.is_gt, 0, [[-1, C]], 1)
                        select(m[rows, 1, :], ALU.is_gt, 0, [[1, C]], -1)
                        select(m[rows, 2, :], ALU.is_ge, 0, [[1, C]], -1)
                    step(nc.gpsimd.memset(own[rows, :], 1.0))
                    for ap, pattern in ((masks["s"][rows, :, :], [[0, 3], [-ST, SB], [0, ST]]), (own[rows, :], [[-ST, SB]])):
                        select(ap, ALU.is_ge, 0, pattern, 1)
                        select(ap, ALU.is_ge, ST - 1, [[-x_, n_] for x_, n_ in pattern], -1)
                    step(nc.gpsimd.tensor_copy(I2[rows, :], ident[rows, rows]))
                assert count[0] == BUILT

                def stage(n, u, r):
                    m = rows_of(n)
                    pool.wait_ge(g["y_done"], 2 * n + 2)
                    nc.gpsimd.tensor_copy(stR[:, u, :, 0:m], R[:, 0:6, bass.ds(n * P, m)]).then_inc(g["staged"], 1)
                    nc.gpsimd.tensor_copy(stB[:, u, :, 0:m],
                                          B[:, :, :, :].rearrange("p m f t -> p (m f) t")[:, :, bass.ds(n * P, m)]
                                          ).then_inc(g["staged"], 1)

                pool.sem_inc(g["y_done"], 4)
                each(pool, NT + 1, stage)

            @block.tensor
            def _(pe):
                def units(chunks):
                    return [(c, f, h) for c in range(chunks) for f in range(2) for h in range(2)]

                def ready(sem, value):
                    wait_apart(pe, sem, value, g["passed"])

                def mm(out, lhsT, rhs, start=True, stop=True):
                    return nc.tensor.matmul(out, lhsT, rhs, start=start, stop=stop, skip_group_check=True)

                def before_state(n, u, chunks):
                    def st(x_, f, c):
                        at = slice(c * C, c * C + C)
                        return stR[:, u, x_ * 2 + f, at] if x_ < 3 else stB[:, u, (x_ - 3) * 2 + f, at]

                    r_, k_, v_, a_, b_, bt_, kt_ = range(7)
                    U_ = units(chunks)
                    ready(g["staged"], 2 * n + 2)
                    for c, f, h in U_:
                        rows, q = HALF[h], 2 * c + f
                        mm(q4(0, L_)[rows, q, :], st(a_, f, c)[rows, :], st(b_, f, c)[rows, :])
                        last = mm(q4(0, N_)[rows, q, :], st(b_, f, c)[rows, :], st(a_, f, c)[rows, :])
                    last.then_inc(g["pairs"], 1)
                    for x_, (b, half) in ((a_, (3, 0)), (bt_, (3, 1)), (kt_, (4, 0)), (v_, (4, 1))):
                        for c, f, h in U_:
                            rows, q = HALF[h], 2 * c + f
                            last = mm(q4(b, half)[rows, q, :], st(x_, f, c)[rows, :], I2[rows, :])
                    last.then_inc(g["turned_tok"], 1)
                    ready(g["s_kept"], 2 * n + 1)
                    for c, f, h in U_:
                        rows, q = HALF[h], 2 * c + f
                        last = mm(q4(2)[rows, q, :], st(k_, f, c)[rows, :], st(a_, f, c)[rows, :])
                    last.then_inc(g["lk_done"], 1)
                    for c, f, h in U_:
                        rows, q = HALF[h], 2 * c + f
                        mm(q4(1, 0)[rows, q, :], st(b_, f, c)[rows, :], st(r_, f, c)[rows, :])
                        last = mm(q4(1, 1)[rows, q, :], st(k_, f, c)[rows, :], st(r_, f, c)[rows, :])
                    last.then_inc(g["m_done"], 1)

                    def square(k):
                        ready(g["ln_kept"], (LEVELS + 1) * n + k)
                        for c, f, h in U_:
                            rows, q = HALF[h], 2 * c + f
                            Lk, Nk = pw[rows, (k - 1) % RING, L_, q, :], pw[rows, (k - 1) % RING, N_, q, :]
                            last = mm(q4(5 + k % 2, L_)[rows, q, :], Nk, Lk)
                            if k < LEVELS:
                                last = mm(q4(5 + k % 2, N_)[rows, q, :], Lk, Nk)
                        last.then_inc(g["powers"], 1)

                    def times(k):
                        ready(g["ln_kept"], (LEVELS + 1) * n + k + 1)
                        ready(g["inv_kept"], (LEVELS + 1) * n + k)
                        for c, f, h in U_:
                            rows, q = HALF[h], 2 * c + f
                            last = mm(q4(7)[rows, q, :], pw[rows, k % RING, L_, q, :], inv[rows, q, :])
                        last.then_inc(g["inverses"], 1)

                    ready(g["y_kept"], n + 1)
                    square(1)
                    for k in range(1, LEVELS):
                        square(k + 1)
                        times(k)
                    times(LEVELS)
                    ready(g["tok_kept"], n + 1)
                    ready(g["lk_kept"], n + 1)
                    for c, f, h in U_:
                        rows, q = HALF[h], 2 * c + f
                        last = mm(q4(0, 0)[rows, q, :], LkT[rows, q, :], tok[rows, 3, q, :])
                    ready(g["inv_kept"], (LEVELS + 1) * n + LEVELS + 1)
                    for c, f, h in U_:
                        rows, q = HALF[h], 2 * c + f
                        last = mm(q4(0, 1)[rows, q, :], tok[rows, 0, q, :], inv[rows, q, :])
                    last.then_inc(g["xw_done"], 1)
                    ready(g["x_kept"], n + 1)
                    ready(g["m_kept"], n + 1)

                def turn_of_prompt(n, u, r):
                    before_state(n, u, 2)
                    for c in range(2):
                        ready(g["s_kept"], 2 * n + c + 1)
                        for f in range(2):
                            for rows in HALF:
                                q = 2 * c + f
                                mm(q4(3)[rows, f, :], XW[rows, 1, q, :], S[rows, c, f, :], stop=False)
                                last = mm(q4(3)[rows, f, :], inv[rows, q, :], XW[rows, 0, q, :], start=False)
                        last.then_inc(g["u_done"], 1)
                        for f in range(2):
                            for rows in HALF:
                                q = 2 * c + f
                                at = slice(c * C, c * C + C)
                                mm(q4(6)[rows, q, :], S[rows, c, f, :], stR[rows, u, f, at], stop=False)
                                mm(q4(6)[rows, q, :], tok[rows, 3, q, :], M[rows, 1, q, :], start=False, stop=False)
                                if f == 0:
                                    ready(g["u_kept"], 2 * n + c + 1)
                                mm(q4(6)[rows, q, :], U[rows, f, :], M[rows, 0, q, :], start=False)
                                mm(q4(2)[rows, f, :], tok[rows, 2, q, :], tok[rows, 3, q, :], stop=False)
                                last = mm(q4(2)[rows, f, :], tok[rows, 1, q, :], U[rows, f, :], start=False)
                        last.then_inc(g["y_done"], 1)

                pe.wait_ge(g["built"], BUILT)
                pe.wait_ge(g["loaded"], 64)
                for f in range(2):
                    for b in range(SB):
                        for rows in HALF:
                            last = mm(bank[f][rows, b * HD:(b + 1) * HD], Ss[rows, f, b, :], I2[rows, :])
                last.then_inc(g["S_turned"], 1)
                pe.wait_ge(g["S_ready"], 2)
                each(pe, TURNS, turn_of_prompt)

                u = TURNS % 2
                before_state(TURNS, u, 1)
                for f in range(2):
                    for rows in HALF:
                        mm(bank[3 + f][rows, :], XW[rows, 1, f, :], Ss[rows, f, :, :].rearrange("p b i -> p (b i)"))
                        last = mm(q4(7)[rows, f, :], inv[rows, f, :], XW[rows, 0, f, :])
                last.then_inc(g["u_done"], 1)
                pe.wait_ge(g["u_kept"], 2 * TURNS + 1)
                for f in range(2):
                    for rows in HALF:
                        y = q4(6)[rows, f, :]
                        mm(y, U[rows, f, :], M[rows, 0, f, :], stop=False)
                        mm(y, tok[rows, 3, f, :], M[rows, 1, f, :], start=False, stop=False)
                        for b in range(SB):
                            at = slice(b * ST, b * ST + ST)
                            last = mm(y[:, at], Ss[rows, f, b, :], stR[rows, u, f, at], start=False)
                last.then_inc(g["y_done"], 2)
                for f in range(2):
                    pe.wait_ge(g["masked_uv"], 2 * f + 2)
                    for rows in HALF:
                        mm(bank[f][rows, :], tok[rows, 1, f, :], UVm[rows, 0, :, :].rearrange("p b i -> p (b i)"), stop=False)
                        last = mm(bank[f][rows, :], tok[rows, 2, f, :], UVm[rows, 1, :, :].rearrange("p b i -> p (b i)"), start=False)
                    last.then_inc(g["s_done"], 1)
                pe.wait_ge(g["s_kept"], 2 * TURNS + 1 + 2)
                for f in range(2):
                    for rows in HALF:
                        mm(q4(2)[rows, f, :], S[rows, 0, f, :], I2[rows, :])
                        for b in range(SB):
                            last = mm(bank[3 + f][rows, b * HD:(b + 1) * HD], Ss[rows, f, b, :], I2[rows, :])
                last.then_inc(g["out_turned"], 1)

            @block.scalar
            def _(act):
                act.sem_inc(g["y_kept"], 1)
                act.wait_ge(g["S_turned"], 1)
                for f in range(2):
                    nc.scalar.activation(Ss[:, f, :, :].rearrange("p b i -> p (b i)"), bank[f][:, :], ACT.Copy).then_inc(g["S_ready"], 1)

                def keep_turn(n, u, Q):
                    act.wait_ge(g["turned_tok"], n + 1)
                    for b in (3, 4):
                        at = 2 * (b - 3)
                        last = nc.scalar.activation(tok[:, at:at + 2, 0:Q, :],
                                                    bank[b][:, :].rearrange("p (x q c) -> p x q c", x=2, c=C)[:, :, 0:Q, :],
                                                    ACT.Copy)
                    last.then_inc(g["tok_kept"], 1)
                    act.wait_ge(g["xw_done"], n + 1)
                    nc.scalar.activation(XW[:, :, 0:Q, :],
                                         bank[0][:, :].rearrange("p (x q c) -> p x q c", x=2, c=C)[:, :, 0:Q, :],
                                         ACT.Copy).then_inc(g["x_kept"], 1)
                    act.wait_ge(g["y_done"], 2 * n + 2 + 4)

                def prompt(n, u, r):
                    keep_turn(n, u, 4)
                    nc.scalar.activation(mT[:, 0:2, bass.ds(n * P, P)].rearrange("p f (c t) -> p c f t", c=2),
                                         q4(6).rearrange("p (c f) t -> p c f t", c=2), ACT.Copy).then_inc(g["y_kept"], 1)

                each(act, TURNS, prompt)
                keep_turn(TURNS, 0, 2)
                nc.scalar.activation(mT[:, 0:2, SEQ:TOK], q4(6)[:, 0:2, :], ACT.Copy).then_inc(g["y_kept"], 1)
                act.wait_ge(g["out_turned"], 1)
                for f in range(2):
                    nc.scalar.activation(S_out_prompt[:, f, :], q4(2)[:, f, :], ACT.Copy)
                    last = nc.scalar.activation(S_out[:, f, :, :], bank[3 + f][:, :].rearrange("p (b i) -> p b i", b=SB),
                                                ACT.Copy)
                    last.then_inc(g["out_kept"], 1)

            @block.vector
            def _(dve):
                def keep_turn(n, u, Q, mask):
                    dve.wait_ge(g["pairs"], n + 1)
                    nc.vector.tensor_tensor(pw[:, 0, :, 0:Q, :], bank[0][:, :].rearrange("p (x q c) -> p x q c", x=2, c=C)[:, :, 0:Q, :],
                                            bc(mask[:, 0:2, :], 2, Q), ALU.mult).then_inc(g["ln_kept"], 1)
                    dve.wait_ge(g["ln_kept"], (LEVELS + 1) * n + 1)
                    nc.vector.tensor_tensor(inv[:, 0:Q, :], pw[:, 0, N_, 0:Q, :], bc(I2[:, :], 1, Q), ALU.add).then_inc(g["inv_kept"], 1)
                    dve.wait_ge(g["lk_done"], n + 1)
                    nc.vector.tensor_tensor(LkT[:, 0:Q, :], q4(2)[:, 0:Q, :], bc(mask[:, 1, :], 1, Q), ALU.mult).then_inc(g["lk_kept"], 1)
                    dve.wait_ge(g["m_done"], n + 1)
                    nc.vector.tensor_tensor(M[:, :, 0:Q, :], bank[1][:, :].rearrange("p (x q c) -> p x q c", x=2, c=C)[:, :, 0:Q, :],
                                            bc(bc(mask[:, 2, :], 1, Q), 1, 2), ALU.mult).then_inc(g["m_kept"], 1)

                    def keep_power(k):
                        dve.wait_ge(g["powers"], LEVELS * n + k)
                        w = 2 if k < LEVELS else 1
                        nc.vector.tensor_copy(pw[:, k % RING, 0:w, 0:Q, :],
                                              bank[5 + k % 2][:, :].rearrange("p (x q c) -> p x q c", x=2, c=C)[:, 0:w, 0:Q, :]
                                              ).then_inc(g["ln_kept"], 1)

                    def keep_inverse(k):
                        dve.wait_ge(g["inverses"], LEVELS * n + k)
                        nc.vector.tensor_tensor(inv[:, 0:Q, :], inv[:, 0:Q, :], q4(7)[:, 0:Q, :], ALU.add).then_inc(g["inv_kept"], 1)

                    keep_power(1)
                    for k in range(1, LEVELS):
                        keep_power(k + 1)
                        keep_inverse(k)
                    keep_inverse(LEVELS)

                def prompt(n, u, r):
                    keep_turn(n, u, 4, masks["p"])
                    for c in range(2):
                        dve.wait_ge(g["u_done"], 2 * n + c + 1)
                        nc.vector.tensor_copy(U[:, :, :], q4(3)[:, 0:2, :]).then_inc(g["u_kept"], 1)
                        dve.wait_ge(g["y_done"], 2 * n + c + 1 + 4)
                        for f in range(2):
                            last = nc.vector.scalar_tensor_tensor(S[:, 1 - c, f, :], S[:, c, f, :],
                                                                  ends[:, f, bass.ds(n * 2 + c, 1)], q4(2)[:, f, :],
                                                                  ALU.mult, ALU.add)
                        last.then_inc(g["s_kept"], 1)

                nc.vector.memset(S[:, 0, :, :], 0.0).then_inc(g["s_kept"], 1)
                dve.wait_ge(g["built"], BUILT)
                each(dve, TURNS, prompt)
                keep_turn(TURNS, 0, 2, masks["s"])
                dve.wait_ge(g["u_done"], 2 * TURNS + 1)
                for f in range(2):
                    nc.vector.tensor_tensor(UVm[:, f, :, :], bank[3 + f][:, :].rearrange("p (b i) -> p b i", b=SB),
                                            bc(own[:, :], 2, C), ALU.mult).then_inc(g["parts"], 1)
                dve.wait_ge(g["parts"], 2)
                for f in range(2):
                    nc.vector.tensor_reduce(U[:, f, :], UVm[:, f, :, :].rearrange("p b i -> p i b"), axis=AXX, op=ALU.add).then_inc(g["parts"], 1)
                dve.wait_ge(g["parts"], 4)
                nc.vector.tensor_tensor(U[:, :, :], U[:, :, :], q4(7)[:, 0:2, :], ALU.add).then_inc(g["u_kept"], 1)
                dve.wait_ge(g["u_kept"], 2 * TURNS + 1)
                for f in range(2):
                    if f:
                        dve.wait_ge(g["s_done"], 1)
                    for x_, src in ((0, U[:, f, :]), (1, tok[:, 3, f, :])):
                        nc.vector.tensor_tensor(UVm[:, x_, :, :], bc(src, 1, SB), bc(own[:, :], 2, C), ALU.mult).then_inc(g["masked_uv"], 1)
                dve.wait_ge(g["y_done"], 2 * TURNS + 2 + 4)
                dve.wait_ge(g["s_done"], 2)
                for f in range(2):
                    nc.vector.tensor_tensor(Ss[:, f, :, :], Ss[:, f, :, :], bc(ends[:, f, NC:], 2, HD), ALU.mult).then_inc(g["parts"], 1)
                dve.wait_ge(g["parts"], 6)
                for f in range(2):
                    nc.vector.tensor_tensor(Ss[:, f, :, :], Ss[:, f, :, :], bank[f][:, :].rearrange("p (b i) -> p b i", b=SB),
                                            ALU.add).then_inc(g["s_kept"], 1)


def rwkv_finish(nc, T, keep):
    mT, head_ones = keep["mT"], keep["head_ones"]
    with Phase(nc, "rf") as ph:
        sq, t = ph.sb("sq", [P, TOK]), ph.sb("t", [P, TOK])
        ln_g, ln_b = ph.sb("ln_g", [P, 2]), ph.sb("ln_b", [P, 2])
        ps_m, ps_s = ph.ps("ps_m", [P, 1536]), ph.ps("ps_s", [P, 1536])
        loaded, means, squared, sums, rooted, did = (ph.sem(x_) for x_ in ("loaded", "means", "squared", "sums", "rooted", "did"))
        n_steps = 7
        with nc.Block() as block:
            @block.sync
            def _(sp):
                with nc.allow_non_contiguous_dma(reason="one scalar per feature"):
                    sp.dma_start(ln_g[:, :], T["rwkv_ln_g"].rearrange("a (f p) -> p (a f)", p=P)).then_inc(loaded, 16)
                    sp.dma_start(ln_b[:, :], T["rwkv_ln_b"].rearrange("a (f p) -> p (a f)", p=P)).then_inc(loaded, 16)

            @block.tensor
            def _(pe):
                for f in range(2):
                    if f:
                        pe.wait_ge(did, n_steps)
                    for lo, hi in COLS:
                        last = nc.tensor.matmul(ps_m[:, lo:hi], head_ones[:, :], mT[:, f, lo:hi], start=True, stop=True)
                    last.then_inc(means, 1)
                    pe.wait_ge(squared, f + 1)
                    for lo, hi in COLS:
                        last = nc.tensor.matmul(ps_s[:, lo:hi], head_ones[:, :], sq[:, lo:hi], start=True, stop=True)
                    last.then_inc(sums, 1)

            @block.scalar
            def _(act):
                for f in range(2):
                    act.wait_ge(did, f * n_steps + 1)
                    nc.scalar.activation(sq[:, :], mT[:, f, :], ACT.Square).then_inc(squared, 1)
                    act.wait_ge(did, f * n_steps + 2)
                    nc.scalar.activation(t[:, :], t[:, :], ACT.Sqrt).then_inc(rooted, 1)

            @block.vector
            def _(dve):
                count = [0]

                def step(ins):
                    count[0] += 1
                    ins.then_inc(did, 1)
                    dve.wait_ge(did, count[0])

                dve.wait_ge(loaded, 32)
                for f in range(2):
                    y = mT[:, f, :]
                    dve.wait_ge(means, f + 1)
                    step(nc.vector.scalar_tensor_tensor(y, ps_m[:, 0:TOK], -1.0 / HD, y, ALU.mult, ALU.add))
                    dve.wait_ge(sums, f + 1)
                    step(nc.vector.tensor_scalar(t[:, :], ps_s[:, 0:TOK], 1.0 / HD, GN_EPS, ALU.mult, ALU.add))
                    dve.wait_ge(rooted, f + 1)
                    step(nc.vector.reciprocal(t[:, :], t[:, :]))
                    step(nc.vector.tensor_tensor(y, y, t[:, :], ALU.mult))
                    step(nc.vector.tensor_scalar(y, y, ln_g[:, f:f + 1], ln_b[:, f:f + 1], ALU.mult, ALU.add))
                    step(nc.vector.tensor_tensor(y, y, mT[:, 4 + f, :], ALU.add))
                    step(nc.vector.tensor_tensor(y, y, mT[:, 2 + f, :], ALU.mult))
                assert count[0] == 2 * n_steps


def gated_mlp(nc, T, keep):
    hT, mT, v_g, ident = keep["hT"], keep["mT"], keep["v_g"], keep["ident"]
    w_view = T["w_in"].rearrange("(k p) n -> p k n", p=P)
    G = GG * NT
    parts = [(slice(0, P), slice(0, NT), G, 0), (slice(0, NS), slice(NT, NT + 1), GG, 1)]
    with Phase(nc, "gm") as ph:
        w = ph.sb("w", [P, KT, GW])
        ws, wsT = ph.sb("ws", [P, GG, P]), ph.sb("wsT", [P, GG, P])
        ws_s, ws_sT = ph.sb("ws_s", [NS, GG, NS]), ph.sb("ws_sT", [NS, GG, NS])
        bs, bs_s = ph.sb("bs", [P, 2, P]), ph.sb("bs_s", [P, 2, ST])
        g, b = ph.sb("g", [P, GW]), ph.sb("b", [P, GW])
        sq = ph.sb("sq", [P, NT + 1, GW])
        st = [ph.sb(f"st{x_}", [P, 2, G]) for x_ in range(3)]
        mixed = ph.sb("mixed", [P, 2, TOK])
        ps_u, ps_m, ps_s = ph.ps("ps_u", [P, 1536]), ph.ps("ps_m", [P, 2, SEQ]), ph.ps("ps_s", [P, 512])
        (loaded, zeroed, w_loaded, masked, u_done, u_kept, gelus, squared, rooted, turned, turned_kept, did, mixes,
         stored) = (ph.sem(x_) for x_ in (
             "loaded", "zeroed", "w_loaded", "masked", "u_done", "u_kept", "gelus", "squared", "rooted", "turned",
             "turned_kept", "did", "mixes", "stored"))

        def groups(t, part, size=None):
            rows, tiles, n, _ = part
            return t[rows, tiles, :].rearrange("p t (g c) -> p (t g) c", c=HD)

        with nc.Block() as block:
            @block.sync
            def _(sp):
                sp.dma_start(w[:, :, :], w_view[:, :, OG:OG + GW]).then_inc(w_loaded, 16)
                sp.dma_start(ws[:, :, :], T["gmlp_ws"].rearrange("g t s -> t g s")).then_inc(loaded, 16)
                sp.dma_start(g[:, :], T["gmlp_ln_g"].to_broadcast([P, GW])).then_inc(loaded, 16)
                sp.dma_start(b[:, :], T["gmlp_ln_b"].to_broadcast([P, GW])).then_inc(loaded, 16)
                for x_ in range(GG):
                    rows = slice(x_ % 2 * HD, x_ % 2 * HD + HD)
                    sp.dma_start(bs[rows, x_ // 2, :], T["gmlp_bs"][x_:x_ + 1, :].to_broadcast([HD, P])).then_inc(loaded, 16)
                    sp.dma_start(bs_s[rows, x_ // 2, :], T["gmlp_bs"][x_:x_ + 1, 0:ST].to_broadcast([HD, ST])).then_inc(loaded, 16)
                sp.wait_ge(zeroed, 1)
                for x_ in range(SB):
                    at = slice(x_ * ST, x_ * ST + ST)
                    sp.dma_start(ws_s[at, :, at], T["gmlp_ws"][:, 0:ST, 0:ST].rearrange("g t s -> t g s")).then_inc(loaded, 16)
                sp.wait_ge(did, LN_STEPS)
                sp.dma_start(T["g_v_sample"], v_g[0:NS, NT, :]).then_inc(stored, 16)
                sp.wait_ge(stored, 16)

            @block.gpsimd
            def _(pool):
                nc.gpsimd.memset(ws_s[:, :, :], 0.0).then_inc(zeroed, 1)
                pool.wait_ge(loaded, 16 * (3 + 2 * GG + SB))
                nc.gpsimd.affine_select(out=ws[:, :, :], in_=ws[:, :, :], compare_op=ALU.is_ge, fill=0.0, base=0,
                                        pattern=[[0, GG], [-1, P]], channel_multiplier=1).then_inc(masked, 1)
                nc.gpsimd.affine_select(out=ws_s[:, :, :], in_=ws_s[:, :, :], compare_op=ALU.is_ge, fill=0.0, base=0,
                                        pattern=[[0, GG], [-1, NS]], channel_multiplier=1).then_inc(masked, 1)

            @block.tensor
            def _(pe):
                pe.wait_ge(w_loaded, 16)
                for f in range(2):
                    if f:
                        pe.wait_ge(u_kept, f)
                    for lo, hi in COLS:
                        for k in range(KT):
                            last = nc.tensor.matmul(ps_u[:, lo:hi], w[:, k, f * P:(f + 1) * P], hT[:, k, lo:hi],
                                                    start=(k == 0), stop=(k == KT - 1))
                    last.then_inc(u_done, 1)
                pe.wait_ge(masked, 2)
                for x_ in range(GG):
                    nc.tensor.transpose(ps_s[:, x_ * P:(x_ + 1) * P], ws[:, x_, :], ident[:, :])
                    last = nc.tensor.transpose(ps_m[0:NS, 0, x_ * NS:(x_ + 1) * NS], ws_s[:, x_, :], ident[0:NS, 0:NS])
                last.then_inc(turned, 1)
                pe.wait_ge(turned_kept, 2)
                pe.wait_ge(did, LN_STEPS)
                for x_ in range(GG):
                    rows, cols = slice(x_ % 2 * HD, x_ % 2 * HD + HD), slice(x_ * HD, x_ * HD + HD)
                    for n in range(NT):
                        nc.tensor.matmul(ps_m[rows, x_ // 2, n * P:(n + 1) * P], v_g[:, n, cols], wsT[:, x_, :],
                                         start=True, stop=True)
                    last = nc.tensor.matmul(ps_s[rows, x_ // 2 * NS:(x_ // 2 + 1) * NS], v_g[0:NS, NT, cols], ws_sT[:, x_, :],
                                            start=True, stop=True)
                last.then_inc(mixes, 1)

            @block.scalar
            def _(act):
                for rows, tiles, _, _ in parts:
                    nc.scalar.activation(v_g[rows, tiles, :], v_g[rows, tiles, :], ACT.Gelu_apprx_tanh).then_inc(gelus, 1)
                for f in range(2):
                    act.wait_ge(u_done, f + 1)
                    nc.scalar.activation(mT[:, 2 + f, :], ps_u[:, 0:TOK], ACT.Gelu_apprx_tanh).then_inc(u_kept, 1)
                act.wait_ge(turned, 1)
                nc.scalar.activation(wsT[:, :, :].rearrange("p g t -> p (g t)"), ps_s[:, :], ACT.Copy).then_inc(turned_kept, 1)
                nc.scalar.activation(ws_sT[:, :, :].rearrange("p g t -> p (g t)"), ps_m[0:NS, 0, 0:GG * NS],
                                     ACT.Copy).then_inc(turned_kept, 1)
                for i, (rows, _, n, _) in enumerate(parts):
                    act.wait_ge(did, LN_STEPS // 2 * i + 6)
                    nc.scalar.activation(st[2][rows, i, 0:n], st[1][rows, i, 0:n], ACT.Sqrt).then_inc(rooted, 1)

            @block.vector
            def _(dve):
                count = [0]

                def step(ins):
                    count[0] += 1
                    ins.then_inc(did, 1)
                    dve.wait_ge(did, count[0])

                dve.wait_ge(loaded, 16 * (3 + 2 * GG + SB))
                for i, part in enumerate(parts):
                    rows, tiles, n, _ = part
                    v, s = groups(v_g, part), groups(sq, part)
                    mean, ms, rt = (x_[rows, i, 0:n] for x_ in st)
                    m_tiles = NT if i == 0 else 1
                    dve.wait_ge(gelus, i + 1)
                    step(nc.vector.tensor_reduce(mean, v, axis=AXX, op=ALU.add))
                    step(nc.vector.tensor_scalar(mean, mean, 1.0 / HD, None, ALU.mult))
                    step(nc.vector.tensor_tensor(v, v, bc(mean, 2, HD), ALU.subtract))
                    step(nc.vector.tensor_tensor(s, v, v, ALU.mult))
                    step(nc.vector.tensor_reduce(ms, s, axis=AXX, op=ALU.add))
                    step(nc.vector.tensor_scalar(ms, ms, 1.0 / HD, LN_EPS, ALU.mult, ALU.add))
                    dve.wait_ge(rooted, i + 1)
                    step(nc.vector.reciprocal(rt, rt))
                    step(nc.vector.tensor_tensor(v, v, bc(rt, 2, HD), ALU.mult))
                    t = v_g[rows, tiles, :]
                    step(nc.vector.tensor_tensor(t, t, bc(g[rows, :], 1, m_tiles), ALU.mult))
                    step(nc.vector.tensor_tensor(t, t, bc(b[rows, :], 1, m_tiles), ALU.add))
                assert count[0] == LN_STEPS
                dve.wait_ge(mixes, 1)
                dve.wait_ge(u_kept, 2)
                for f in range(2):
                    step(nc.vector.tensor_tensor(mixed[:, f, 0:SEQ].rearrange("p (n t) -> p n t", n=NT),
                                                 ps_m[:, f, :].rearrange("p (n t) -> p n t", n=NT), bc(bs[:, f, :], 1, NT), ALU.add))
                    step(nc.vector.tensor_tensor(mixed[:, f, SEQ:].rearrange("p (n t) -> p n t", n=SB),
                                                 ps_s[:, f * NS:(f + 1) * NS].rearrange("p (n t) -> p n t", n=SB),
                                                 bc(bs_s[:, f, :], 1, SB), ALU.add))
                    step(nc.vector.tensor_tensor(mT[:, 2 + f, :], mT[:, 2 + f, :], mixed[:, f, :], ALU.mult))


def attention(nc, T, keep):
    hT, mT, v_sb, qs, ks = keep["hT"], keep["mT"], keep["v_sb"], keep["qs"], keep["ks"]
    ident, neg_from, neg_ones = keep["ident"], keep["neg_from"], keep["neg_ones"]
    w_view = T["w_in"].rearrange("(k p) n -> p k n", p=P)
    WT, TT = 512, 512 // P
    blocks = []
    for half in range(2):
        for run in range(SEQ // WT):
            tiles = list(range(TT * run + TT - 1, -1, -1))
            for s in tiles:
                blocks.append((half, run, s, max(0, s - TT * run) * P, s == tiles[0], s == tiles[-1]))
    NB, NR = len(blocks), 4
    BANKS, BUF = 4, 3
    with Phase(nc, "at") as ph:
        w = ph.sb("w", [P, 2, KT, P])
        qk = ph.sb("qk", [P, 2, SEQ])
        k_tok = ph.sb("k_tok", [P, NT + 1, P])
        v_pair = ph.sb("v_pair", [P, NT, P])
        k_s = ph.sb("k_s", [P, NS])
        bias = ph.sb("bias", [P, SH])
        zc, sp_ = ph.sb("zc", [P, BUF, WT]), ph.sb("sp", [P, BUF, WT])
        acc, A = ph.sb("acc", [P, 2, WT]), ph.sb("A", [P, BUF, WT])
        ps_p, ps_z = ph.ps("ps_p", [P, 1536]), ph.ps("ps_z", [P, BANKS, 512])
        names = ("bias_loaded w_loaded proj_done qk_kept ks_kept k_turned k_tok_kept k_stored z_done z_clipped exp_done "
                 "ln_done sp_done sp_masked acc_zero acc_done cum_done a_done a_masked av_done run_kept v_staged passed")
        g = {x_: ph.sem(x_) for x_ in names.split()}

        def cols(b):
            return slice(blocks[b][3], WT)

        def diagonal(b):
            half, run, s, lo, _, _ = blocks[b]
            return s >= TT * run

        n_diag = sum(diagonal(b) for b in range(NB))
        diag_before = [sum(diagonal(x_) for x_ in range(b)) for b in range(NB + 1)]

        with nc.Block() as block:
            @block.sync
            def _(sp):
                sp.dma_start(bias[:, :], T["sb_bias"].to_broadcast([P, SH])).then_inc(g["bias_loaded"], 16)

                def load(j, u, r):
                    wait_apart(sp, g["proj_done"], 2 * j + 2, g["passed"])
                    for x_ in range(2):
                        sp.dma_start(w[:, x_, :, :], w_view[:, :, bass.ds(j * P + (OQ + x_ * SBW), P)]).then_inc(g["w_loaded"], 16)
                    wait_apart(sp, g["k_tok_kept"], j + 2, g["passed"])
                    sp.dma_start(T["k_prompt"].rearrange("(n p) c -> p n c", p=P)[:, :, bass.ds(j * P, P)],
                                 k_tok[:, 0:NT, :]).then_inc(g["k_stored"], 16)
                    sp.dma_start(T["k_sample"][:, bass.ds(j * P, P)], k_tok[0:NS, NT, :]).then_inc(g["k_stored"], 16)

                each(sp, SH // 2, load, 1)
                sp.wait_ge(g["k_stored"], 32 + SH // 2 * 32)

            @block.gpsimd
            def _(pool):
                def turn(j, u, r):
                    pool.wait_ge(g["qk_kept"], 4 * j + 4)
                    nc.gpsimd.tensor_copy(ks[:, bass.ds(j, 1), :].squeeze(1), k_s[:, :]).then_inc(g["ks_kept"], 1)
                    pool.wait_ge(g["av_done"], j * NB + 1)
                    nc.gpsimd.tensor_copy(v_pair[:, :, :], v_sb[:, 0:NT, bass.ds(j * P, P)]).then_inc(g["v_staged"], 1)

                    def mask(t, b, done):
                        lo = blocks[b][3]
                        nc.gpsimd.affine_select(out=t[:, b % BUF, lo:lo + P], in_=t[:, b % BUF, lo:lo + P],
                                                compare_op=ALU.is_gt, fill=0.0, base=0, pattern=[[1, P]],
                                                channel_multiplier=-1).then_inc(done, 1)

                    for i in range(NB + 1):
                        if i < NB and diagonal(i):
                            wait_apart(pool, g["sp_done"], j * NB + i + 1, g["passed"])
                            mask(sp_, i, g["sp_masked"])
                        if i >= 1 and diagonal(i - 1):
                            wait_apart(pool, g["a_done"], j * NB + i + 1, g["passed"])
                            mask(A, i - 1, g["a_masked"])

                pool.sem_inc(g["k_stored"], 32)
                pool.sem_inc(g["ks_kept"], 1)
                pool.sem_inc(g["av_done"], 1)
                each(pool, SH // 2, turn, 1)

            @block.tensor
            def _(pe):
                pe.sem_inc(g["proj_done"], 2)

                def turn(j, u, r):
                    pe.wait_ge(g["w_loaded"], j * 32 + 32)
                    pe.wait_ge(g["run_kept"], j * NR + 1)
                    for x_, ps in ((0, ps_p[:, :]), (1, ps_z[:, 0:3, :].rearrange("p b c -> p (b c)"))):
                        if x_:
                            pe.wait_ge(g["a_done"], j * NB + 1)
                        for lo, hi in COLS:
                            for k in range(KT):
                                last = nc.tensor.matmul(ps[:, lo:hi], w[:, x_, k, :], hT[:, k, lo:hi],
                                                        start=(k == 0), stop=(k == KT - 1))
                        last.then_inc(g["proj_done"], 1)
                    pe.wait_ge(g["qk_kept"], j * 4 + 4)
                    for n in range(NT):
                        nc.tensor.transpose(ps_p[:, n * P:(n + 1) * P], qk[:, 1, n * P:(n + 1) * P], ident[:, :])
                    nc.tensor.transpose(ps_p[0:NS, NT * P:(NT + 1) * P], k_s[:, :], ident[:, :]).then_inc(g["k_turned"], 1)

                    def scores(b):
                        half, run, s, lo, _, _ = blocks[b]
                        rows = slice(half * HD, half * HD + HD)
                        if b >= BANKS:
                            pe.wait_ge(g["a_done"], j * NB + b - BANKS + 2)
                        nc.tensor.matmul(ps_z[:, b % BANKS, cols(b)], qk[rows, 1, s * P:(s + 1) * P],
                                         qk[rows, 0, run * WT + lo:run * WT + WT], start=True, stop=False,
                                         skip_group_check=True).then_inc(g["z_done"], 1)

                    def sums(b):
                        first = blocks[b][4]
                        if diagonal(b):
                            pe.wait_ge(g["sp_masked"], j * n_diag + diag_before[b + 1])
                        pe.wait_ge(g["sp_done"], j * NB + b + 1)
                        out = ps_z[:, b % BANKS, cols(b)]
                        last = nc.tensor.matmul(out, neg_from[:, :], sp_[:, b % BUF, cols(b)], start=False, stop=first,
                                                skip_group_check=True)
                        if not first:
                            pe.wait_ge(g["acc_done"], j * NB + b)
                            last = nc.tensor.matmul(out, neg_ones[:, :], acc[:, b % 2, cols(b)], start=False, stop=True,
                                                    skip_group_check=True)
                        last.then_inc(g["cum_done"], 1)

                    def values(b):
                        half, run, s, lo, first, final = blocks[b]
                        x_ = half * 2 + run
                        if diagonal(b):
                            pe.wait_ge(g["a_masked"], j * n_diag + diag_before[b + 1])
                        pe.wait_ge(g["a_done"], j * NB + b + 2)
                        if first:
                            pe.wait_ge(g["k_tok_kept"], j + 2)
                            if x_ >= 3:
                                pe.wait_ge(g["run_kept"], j * NR + x_ - 1)
                            pe.wait_ge(g["v_staged"], j + 1)
                        rows = slice(half * HD, half * HD + HD)
                        nc.tensor.matmul(ps_p[rows, x_ % 3 * 512 + lo:x_ % 3 * 512 + WT], v_pair[:, s, rows],
                                         A[:, b % BUF, cols(b)], start=first, stop=final,
                                         skip_group_check=True).then_inc(g["av_done"], 1)

                    for i in range(NB + 3):
                        if i < NB:
                            scores(i)
                        if 2 <= i < NB + 2:
                            sums(i - 2)
                        if i >= 3:
                            values(i - 3)

                each(pe, SH // 2, turn, 1)

            @block.scalar
            def _(act):
                act.sem_inc(g["a_done"], 1)
                act.sem_inc(g["k_tok_kept"], 1)
                act.wait_ge(g["bias_loaded"], 16)
                nc.scalar.preload_act_table_set("natural_log_exp_and_others")

                def turn(j, u, r):
                    act.wait_ge(g["proj_done"], 2 * j + 3)
                    nc.scalar.activation(qk[:, 0, :], ps_p[:, 0:SEQ], ACT.Copy, scale=HD ** -0.5).then_inc(g["qk_kept"], 1)
                    nc.scalar.activation(qs[:, bass.ds(j, 1), :].squeeze(1), ps_p[:, SEQ:TOK], ACT.Copy,
                                         scale=HD ** -0.5).then_inc(g["qk_kept"], 1)
                    act.wait_ge(g["proj_done"], 2 * j + 4)
                    ps_k = ps_z[:, 0:3, :].rearrange("p b c -> p (b c)")
                    nc.scalar.activation(qk[:, 1, :], ps_k[:, 0:SEQ], ACT.Copy).then_inc(g["qk_kept"], 1)
                    act.wait_ge(g["ks_kept"], j + 1)
                    nc.scalar.activation(k_s[:, :], ps_k[:, SEQ:TOK], ACT.Copy).then_inc(g["qk_kept"], 1)
                    act.wait_ge(g["k_turned"], j + 1)
                    act.wait_ge(g["k_stored"], j * 32 + 32)
                    nc.scalar.activation(k_tok[:, 0:NT, :].rearrange("p n c -> p (n c)"), ps_p[:, 0:SEQ], ACT.Copy)
                    nc.scalar.activation(k_tok[0:NS, NT, :], ps_p[0:NS, SEQ:SEQ + P], ACT.Copy).then_inc(g["k_tok_kept"], 1)
                    head = lambda b: bias[:, bass.ds(j * 2 + blocks[b][0], 1)]

                    def logs(b):
                        act.wait_ge(g["z_clipped"], j * NB + b + 1)
                        z = zc[:, b % BUF, cols(b)]
                        nc.scalar.activation(z, z, ACT.Exp).then_inc(g["exp_done"], 1)
                        act.wait_ge(g["exp_done"], j * NB + b + 1)
                        nc.scalar.activation(z, z, ACT.Ln, bias=1.0).then_inc(g["ln_done"], 1)

                    def weights(b):
                        if b >= BUF:
                            act.wait_ge(g["av_done"], j * NB + b - BUF + 2)
                        wait_apart(act, g["cum_done"], j * NB + b + 1, g["passed"])
                        nc.scalar.activation(A[:, b % BUF, cols(b)], ps_z[:, b % BANKS, cols(b)], ACT.Exp,
                                             bias=head(b)).then_inc(g["a_done"], 1)

                    for i in range(NB + 2):
                        if i < NB:
                            logs(i)
                        if i >= 2:
                            weights(i - 2)

                each(act, SH // 2, turn, 1)

            @block.vector
            def _(dve):
                dve.sem_inc(g["run_kept"], 1)
                dve.wait_ge(g["bias_loaded"], 16)

                def turn(j, u, r):
                    head = lambda b: bias[:, bass.ds(j * 2 + blocks[b][0], 1)]

                    def clip(b):
                        dve.wait_ge(g["z_done"], j * NB + b + 1)
                        nc.vector.tensor_scalar(zc[:, b % BUF, cols(b)], ps_z[:, b % BANKS, cols(b)], head(b), CLIP,
                                                ALU.add, ALU.min).then_inc(g["z_clipped"], 1)

                    def softplus(b):
                        half, run, s, lo, first, final = blocks[b]
                        dve.wait_ge(g["ln_done"], j * NB + b + 1)
                        if b >= BUF:
                            dve.wait_ge(g["cum_done"], j * NB + b - BUF + 1)
                        nc.vector.scalar_tensor_tensor(sp_[:, b % BUF, cols(b)], ps_z[:, b % BANKS, cols(b)], head(b),
                                                       zc[:, b % BUF, cols(b)], ALU.add, ALU.max).then_inc(g["sp_done"], 1)
                        if first:
                            if b:
                                dve.wait_ge(g["cum_done"], j * NB + b)
                            nc.vector.memset(acc[:, :, :], 0.0).then_inc(g["acc_zero"], 1)
                            dve.wait_ge(g["acc_zero"], j * NR + half * 2 + run + 1)
                        if diagonal(b):
                            dve.wait_ge(g["sp_masked"], j * n_diag + diag_before[b + 1])
                        else:
                            dve.wait_ge(g["sp_done"], j * NB + b + 1)
                        if b:
                            dve.wait_ge(g["acc_done"], j * NB + b)
                            dve.wait_ge(g["cum_done"], j * NB + b)
                        if not final:
                            nc.vector.tensor_tensor(acc[:, (b + 1) % 2, cols(b)], acc[:, b % 2, cols(b)],
                                                    sp_[:, b % BUF, cols(b)], ALU.add).then_inc(g["acc_done"], 1)
                        else:
                            dve.sem_inc(g["acc_done"], 1)

                    def keep_run(x_):
                        half, run = x_ // 2, x_ % 2
                        end = max(b for b in range(NB) if blocks[b][0:2] == (half, run))
                        rows = slice(half * HD, half * HD + HD)
                        dve.wait_ge(g["av_done"], j * NB + end + 2)
                        nc.vector.tensor_copy(mT[rows, bass.ds(j + KT - SBW // P, 1), run * WT:(run + 1) * WT].squeeze(1),
                                              ps_p[rows, x_ % 3 * 512:x_ % 3 * 512 + WT]).then_inc(g["run_kept"], 1)

                    ends = {b: blocks[b][0] * 2 + blocks[b][1] for b in range(NB) if blocks[b][5]}
                    for i in range(NB + 3):
                        if i < NB:
                            clip(i)
                        if 1 <= i < NB + 1:
                            softplus(i - 1)
                        if i >= 3 and i - 3 in ends:
                            keep_run(ends[i - 3])

                each(dve, SH // 2, turn, 1)


def sampled_attention(nc, T, keep):
    mT, v_sb, qs, ks = keep["mT"], keep["v_sb"], keep["qs"], keep["ks"]
    ident, neg_from, neg_ones = keep["ident"], keep["neg_from"], keep["neg_ones"]
    FT, HC = SBW // P, SH * ST
    TWO = 2 * ST
    with Phase(nc, "sa") as ph:
        k, v = ph.sb("k", [P, 2, NPAGE, SBW]), ph.sb("v", [P, 2, NPAGE, SBW])
        table = ph.sb("table", [1, SB * NPAGE], I32)
        kt = ph.sb("kt", [P, 2, SBW])
        q2 = ph.sb("q2", [P, FT, SB, TWO])
        bias = ph.sb("bias", [P, SH])
        head_bias = ph.sb("head_bias", [P, SH, ST])
        bias2 = ph.sb("bias2", [P, SB, HC])
        mask, mask_n = ph.sb("mask", [NS, SB, ST]), ph.sb("mask_n", [NS, FT, SB, TWO])
        zn, cn = ph.sb("zn", [NS, FT, SB, TWO]), ph.sb("cn", [NS, FT, SB, TWO])
        an = ph.sb("an", [NS, FT, SB, TWO])
        y_new = ph.sb("y_new", [P, FT, SB, TWO])
        y_rows = ph.sb("y_rows", [HC, SBW])
        zb, zc, sp_, suf, a_in, A = (ph.sb(x_, [P, 2, NPAGE, HC]) for x_ in ("zb", "zc", "sp", "suf", "a_in", "A"))
        ps_t, ps_z = ph.ps("ps_t", [P, 2, 512]), ph.ps("ps_z", [P, 2, NPAGE, HC])
        ps_y, ps_o = ph.ps("ps_y", [P, 512]), ph.ps("ps_o", [P, FT, TWO])
        ps_n, ps_c = ph.ps("ps_n", [P, FT, SB, TWO]), ph.ps("ps_c", [P, FT, SB, TWO])
        names = ("bias_loaded did masked new_z new_clipped new_logs new_cum new_a q_ready turned kt_kept "
                 "page_scored z_done z_read clipped logged sp_done suf_done cum_done a_in_done a_done values_done rows_kept y_new_done y_new_kept y_turned y_kept table_loaded passed")
        g = {x_: ph.sem(x_) for x_ in names.split()}
        k_loaded, v_loaded = ([ph.sem(f"{x_}_loaded{u}") for u in range(2)] for x_ in "kv")
        flat = lambda ap: ap.rearrange("p f b c -> p (f b c)")
        row = lambda ap: ap.rearrange("p n c -> p (n c)")
        with nc.Block() as block:
            @block.sync
            def _(sp):
                sp.dma_start(table[:, :], T["page_table"]).then_inc(g["table_loaded"], 16)
                sp.dma_start(bias[:, :], T["sb_bias"].to_broadcast([P, SH])).then_inc(g["bias_loaded"], 16)
                sp.wait_ge(g["table_loaded"], 16)

                def load(b, u, r):
                    wait_apart(sp, g["turned"], b * NPAGE + NPAGE, g["passed"])
                    pages = [sp.value_load(table[0:1, bass.ds(b * NPAGE + n, 1)], min_val=0, max_val=79) for n in range(NPAGE)]
                    for n, page in enumerate(pages):
                        sp.dma_start(k[:, u, n, :], T["cache_k"][bass.ds(page, 1), :, :].squeeze(0)).then_inc(k_loaded[u], 16)
                    wait_apart(sp, g["values_done"], b + 1, g["passed"])
                    for n, page in enumerate(pages):
                        sp.dma_start(v[:, u, n, :], T["cache_v"][bass.ds(page, 1), :, :].squeeze(0)).then_inc(v_loaded[u], 16)

                each(sp, SB, load)

            @block.gpsimd
            def _(pool):
                nc.gpsimd.memset(mask[:, :, :], 1.0).then_inc(g["masked"], 1)
                pool.wait_ge(g["masked"], 1)
                nc.gpsimd.affine_select(out=mask[:, :, :], in_=mask[:, :, :], compare_op=ALU.is_gt, fill=0.0, base=0,
                                        pattern=[[ST, SB], [1, ST]], channel_multiplier=-1).then_inc(g["masked"], 1)
                pool.wait_ge(g["masked"], 2)
                nc.gpsimd.affine_select(out=mask[:, :, :], in_=mask[:, :, :], compare_op=ALU.is_ge, fill=0.0, base=0,
                                        pattern=[[-ST, SB], [0, ST]], channel_multiplier=1).then_inc(g["masked"], 1)

            @block.tensor
            def _(pe):
                pe.sem_inc(g["turned"], 2 * NPAGE)
                pe.sem_inc(g["page_scored"], 2)
                pe.sem_inc(g["cum_done"], 2)
                pe.sem_inc(g["values_done"], 2)
                pe.wait_ge(g["q_ready"], 3)
                for f in range(FT):
                    last = nc.tensor.matmul(ps_n[0:NS, f, :, :], ks[:, f, :], q2[:, f, :, :], start=(f == 0), stop=False,
                                            skip_group_check=True)
                last.then_inc(g["new_z"], 1)
                pe.wait_ge(g["new_logs"], 2)
                nc.tensor.matmul(flat(ps_n[0:NS]), neg_from[0:NS, 0:NS], flat(zn), start=False, stop=True,
                                 skip_group_check=True)
                nc.tensor.matmul(flat(ps_c), neg_ones[0:NS, :], flat(zn), start=True, stop=True).then_inc(g["new_cum"], 1)

                pe.wait_ge(g["new_a"], 3)
                for f in range(FT):
                    last = nc.tensor.matmul(ps_y[:, f * P:(f + 1) * P], v_sb[0:NS, NT, f * P:(f + 1) * P],
                                            an[:, f, :, :].rearrange("p b c -> p (b c)"), start=True, stop=True)
                last.then_inc(g["y_new_done"], 1)
                pe.wait_ge(g["y_new_kept"], 1)

                def score(b, u, r, half):
                    if half == 0:
                        pe.wait_ge(k_loaded[u], r * (16 * NPAGE) + 16 * NPAGE)
                    first = half * NPAGE // 2
                    for n in range(first, first + NPAGE // 2 + half):
                        if n < NPAGE:
                            pe.wait_ge(g["kt_kept"], b * NPAGE + n + 1)
                            for f in range(FT):
                                last = nc.tensor.transpose(ps_t[:, n % 2, f * P:(f + 1) * P], k[:, u, n, f * P:(f + 1) * P], ident[:, :])
                            last.then_inc(g["turned"], 1)
                        if n >= 1:
                            if n == 1:
                                pe.wait_ge(g["a_in_done"], b + 1)
                            pe.wait_ge(g["kt_kept"], b * NPAGE + n + 2)
                            for f in range(FT):
                                last = nc.tensor.matmul(ps_z[:, u, n - 1, f * TWO:(f + 1) * TWO], kt[:, (n - 1) % 2, f * P:(f + 1) * P],
                                                        q2[:, f, bass.ds(b, 1), :].squeeze(1), start=(n == 1 and f == 0), stop=False,
                                                        skip_group_check=True)
                            last.then_inc(g["page_scored"], 1)

                def sums(b, u, r):
                    pe.wait_ge(g["sp_done"], b + 1)
                    nc.tensor.matmul(row(ps_z[:, u]), neg_from[:, :], row(sp_[:, u]), start=False, stop=False, skip_group_check=True)
                    pe.wait_ge(g["suf_done"], b * (NPAGE - 1) + NPAGE - 1 + 2)
                    nc.tensor.matmul(row(ps_z[:, u]), neg_ones[:, :], row(suf[:, u]), start=False, stop=True,
                                     skip_group_check=True).then_inc(g["cum_done"], 1)

                def values(b, u, r):
                    pe.wait_ge(v_loaded[u], r * (16 * NPAGE) + 16 * NPAGE)
                    pe.wait_ge(g["rows_kept"], b + 1)
                    pe.wait_ge(g["a_done"], b + 3)
                    for n in range(NPAGE):
                        last = nc.tensor.matmul(ps_y[0:HC, :], A[:, u, n, :], v[:, u, n, :], start=(n == 0), stop=(n == NPAGE - 1))
                    last.then_inc(g["values_done"], 1)

                def turn_rows(b):
                    pe.wait_ge(g["rows_kept"], b + 2)
                    pe.wait_ge(g["y_kept"], b * 2 + 1)
                    for f in range(FT):
                        last = nc.tensor.matmul(ps_o[:, f, :], y_rows[:, f * P:(f + 1) * P], ident[0:HC, f * TWO:(f + 1) * TWO],
                                                start=True, stop=True)
                    last.then_inc(g["y_turned"], 1)

                def both(b, u, r, last=False, first=False):
                    v, q = (u + 1) % 2, r + u
                    if not last:
                        score(b + 1, v, q, 0)
                    if not first:
                        turn_rows(b - 1)
                    sums(b, u, r)
                    if not last:
                        score(b + 1, v, q, 1)
                    values(b, u, r)

                score(0, 0, 0, 0)
                score(0, 0, 0, 1)
                both(0, 0, 0, first=True)
                with pe.Fori(0, (SB - 2) // 2) as i:
                    both(i * 2 + 1, 1, i)
                    both(i * 2 + 2, 0, i + 1)
                both(SB - 1, 1, SB // 2 - 1, last=True)
                turn_rows(SB - 1)

            @block.scalar
            def _(act):
                act.sem_inc(g["kt_kept"], 2)
                act.sem_inc(g["a_done"], 2)
                nc.scalar.preload_act_table_set("natural_log_exp_and_others")
                act.wait_ge(g["new_clipped"], 1)
                nc.scalar.activation(flat(cn), flat(cn), ACT.Exp).then_inc(g["new_clipped"], 1)
                act.wait_ge(g["new_clipped"], 2)
                nc.scalar.activation(flat(cn), flat(cn), ACT.Ln, bias=1.0).then_inc(g["new_clipped"], 1)
                act.wait_ge(g["new_a"], 1)
                nc.scalar.activation(flat(an), flat(an), ACT.Exp).then_inc(g["new_a"], 1)

                def keep_keys(b):
                    for n in range(NPAGE):
                        act.wait_ge(g["turned"], b * NPAGE + n + 1 + 2 * NPAGE)
                        act.wait_ge(g["page_scored"], b * NPAGE + n + 1)
                        nc.scalar.activation(kt[:, n % 2, :], ps_t[:, n % 2, :], ACT.Copy).then_inc(g["kt_kept"], 1)

                def logs(b, u):
                    act.wait_ge(g["clipped"], b + 1)
                    z = row(zc[:, u])
                    nc.scalar.activation(z, z, ACT.Exp).then_inc(g["logged"], 1)
                    act.wait_ge(g["logged"], 2 * b + 1)
                    nc.scalar.activation(z, z, ACT.Ln, bias=1.0).then_inc(g["logged"], 1)

                def weights(b, u):
                    act.wait_ge(g["values_done"], b + 1)
                    act.wait_ge(g["a_in_done"], b + 3)
                    nc.scalar.activation(row(A[:, u]), row(a_in[:, u]), ACT.Exp).then_inc(g["a_done"], 1)

                def both(b, u, r):
                    keep_keys(b + 1)
                    weights(b, u)
                    logs(b + 1, (u + 1) % 2)

                keep_keys(0)
                logs(0, 0)
                each(act, SB - 2, both)
                both(SB - 2, 0, 0)
                weights(SB - 1, 1)

            @block.vector
            def _(dve):
                count = [0]

                def step(ins, sem="did"):
                    if sem == "did":
                        count[0] += 1
                    ins.then_inc(g[sem], 1)
                    if sem == "did":
                        dve.wait_ge(g["did"], count[0])

                dve.sem_inc(g["a_in_done"], 2)
                dve.sem_inc(g["y_kept"], 2)
                dve.sem_inc(g["rows_kept"], 1)
                dve.sem_inc(g["y_turned"], 1)
                step(nc.vector.memset(flat(q2), 0.0))
                nc.vector.tensor_copy(q2[0:HD, :, :, 0:ST], qs[0:HD, :, :].rearrange("p f (b t) -> p f b t", b=SB)).then_inc(g["q_ready"], 1)
                nc.vector.tensor_copy(q2[HD:P, :, :, ST:TWO], qs[HD:P, :, :].rearrange("p f (b t) -> p f b t", b=SB)).then_inc(g["q_ready"], 1)
                dve.wait_ge(g["q_ready"], 2)
                dve.sem_inc(g["q_ready"], 1)
                nc.vector.memset(suf[:, 0, NPAGE - 1, :], 0.0).then_inc(g["suf_done"], 1)
                nc.vector.memset(suf[:, 1, NPAGE - 1, :], 0.0).then_inc(g["suf_done"], 1)
                dve.wait_ge(g["bias_loaded"], 16)
                step(nc.vector.tensor_copy(head_bias[:, :, :], bc(bias[:, :], 2, ST)))
                dve.wait_ge(g["masked"], 3)
                for f in range(FT):
                    for x_ in range(2):
                        step(nc.vector.tensor_copy(mask_n[:, f, :, x_ * ST:(x_ + 1) * ST], mask[:, :, :]))
                dve.wait_ge(g["new_z"], 1)
                hb = lambda rows, f: bc(head_bias[rows, 2 * f:2 * f + 2, :].rearrange("p h t -> p (h t)"), 1, SB)
                for f in range(FT):
                    step(nc.vector.tensor_tensor(zn[:, f, :, :], ps_n[0:NS, f, :, :], hb(slice(0, NS), f), ALU.add))
                nc.vector.tensor_scalar(flat(cn), flat(zn), CLIP, None, ALU.min).then_inc(g["new_clipped"], 1)
                dve.wait_ge(g["new_clipped"], 3)
                nc.vector.tensor_tensor(flat(zn), flat(zn), flat(cn), ALU.max).then_inc(g["new_logs"], 1)
                dve.wait_ge(g["new_logs"], 1)
                nc.vector.tensor_tensor(flat(zn), flat(zn), flat(mask_n), ALU.mult).then_inc(g["new_logs"], 1)
                dve.wait_ge(g["new_cum"], 1)
                for f in range(FT):
                    step(nc.vector.tensor_tensor(an[:, f, :, :], ps_n[0:NS, f, :, :], hb(slice(0, NS), f), ALU.add))
                    step(nc.vector.tensor_tensor(bias2[:, :, f * TWO:(f + 1) * TWO], ps_c[:, f, :, :], hb(slice(0, P), f), ALU.add))
                nc.vector.tensor_tensor(flat(an), flat(an), flat(mask_n), ALU.mult).then_inc(g["new_a"], 1)
                dve.wait_ge(g["new_a"], 2)
                nc.vector.tensor_tensor(flat(an), flat(an), flat(mask_n), ALU.mult).then_inc(g["new_a"], 1)
                dve.wait_ge(g["y_new_done"], 1)
                nc.vector.tensor_copy(flat(y_new), ps_y[:, :]).then_inc(g["y_new_kept"], 1)

                def softplus(b, u):
                    dve.wait_ge(g["page_scored"], b * NPAGE + NPAGE + 2)
                    page_bias = bc(head_bias[:, :, :].rearrange("p h t -> p (h t)"), 1, NPAGE)
                    nc.vector.tensor_tensor(zb[:, u], ps_z[:, u], page_bias, ALU.add).then_inc(g["z_read"], 1)
                    dve.wait_ge(g["z_read"], b + 1)
                    nc.vector.tensor_scalar(row(zc[:, u]), row(zb[:, u]), CLIP, None, ALU.min).then_inc(g["clipped"], 1)
                    dve.wait_ge(g["logged"], 2 * b + 2)
                    dve.wait_ge(g["cum_done"], b + 1)
                    nc.vector.tensor_tensor(row(sp_[:, u]), row(zb[:, u]), row(zc[:, u]), ALU.max).then_inc(g["sp_done"], 1)
                    dve.wait_ge(g["sp_done"], b + 1)
                    for n in range(NPAGE - 2, -1, -1):
                        dve.wait_ge(g["suf_done"], b * (NPAGE - 1) + NPAGE - n)
                        nc.vector.tensor_tensor(suf[:, u, n, :], suf[:, u, n + 1, :], sp_[:, u, n + 1, :], ALU.add).then_inc(g["suf_done"], 1)

                def weights_in(b, u):
                    dve.wait_ge(g["cum_done"], b + 3)
                    dve.wait_ge(g["a_done"], b + 1)
                    nc.vector.tensor_tensor(a_in[:, u], ps_z[:, u], bc(bias2[:, bass.ds(b, 1), :].squeeze(1), 1, NPAGE),
                                            ALU.add).then_inc(g["a_in_done"], 1)

                def keep_rows(b):
                    dve.wait_ge(g["values_done"], b + 3)
                    dve.wait_ge(g["y_turned"], b + 1)
                    nc.vector.tensor_copy(y_rows[:, :], ps_y[0:HC, :]).then_inc(g["rows_kept"], 1)

                def keep_output(b):
                    dve.wait_ge(g["y_turned"], b + 2)
                    for x_ in range(2):
                        rows, at = slice(x_ * HD, x_ * HD + HD), slice(x_ * ST, (x_ + 1) * ST)
                        nc.vector.tensor_tensor(mT[rows, KT - FT:KT, bass.ds(b * ST + SEQ, ST)], ps_o[rows, :, at],
                                                y_new[rows, :, bass.ds(b, 1), at].squeeze(2), ALU.add).then_inc(g["y_kept"], 1)

                def both(b, u, r, first=False):
                    if not first:
                        keep_output(b - 1)
                    weights_in(b, u)
                    softplus(b + 1, (u + 1) % 2)
                    keep_rows(b)

                softplus(0, 0)
                both(0, 0, 0, first=True)
                with dve.Fori(0, (SB - 2) // 2) as i:
                    both(i * 2 + 1, 1, i)
                    both(i * 2 + 2, 0, i + 1)
                keep_output(SB - 2)
                weights_in(SB - 1, 1)
                keep_rows(SB - 1)
                keep_output(SB - 1)


def out_project(nc, T, keep, mod_rows, h2_rows):
    mT, x1, logits, ident = keep["mT"], keep["x1"], keep["logits"], keep["ident"]
    NL = NGR + NE
    with Phase(nc, "op") as ph:
        w = ph.sb("w", [P, KT, D])
        wr, br = ph.sb("wr", [P, KT, NL]), ph.sb("br", [P, NL])
        g = ph.sb("g", [P, D])
        gate = {"p": ph.sb("gate_p", [P, D]), "s": ph.sb("gate_s", [NS, D])}
        gain = {"p": ph.sb("gain_p", [P, D]), "s": ph.sb("gain_s", [NS, D])}
        shift = {"p": ph.sb("shift_p", [P, D]), "s": ph.sb("shift_s", [NS, D])}
        m_t = ph.sb("m_t", [P, 2, KT, P])
        gated, squares, h2 = (ph.sb(x_, [P, 2, D]) for x_ in ("gated", "squares", "h2"))
        ht = ph.sb("ht", [P, KT, P])
        ss, ms, rt, rstd = (ph.sb(x_, [P, 2]) for x_ in ("ss", "ms", "rt", "rstd"))
        ps_o, ps_h, ps_l = ph.ps("ps_o", [P, 2, D]), ph.ps("ps_h", [P, KT, P]), ph.ps("ps_l", [P, NL])
        names = ("x_loaded w_loaded r_loaded mod_loaded gains staged product_done gated_done x1_done sq_done ms_done rt_done rstd_done "
                 "scaled h2_done turned ht_kept routed logits_kept")
        s = {x_: ph.sem(x_) for x_ in names.split()}
        stored = [ph.sem(f"stored{u}") for u in range(2)]
        with nc.Block() as block:
            @block.sync
            def _(sp):
                sp.dma_start(w[:, :, :], T["w_out"].rearrange("(k p) n -> p k n", p=P)).then_inc(s["w_loaded"], 16)
                load_mod(sp, gate["p"][:, :], gate["s"], mod_rows, 2, s["mod_loaded"])
                load_mod(sp, gain["p"][:, :], gain["s"], mod_rows, 4, s["mod_loaded"])
                load_mod(sp, shift["p"][:, :], shift["s"], mod_rows, 3, s["mod_loaded"])
                sp.dma_start(wr[:, :, 0:NGR], T["router_g_w"].rearrange("(k p) n -> p k n", p=P)).then_inc(s["r_loaded"], 16)
                sp.dma_start(wr[:, :, NGR:], T["router_e_w"].rearrange("(k p) n -> p k n", p=P)).then_inc(s["r_loaded"], 16)

                def store(n, u, r):
                    m = rows_of(n)
                    sp.wait_ge(s["h2_done"], n + 1)
                    sp.dma_start(h2_rows[bass.ds(n * P, m), :], h2[0:m, u, :]).then_inc(stored[u], 16)

                each(sp, NT + 1, store)
                sp.wait_ge(stored[0], 16 + 16 * (NT // 2 + 1))
                sp.wait_ge(stored[1], 16 + 16 * (NT // 2))

            @block.gpsimd
            def _(pool):
                pool.sem_inc(s["product_done"], 2)

                def stage(n, u, r):
                    m = rows_of(n)
                    pool.wait_ge(s["product_done"], n + 1)
                    nc.gpsimd.tensor_copy(m_t[:, u, :, 0:m], mT[:, :, bass.ds(n * P, m)]).then_inc(s["staged"], 1)

                each(pool, NT + 1, stage)

            @block.tensor
            def _(pe):
                pe.wait_ge(s["w_loaded"], 16)

                def product(n, u, r):
                    m = rows_of(n)
                    pe.wait_ge(s["staged"], n + 1)
                    pe.wait_ge(s["gated_done"], n + 1)
                    for lo in range(0, D, 512):
                        for k in range(KT):
                            last = nc.tensor.matmul(ps_o[0:m, u, lo:lo + 512], m_t[:, u, k, 0:m], w[:, k, lo:lo + 512],
                                                    start=(k == 0), stop=(k == KT - 1))
                    last.then_inc(s["product_done"], 1)

                def route(n, u, r):
                    m = rows_of(n)
                    pe.wait_ge(s["h2_done"], n + 1)
                    pe.wait_ge(s["ht_kept"], n + 1)
                    for k in range(KT):
                        last = nc.tensor.transpose(ps_h[:, k, 0:m], h2[0:m, u, k * P:(k + 1) * P], ident[0:m, 0:m])
                    last.then_inc(s["turned"], 1)
                    pe.wait_ge(s["ht_kept"], n + 2)
                    pe.wait_ge(s["logits_kept"], n + 1)
                    pe.wait_ge(s["r_loaded"], 48)
                    for k in range(KT):
                        last = nc.tensor.matmul(ps_l[0:m, :], ht[:, k, 0:m], wr[:, k, :], start=(k == 0), stop=(k == KT - 1))
                    last.then_inc(s["routed"], 1)

                ahead(pe, NT + 1, product, route)

            @block.scalar
            def _(act):
                act.dma_start(x1[:, 0:NT, :], T["x_prompt"].rearrange("(n p) d -> p n d", p=P)).then_inc(s["x_loaded"], 16)
                act.dma_start(x1[0:NS, NT, :], T["x_sample"]).then_inc(s["x_loaded"], 16)
                act.dma_start(g[:, :], T["norm2_g"].to_broadcast([P, D])).then_inc(s["r_loaded"], 16)
                act.dma_start(br[:, 0:NGR], T["router_g_b"].to_broadcast([P, NGR])).then_inc(s["mod_loaded"], 16)
                act.dma_start(br[:, NGR:], T["router_e_b"].to_broadcast([P, NE])).then_inc(s["mod_loaded"], 16)
                act.sem_inc(s["ht_kept"], 1)

                def stats(n, u, r):
                    m = rows_of(n)
                    act.wait_ge(s["x1_done"], n + 1)
                    nc.scalar.activation(squares[0:m, u, :], x1[0:m, bass.ds(n, 1), :].squeeze(1), ACT.Square,
                                         accum_out=ss[0:m, u:u + 1]).then_inc(s["sq_done"], 1)
                    act.wait_ge(s["ms_done"], n + 1)
                    nc.scalar.activation(rt[0:m, u:u + 1], ms[0:m, u:u + 1], ACT.Sqrt).then_inc(s["rt_done"], 1)

                def evacuate(n, u, r):
                    m = rows_of(n)
                    act.wait_ge(s["turned"], n + 1)
                    act.wait_ge(s["routed"], n + 1)
                    nc.scalar.activation(ht[:, :, 0:m], ps_h[:, :, 0:m], ACT.Copy).then_inc(s["ht_kept"], 1)

                ahead(act, NT + 1, stats, evacuate, back_first=True)

            @block.vector
            def _(dve):
                dve.sem_inc(s["gated_done"], 2)
                for u in range(2):
                    dve.sem_inc(stored[u], 16)
                dve.sem_inc(s["logits_kept"], 1)
                dve.sem_inc(s["routed"], 1)
                nc.vector.memset(logits[:, NT, :], 0.0).then_inc(s["gains"], 1)
                dve.wait_ge(s["r_loaded"], 48)
                dve.wait_ge(s["mod_loaded"], 3 * MOD_LOADS + 32)
                for x_, rows in (("p", P), ("s", NS)):
                    nc.vector.scalar_tensor_tensor(gain[x_][:, :], gain[x_][:, :], 1.0, g[0:rows, :],
                                                   ALU.add, ALU.mult).then_inc(s["gains"], 1)
                dve.wait_ge(s["gains"], 3)
                dve.wait_ge(s["x_loaded"], 32)

                def norm(n, u, r):
                    m = rows_of(n)
                    group = "s" if m == NS else "p"
                    x = x1[0:m, bass.ds(n, 1), :].squeeze(1)
                    dve.wait_ge(s["product_done"], n + 3)
                    nc.vector.tensor_tensor(gated[0:m, u, :], ps_o[0:m, u, :], gate[group][0:m, :], ALU.mult).then_inc(s["gated_done"], 1)
                    dve.wait_ge(s["gated_done"], n + 3)
                    nc.vector.tensor_tensor(x, x, gated[0:m, u, :], ALU.add).then_inc(s["x1_done"], 1)
                    dve.wait_ge(s["sq_done"], n + 1)
                    nc.vector.tensor_scalar(ms[0:m, u:u + 1], ss[0:m, u:u + 1], 1.0 / D, RMS_EPS,
                                            ALU.mult, ALU.add).then_inc(s["ms_done"], 1)
                    dve.wait_ge(s["rt_done"], n + 1)
                    nc.vector.reciprocal(rstd[0:m, u:u + 1], rt[0:m, u:u + 1]).then_inc(s["rstd_done"], 1)
                    dve.wait_ge(s["rstd_done"], n + 1)
                    dve.wait_ge(stored[u], r * 16 + 16)
                    nc.vector.scalar_tensor_tensor(h2[0:m, u, :], x, rstd[0:m, u:u + 1], gain[group][0:m, :],
                                                   ALU.mult, ALU.mult).then_inc(s["scaled"], 1)
                    dve.wait_ge(s["scaled"], n + 1)
                    nc.vector.tensor_tensor(h2[0:m, u, :], h2[0:m, u, :], shift[group][0:m, :], ALU.add).then_inc(s["h2_done"], 1)

                def keep_logits(n, u, r):
                    m = rows_of(n)
                    dve.wait_ge(s["routed"], n + 2)
                    nc.vector.tensor_tensor(logits[0:m, bass.ds(n, 1), :].squeeze(1), ps_l[0:m, :], br[0:m, :],
                                            ALU.add).then_inc(s["logits_kept"], 1)

                ahead(dve, NT + 1, norm, keep_logits)


def route(nc, T, keep, slot_token, tile_expert):
    logits, slots, gates, neg_ones = keep["logits"], keep["slots"], keep["gates"], keep["neg_ones"]
    N, EG = NT + 1, NE // NGR
    MAX_TILES = -(-TOK // P)
    with Phase(nc, "rt") as ph:
        low_first = ph.sb("low_first", [P, EG])
        before = ph.sb("before", [P, P])
        experts_before = ph.sb("experts_before", [P, NE, NE])
        starts, tiles_at = ph.sb("starts", [P, MAX_TILES]), ph.sb("tiles_at", [P, ET])
        token = ph.sb("token", [P, N], I32)
        zeros = ph.sb("zeros", [P, ET], I32)
        gl, el = ph.sb("gl", [P, N, EG]), ph.sb("el", [P, N, EG])
        top, total, pg, two = (ph.sb(x_, [P, N]) for x_ in ("top", "total", "pg", "two"))
        key, pick_g = ph.sb("key", [P, N, EG]), ph.sb("pick_g", [P, N, EG])
        picks = ph.sb("picks", [P, N, 2, EG])
        tmp = ph.sb("tmp", [P, N, NGR, EG])
        chosen, place = ph.sb("chosen", [P, N * 2, NE]), ph.sb("place", [P, N * 2, NE])
        run = ph.sb("run", [P, N * 2 + 1, NE])
        tiles, first = ph.sb("tiles", [P, NE]), ph.sb("first", [P, NE])
        cmp1, cmp2, cmp3 = ph.sb("cmp1", [P, NE, MAX_TILES]), ph.sb("cmp2", [P, NE, NE]), ph.sb("cmp3", [P, ET, NE])
        slot_f, expert_f = ph.sb("slot_f", [P, N * 2]), ph.sb("expert_f", [P, ET])
        expert = ph.sb("expert", [P, ET], I32)
        iota_i, iota_j = ph.sb("iota_i", [P, ET], I32), ph.sb("iota_j", [P, MAX_TILES], I32)
        ps_before, ps_total = ph.ps("ps_before", [P, N * 2, NE]), ph.ps("ps_total", [P, N * 2, NE])
        built, did, exped, counted, zeroed, stored, scattered = (ph.sem(x_) for x_ in (
            "built", "did", "exped", "counted", "zeroed", "stored", "scattered"))
        PICKED, PLACED, EXPERT = 34, 68, 72
        with nc.Block() as block:
            @block.gpsimd
            def _(pool):
                nc.gpsimd.memset(before[:, :], -1.0).then_inc(built, 1)
                nc.gpsimd.memset(experts_before[:, :, :], 1.0).then_inc(built, 1)
                nc.gpsimd.memset(zeros[:, :], 0).then_inc(built, 1)
                nc.gpsimd.iota(token[:, :], pattern=[[P, N]], base=0, channel_multiplier=1).then_inc(built, 1)
                nc.gpsimd.iota(iota_i[:, :], pattern=[[1, ET]], base=0, channel_multiplier=0).then_inc(built, 1)
                nc.gpsimd.iota(iota_j[:, :], pattern=[[P, MAX_TILES]], base=0, channel_multiplier=0).then_inc(built, 1)
                pool.wait_ge(built, 6)
                nc.gpsimd.affine_select(out=before[:, :], in_=before[:, :], compare_op=ALU.is_gt, fill=0.0, base=0,
                                        pattern=[[1, P]], channel_multiplier=-1).then_inc(built, 1)
                nc.gpsimd.affine_select(out=experts_before[:, :, :], in_=experts_before[:, :, :], compare_op=ALU.is_gt,
                                        fill=0.0, base=0, pattern=[[1, NE], [-1, NE]], channel_multiplier=0).then_inc(built, 1)
                pool.wait_ge(zeroed, 16)
                pool.wait_ge(did, PLACED)
                for n in range(N):
                    for c in range(2):
                        m = rows_of(n)
                        nc.gpsimd.indirect_dma_start(
                            slot_token, bass.IndirectOffsetOnAxis(ap=slots[0:m, n * 2 + c:n * 2 + c + 1], axis=0),
                            token[0:m, n:n + 1].bitcast(U32), None).then_inc(scattered, 16)
                pool.wait_ge(scattered, 16 * 2 * N)

            @block.sync
            def _(sp):
                sp.wait_ge(built, 6)
                sp.dma_start(slot_token.rearrange("(p t) a -> p (t a)", p=P), zeros[:, :].bitcast(U32)).then_inc(zeroed, 16)
                sp.wait_ge(did, EXPERT)
                sp.dma_start(tile_expert, expert[0:1, :]).then_inc(stored, 16)
                sp.wait_ge(stored, 16)

            @block.tensor
            def _(pe):
                pe.wait_ge(built, 8)
                pe.wait_ge(did, PICKED)
                for out, w in ((ps_before, before), (ps_total, neg_ones)):
                    nc.tensor.matmul(out[:, :, :].rearrange("p n e -> p (n e)"), w[:, :],
                                     chosen[:, :, :].rearrange("p n e -> p (n e)"), start=True, stop=True).then_inc(counted, 1)

            @block.scalar
            def _(act):
                for i, (t, after) in enumerate(((gl, 6), (el, 16))):
                    act.wait_ge(did, after)
                    nc.scalar.activation(t[:, :, :], t[:, :, :], ACT.Exp).then_inc(exped, 1)

            @block.vector
            def _(dve):
                count = [0]

                def step(ins):
                    count[0] += 1
                    ins.then_inc(did, 1)
                    dve.wait_ge(did, count[0])

                V = nc.vector

                def pick(out, values, best):
                    step(V.tensor_tensor(key[:, :, :], values, bc(best, 2, EG), ALU.is_equal))
                    step(V.tensor_tensor(key[:, :, :], key[:, :, :], bc(low_first[:, :], 1, N), ALU.mult))
                    step(V.tensor_reduce(two[:, :], key[:, :, :], axis=AXX, op=ALU.max))
                    step(V.tensor_tensor(out, key[:, :, :], bc(two[:, :], 2, EG), ALU.is_equal))

                for e in range(EG):
                    step(V.memset(low_first[:, e:e + 1], float(EG - e)))
                step(V.tensor_reduce(top[:, :], logits[:, :, 0:NGR], axis=AXX, op=ALU.max))
                step(V.tensor_tensor(gl[:, :, :], logits[:, :, 0:NGR], bc(top[:, :], 2, NGR), ALU.subtract))
                dve.wait_ge(exped, 1)
                step(V.tensor_reduce(total[:, :], gl[:, :, :], axis=AXX, op=ALU.add))
                step(V.tensor_reduce(top[:, :], gl[:, :, :], axis=AXX, op=ALU.max))
                pick(pick_g[:, :, :], gl[:, :, :], top[:, :])
                el4 = logits[:, :, NGR:].rearrange("p n (g e) -> p n g e", e=EG)
                step(V.tensor_tensor(tmp[:, :, :, :], el4, bc(pick_g[:, :, :], 3, EG), ALU.mult))
                step(V.tensor_reduce(el[:, :, :], tmp[:, :, :, :].rearrange("p n g e -> p n e g"), axis=AXX, op=ALU.add))
                step(V.tensor_reduce(top[:, :], el[:, :, :], axis=AXX, op=ALU.max))
                step(V.tensor_tensor(el[:, :, :], el[:, :, :], bc(top[:, :], 2, EG), ALU.subtract))
                dve.wait_ge(exped, 2)
                step(V.tensor_reduce(gates[:, :, 0], el[:, :, :], axis=AXX, op=ALU.max))
                pick(picks[:, :, 0, :], el[:, :, :], gates[:, :, 0])
                step(V.tensor_tensor(tmp[:, :, 0, :], el[:, :, :], picks[:, :, 0, :], ALU.mult))
                step(V.tensor_tensor(el[:, :, :], el[:, :, :], tmp[:, :, 0, :], ALU.subtract))
                step(V.tensor_tensor(el[:, :, :], el[:, :, :], picks[:, :, 0, :], ALU.subtract))
                step(V.tensor_reduce(gates[:, :, 1], el[:, :, :], axis=AXX, op=ALU.max))
                pick(picks[:, :, 1, :], el[:, :, :], gates[:, :, 1])
                for c in range(2):
                    step(V.tensor_tensor(tmp[:, :, :, :], bc(pick_g[:, :, :], 3, EG), bc(picks[:, :, c, :], 2, NGR), ALU.mult))
                    step(V.tensor_copy(chosen[:, :, :].rearrange("p (n c) e -> p n c e", c=2)[:, :, c, :],
                                       tmp[:, :, :, :].rearrange("p n g e -> p n (g e)")))
                step(V.memset(chosen[NS:P, 2 * NT:, :], 0.0))
                assert count[0] == PICKED, count[0]
                step(V.tensor_tensor(two[:, :], gates[:, :, 0], gates[:, :, 1], ALU.add))
                step(V.tensor_tensor(two[:, :], two[:, :], total[:, :], ALU.mult))
                step(V.reciprocal(pg[:, :], two[:, :]))
                step(V.tensor_tensor(gates[:, :, :], gates[:, :, :], bc(pg[:, :], 2, 2), ALU.mult))
                dve.wait_ge(built, 8)
                step(V.tensor_copy(starts[:, :], iota_j[:, :]))
                step(V.tensor_copy(tiles_at[:, :], iota_i[:, :]))
                step(V.memset(run[:, 0, :], 0.0))
                dve.wait_ge(counted, 2)
                for n in range(2 * N):
                    step(V.tensor_tensor(run[:, n + 1, :], run[:, n, :], ps_total[:, n, :], ALU.subtract))
                step(V.tensor_tensor(cmp1[:, :, :], bc(run[:, 2 * N, :], 2, MAX_TILES), bc(starts[:, :], 1, NE), ALU.is_gt))
                step(V.tensor_reduce(tiles[:, :], cmp1[:, :, :], axis=AXX, op=ALU.add))
                step(V.tensor_tensor(cmp2[:, :, :], bc(tiles[:, :], 1, NE), experts_before[:, :, :], ALU.mult))
                step(V.tensor_reduce(first[:, :], cmp2[:, :, :], axis=AXX, op=ALU.add))
                step(V.tensor_tensor(place[:, :, :], run[:, 0:2 * N, :], ps_before[:, :, :], ALU.subtract))
                step(V.scalar_tensor_tensor(place[:, :, :], bc(first[:, :], 1, 2 * N), float(P), place[:, :, :], ALU.mult, ALU.add))
                step(V.tensor_tensor(place[:, :, :], place[:, :, :], chosen[:, :, :], ALU.mult))
                step(V.tensor_reduce(slot_f[:, :], place[:, :, :], axis=AXX, op=ALU.add))
                step(V.tensor_copy(slots[:, :], slot_f[:, :]))
                assert count[0] == PLACED, count[0]
                step(V.tensor_tensor(cmp3[:, :, :], bc(tiles_at[:, :], 2, NE), bc(first[:, :], 1, ET), ALU.is_ge))
                step(V.tensor_reduce(expert_f[:, :], cmp3[:, :, :], axis=AXX, op=ALU.add))
                step(V.tensor_scalar(expert_f[:, :], expert_f[:, :], -1.0, None, ALU.add))
                step(V.tensor_copy(expert[:, :], expert_f[:, :]))
                assert count[0] == EXPERT, count[0]


def experts(nc, T, keep, h2_rows, slot_token, tile_expert, slot_rows):
    ident = keep["ident"]
    FK = DE // P
    with Phase(nc, "ex") as ph:
        w1, wd = ph.sb("w1", [P, 2, KT, 2 * DE]), ph.sb("wd", [P, 2, FK, D])
        token = ph.sb("token", [P, 2], U32)
        x, xt = ph.sb("x", [P, 2, D]), ph.sb("xt", [P, KT, P])
        hid, hid_T = ph.sb("hid", [P, 2, DE]), ph.sb("hid_T", [P, FK, P])
        y = ph.sb("y", [P, 2, D])
        ps_x, ps_g = ph.ps("ps_x", [P, KT, P]), ph.ps("ps_g", [P, 2, 2 * DE])
        ps_h, ps_y = ph.ps("ps_h", [P, FK, P]), ph.ps("ps_y", [P, D])
        names = ("turned x_kept gu_done gated hid_done hid_turned hid_kept down_done y_kept passed gather_passed")
        s = {x_: ph.sem(x_) for x_ in names.split()}
        w1_loaded, wd_loaded, token_loaded, gathered, stored = ([ph.sem(f"{x_}{u}") for u in range(2)] for x_ in (
            "w1_loaded", "wd_loaded", "token_loaded", "gathered", "stored"))
        with nc.Block() as block:
            @block.sync
            def _(sp):
                def load_tokens(i, u):
                    wait_apart(sp, s["turned"], i + 1, s["passed"])
                    sp.dma_start(token[:, u:u + 1], slot_token[bass.ds(i * P, P), :]).then_inc(token_loaded[u], 16)

                def load_w1(i, u):
                    e = sp.value_load(tile_expert[0:1, bass.ds(i, 1)], min_val=0, max_val=NE - 1)
                    wait_apart(sp, s["gu_done"], i + 1, s["passed"])
                    for x_, name in enumerate(("exp_wg", "exp_wu")):
                        sp.dma_start(w1[:, u, :, x_ * DE:(x_ + 1) * DE],
                                     T[name][bass.ds(e, 1), :, :].squeeze(0).rearrange("(p k) f -> p k f", k=KT)).then_inc(w1_loaded[u], 16)

                def load_wd(i, u):
                    e = sp.value_load(tile_expert[0:1, bass.ds(i, 1)], min_val=0, max_val=NE - 1)
                    wait_apart(sp, s["down_done"], i + 1, s["passed"])
                    sp.dma_start(wd[:, u, :, :], T["exp_wd"][bass.ds(e, 1), :, :].squeeze(0).rearrange("(p k) d -> p k d", k=FK)
                                 ).then_inc(wd_loaded[u], 16)

                def load(i, u, r):
                    load_w1(i + 1, (u + 1) % 2)
                    load_tokens(i + 2, u)
                    load_wd(i, u)

                load_tokens(0, 0)
                load_w1(0, 0)
                load_tokens(1, 1)
                each(sp, ET - 2, load)
                load_w1(ET - 1, 1)
                load_wd(ET - 2, 0)
                load_wd(ET - 1, 1)

            @block.gpsimd
            def _(pool):
                def gather(i, u, r):
                    wait_apart(pool, token_loaded[u], r * 16 + 16, s["gather_passed"])
                    nc.gpsimd.indirect_dma_start(x[:, u, :], None, h2_rows,
                                                 bass.IndirectOffsetOnAxis(ap=token[:, u:u + 1], axis=0)).then_inc(gathered[u], 16)

                each(pool, ET, gather)

            @block.tensor
            def _(pe):
                pe.sem_inc(s["turned"], 2)
                pe.sem_inc(s["gu_done"], 2)
                pe.sem_inc(s["down_done"], 2)

                def turn(i, u, r):
                    pe.wait_ge(gathered[u], r * 16 + 16)
                    pe.wait_ge(s["x_kept"], i + 1)
                    for k in range(KT):
                        last = nc.tensor.transpose(ps_x[:, k, :], x[:, u, :].rearrange("t (p k) -> t k p", k=KT)[:, k, :], ident[:, :])
                    last.then_inc(s["turned"], 1)

                def gate_up(i, u, r):
                    pe.wait_ge(w1_loaded[u], r * 32 + 32)
                    pe.wait_ge(s["x_kept"], i + 2)
                    pe.wait_ge(s["hid_done"], i + 1)
                    for k in range(KT):
                        last = nc.tensor.matmul(ps_g[:, u, :], xt[:, k, :], w1[:, u, k, :], start=(k == 0), stop=(k == KT - 1))
                    last.then_inc(s["gu_done"], 1)

                def turn_hidden(i, u, r):
                    pe.wait_ge(s["hid_done"], i + 3)
                    pe.wait_ge(s["hid_kept"], i + 1)
                    for k in range(FK):
                        last = nc.tensor.transpose(ps_h[:, k, :], hid[:, u, :].rearrange("t (p k) -> t k p", k=FK)[:, k, :], ident[:, :])
                    last.then_inc(s["hid_turned"], 1)

                def down(i, u, r):
                    pe.wait_ge(wd_loaded[u], r * 16 + 16)
                    pe.wait_ge(s["hid_kept"], i + 2)
                    pe.wait_ge(s["y_kept"], i + 1)
                    for lo in range(0, D, 512):
                        for k in range(FK):
                            last = nc.tensor.matmul(ps_y[:, lo:lo + 512], hid_T[:, k, :], wd[:, u, k, lo:lo + 512],
                                                    start=(k == 0), stop=(k == FK - 1))
                    last.then_inc(s["down_done"], 1)

                turn(0, 0, 0)
                gate_up(0, 0, 0)
                turn(1, 1, 0)
                turn_hidden(0, 0, 0)
                gate_up(1, 1, 0)

                def both(i, u, r):
                    turn(i + 2, u, r + 1)
                    down(i, u, r)
                    turn_hidden(i + 1, (u + 1) % 2, r + u)
                    gate_up(i + 2, u, r + 1)

                each(pe, ET - 2, both)
                down(ET - 2, 0, ET // 2 - 1)
                turn_hidden(ET - 1, 1, ET // 2 - 1)
                down(ET - 1, 1, ET // 2 - 1)

            @block.scalar
            def _(act):
                act.sem_inc(s["y_kept"], 1)
                for u in range(2):
                    act.sem_inc(stored[u], 16)

                def front(i, u, r):
                    act.wait_ge(s["gu_done"], i + 3)
                    act.wait_ge(s["hid_turned"], i + 1)
                    nc.scalar.activation(hid[:, u, :], ps_g[:, u, 0:DE], ACT.Silu).then_inc(s["gated"], 1)

                def back(i, u, r):
                    act.wait_ge(s["down_done"], i + 3)
                    act.wait_ge(stored[u], r * 16 + 16)
                    nc.scalar.activation(y[:, u, :], ps_y[:, :], ACT.Copy).then_inc(s["y_kept"], 1)
                    act.wait_ge(s["y_kept"], i + 2)
                    act.dma_start(slot_rows[bass.ds(i * P, P), :], y[:, u, :]).then_inc(stored[u], 16)

                ahead(act, ET, front, back, lead=2, back_first=True)
                for u in range(2):
                    act.wait_ge(stored[u], 16 + ET // 2 * 16)

            @block.vector
            def _(dve):
                dve.sem_inc(s["x_kept"], 1)
                dve.sem_inc(s["hid_done"], 2)
                dve.sem_inc(s["hid_kept"], 1)
                dve.sem_inc(s["hid_turned"], 2)

                def keep_x(i):
                    dve.wait_ge(s["turned"], i + 3)
                    dve.wait_ge(s["gu_done"], i + 2)
                    nc.vector.tensor_copy(xt[:, :, :], ps_x[:, :, :]).then_inc(s["x_kept"], 1)

                def up(i, u):
                    dve.wait_ge(s["gated"], i + 1)
                    nc.vector.tensor_tensor(hid[:, u, :], hid[:, u, :], ps_g[:, u, DE:], ALU.mult).then_inc(s["hid_done"], 1)

                def keep_hidden(i):
                    dve.wait_ge(s["hid_turned"], i + 3)
                    dve.wait_ge(s["down_done"], i + 2)
                    nc.vector.tensor_copy(hid_T[:, :, :], ps_h[:, :, :]).then_inc(s["hid_kept"], 1)

                keep_x(0)
                up(0, 0)

                def both(i, u, r):
                    keep_x(i + 1)
                    keep_hidden(i)
                    up(i + 1, (u + 1) % 2)

                each(dve, ET - 2, both)
                both(ET - 2, 0, ET // 2 - 1)
                keep_hidden(ET - 1)


def combine(nc, T, keep, mod_rows, slot_rows):
    x1, slots, gates = keep["x1"], keep["slots"], keep["gates"]
    with Phase(nc, "cb") as ph:
        rows0, rows1 = ph.sb("rows0", [P, 2, D]), ph.sb("rows1", [P, 2, D])
        gate = {"p": ph.sb("gate_p", [P, D]), "s": ph.sb("gate_s", [NS, D])}
        final = ph.sb("final", [P, D])
        squares, y = ph.sb("squares", [P, 2, D]), ph.sb("y", [P, 2, D])
        ss, ms, rt, rstd = (ph.sb(x_, [P, 2]) for x_ in ("ss", "ms", "rt", "rstd"))
        names = "loaded weighted summed sq_done ms_done rt_done rstd_done y_done steps passed"
        s = {x_: ph.sem(x_) for x_ in names.split()}
        gathered, stored = ([ph.sem(f"{x_}{u}") for u in range(2)] for x_ in ("gathered", "stored"))
        y_tiles = T["y_prompt"].rearrange("(n p) d -> n p d", p=P)
        with nc.Block() as block:
            @block.gpsimd
            def _(pool):
                for n in range(NT + 1):
                    m, u = rows_of(n), n % 2
                    if n >= 2:
                        pool.wait_ge(s["summed"], n - 1)
                    for c, rows in enumerate((rows0, rows1)):
                        nc.gpsimd.indirect_dma_start(rows[0:m, u, :], None, slot_rows, bass.IndirectOffsetOnAxis(
                            ap=slots[0:m, n * 2 + c:n * 2 + c + 1], axis=0)).then_inc(gathered[u], 16)

            @block.sync
            def _(sp):
                load_mod(sp, gate["p"][:, :], gate["s"], mod_rows, 5, s["loaded"])
                sp.dma_start(final[:, :], T["final_g"].to_broadcast([P, D])).then_inc(s["loaded"], 16)
                for u in range(2):
                    sp.sem_inc(stored[u], 16)

                def store(n, u, r):
                    sp.wait_ge(s["y_done"], n + 1)
                    out = T["y_sample"] if rows_of(n) == NS else y_tiles[bass.ds(n, 1), :, :].squeeze(0)
                    sp.dma_start(out, y[0:rows_of(n), u, :]).then_inc(stored[u], 16)

                each(sp, NT + 1, store)
                sp.wait_ge(stored[0], 16 + 16 * (NT // 2 + 1))
                sp.wait_ge(stored[1], 16 + 16 * (NT // 2))

            @block.scalar
            def _(act):
                def stats(n, u, r):
                    m = rows_of(n)
                    act.wait_ge(s["summed"], n + 1)
                    nc.scalar.activation(squares[0:m, u, :], x1[0:m, bass.ds(n, 1), :].squeeze(1), ACT.Square,
                                         accum_out=ss[0:m, u:u + 1]).then_inc(s["sq_done"], 1)
                    act.wait_ge(s["ms_done"], n + 1)
                    nc.scalar.activation(rt[0:m, u:u + 1], ms[0:m, u:u + 1], ACT.Sqrt).then_inc(s["rt_done"], 1)

                each(act, NT + 1, stats)

            @block.vector
            def _(dve):
                dve.wait_ge(s["loaded"], MOD_LOADS + 16)

                def add(n, u, r):
                    m = rows_of(n)
                    group = "s" if m == NS else "p"
                    x = x1[0:m, bass.ds(n, 1), :].squeeze(1)
                    a, b = rows0[0:m, u, :], rows1[0:m, u, :]
                    g0, g1 = (gates[0:m, bass.ds(n, 1), c:c + 1].squeeze(1) for c in range(2))
                    dve.wait_ge(gathered[u], r * 32 + 32)
                    nc.vector.tensor_scalar(a, a, g0, None, ALU.mult).then_inc(s["steps"], 1)
                    dve.wait_ge(s["steps"], n * 3 + 1)
                    nc.vector.scalar_tensor_tensor(a, b, g1, a, ALU.mult, ALU.add).then_inc(s["steps"], 1)
                    dve.wait_ge(s["steps"], n * 3 + 2)
                    nc.vector.tensor_tensor(a, a, gate[group][0:m, :], ALU.mult).then_inc(s["steps"], 1)
                    dve.wait_ge(s["steps"], n * 3 + 3)
                    nc.vector.tensor_tensor(x, x, a, ALU.add).then_inc(s["summed"], 1)

                def norm(n, u, r):
                    m = rows_of(n)
                    x = x1[0:m, bass.ds(n, 1), :].squeeze(1)
                    dve.wait_ge(s["sq_done"], n + 1)
                    nc.vector.tensor_scalar(ms[0:m, u:u + 1], ss[0:m, u:u + 1], 1.0 / D, RMS_EPS,
                                            ALU.mult, ALU.add).then_inc(s["ms_done"], 1)
                    dve.wait_ge(s["rt_done"], n + 1)
                    nc.vector.reciprocal(rstd[0:m, u:u + 1], rt[0:m, u:u + 1]).then_inc(s["rstd_done"], 1)
                    dve.wait_ge(s["rstd_done"], n + 1)
                    dve.wait_ge(stored[u], r * 16 + 16)
                    nc.vector.scalar_tensor_tensor(y[0:m, u, :], x, rstd[0:m, u:u + 1], final[0:m, :],
                                                   ALU.mult, ALU.mult).then_inc(s["y_done"], 1)

                ahead(dve, NT + 1, add, norm)


def build(nc, T, scratch):
    keep = {}
    mod_rows = scratch("mod_rows", [SB + 1, 6 * D])
    h2_rows, slot_rows = scratch("h2_rows", [TOK, D]), scratch("slot_rows", [ET * P, D])
    slot_token, tile_expert = scratch("slot_token", [ET * P, 1], U32), scratch("tile_expert", [1, ET], I32)
    with Phase(nc, "all") as whole:
        for name in ("ident", "head_ones", "neg_from", "neg_ones"):
            keep[name] = whole.sb(name, [P, P])
        keep["mT"] = whole.sb("mT", [P, KT, TOK])
        modulation(nc, T, keep, mod_rows)
        with Phase(nc, "kv") as kv:
            keep["v_sb"] = kv.sb("v_sb", [P, NT + 1, SBW])
            keep["qs"] = kv.sb("qs", [P, SH // 2, NS])
            keep["ks"] = kv.sb("ks", [P, SH // 2, NS])
            with Phase(nc, "mix") as mix:
                keep["hT"] = mix.sb("hT", [P, KT, TOK])
                keep["v_g"] = mix.sb("v_g", [P, NT + 1, GW])
                norm1(nc, T, keep, mod_rows)
                with Phase(nc, "rwkv") as rw:
                    keep["R"] = rw.sb("R", [P, RF, TOK])
                    keep["B"] = rw.sb("B", [P, 4, 2, TOK])
                    keep["ends"] = rw.sb("ends", [P, 2, NC + SB])
                    rwkv_project(nc, T, keep)
                    rwkv_prepare(nc, T, keep)
                    rwkv_chunks(nc, T, keep)
                rwkv_finish(nc, T, keep)
                gated_mlp(nc, T, keep)
                attention(nc, T, keep)
            sampled_attention(nc, T, keep)
        keep["x1"] = whole.sb("x1", [P, NT + 1, D])
        keep["logits"] = whole.sb("logits", [P, NT + 1, NGR + NE])
        keep["slots"] = whole.sb("slots", [P, 2 * (NT + 1)], U32)
        keep["gates"] = whole.sb("gates", [P, NT + 1, 2])
        out_project(nc, T, keep, mod_rows, h2_rows)
        route(nc, T, keep, slot_token, tile_expert)
        experts(nc, T, keep, h2_rows, slot_token, tile_expert, slot_rows)
        combine(nc, T, keep, mod_rows, slot_rows)


INPUTS = ['x_prompt', 'x_sample', 'cache_k', 'cache_v', 'page_table', 'state_rwkv', 'state_rwkv_shift', 'c_prompt',
          'c_sample', 'norm1_g', 'norm2_g', 'w_mod', 'b_mod', 'w_in', 'rwkv_mu', 'rwkv_w0', 'rwkv_w_up', 'rwkv_a0',
          'rwkv_a_up', 'rwkv_g_up', 'rwkv_k_k', 'rwkv_k_a', 'rwkv_r_k', 'rwkv_ln_g', 'rwkv_ln_b', 'gmlp_ln_g',
          'gmlp_ln_b', 'gmlp_ws', 'gmlp_bs', 'sb_bias', 'w_out', 'router_g_w', 'router_g_b', 'router_e_w',
          'router_e_b', 'exp_wg', 'exp_wu', 'exp_wd', 'final_g']
SHAPES = {'x_prompt': (SEQ, D), 'x_sample': (NS, D), 'cache_k': (80, PAGE, SBW), 'cache_v': (80, PAGE, SBW),
          'page_table': (1, SB * NPAGE), 'state_rwkv': (SB, RH, HD, HD), 'state_rwkv_shift': (SB, RPROJ),
          'final_g': (1, D), 'w_mod': (D, 6 * D), 'w_in': (D, 2944), 'w_out': (D, D), 'rwkv_w_up': (32, RW),
          'rwkv_a_up': (32, RW), 'rwkv_g_up': (64, RW), 'rwkv_r_k': (1, RW), 'gmlp_ws': (GG, P, P),
          'gmlp_bs': (GG, P), 'router_g_w': (D, 4), 'router_e_w': (D, NE), 'exp_wg': (NE, D, DE),
          'exp_wu': (NE, D, DE), 'exp_wd': (NE, DE, D)}
OUTPUTS = [('y_prompt', (SEQ, D), (1, SEQ, D)), ('y_sample', (NS, D), (SB, ST, D)),
           ('k_prompt', (SEQ, SBW), (1, 1, SEQ, SH, HD)), ('v_prompt', (SEQ, SBW), (1, 1, SEQ, SH, HD)),
           ('k_sample', (NS, SBW), (1, SB, ST, SH, HD)), ('v_sample', (NS, SBW), (1, SB, ST, SH, HD)),
           ('S_prompt', (RH, HD, HD), (1, 1, RH, HD, HD)), ('shift_prompt', (1, RPROJ), (1, 1, RPROJ)),
           ('S_sample', (SB, RH, HD, HD), (1, SB, RH, HD, HD)), ('shift_sample', (SB, RPROJ), (1, SB, RPROJ)),
           ('g_v_sample', (NS, GW), (1, SB, ST, GW))]


def program(nc, inputs):
    arrays, T = {}, {}
    for name in INPUTS:
        a = np.ascontiguousarray(inputs[name])
        a = a.reshape(SHAPES.get(name, a.shape))
        arrays[f"in_{name}"] = a
        T[name] = nc.dram_tensor(f"in_{name}", a.shape, mybir.dt.from_np(a.dtype), kind="ExternalInput").ap()
    for name, shape, _ in OUTPUTS:
        T[name] = nc.dram_tensor(f"out_{name}", shape, F32, kind="ExternalOutput").ap()

    def scratch(name, shape, dt=F32):
        return nc.dram_tensor(name, tuple(shape), dt, kind="Internal").ap()

    build(nc, T, scratch)
    return arrays


def kernel(**inputs):
    import concourse.bacc as bacc
    from concourse.bass_utils import run_bass_kernel_spmd

    nc = bacc.Bacc("TRN2", target_bir_lowering=False, num_devices=1)
    arrays = program(nc, inputs)
    got = run_bass_kernel_spmd(nc, [arrays], core_ids=[0]).results[0]
    return tuple(got[f"out_{name}"].reshape(shape) for name, _, shape in OUTPUTS)
```

```python
from contextlib import ExitStack

import numpy as np

import concourse.bass as bass
from concourse import mybir

F32 = mybir.dt.float32
I32 = mybir.dt.int32
U32 = mybir.dt.uint32
ALU = mybir.AluOpType
ACT = mybir.ActivationFunctionType
AXX = mybir.AxisListType.X

P = 128
D = 1024
KT = D // P
SEQ, SB, ST = 1024, 8, 8
NS = SB * ST
TOK = SEQ + NS
NT = SEQ // P
COLS = ((0, 512), (512, 1024), (1024, TOK))
HD = 64
RW, RH = 256, 4
RPROJ = 896
RF = RPROJ // P
GW, GG = 256, 4
SBW, SH = 512, 8
OG = RPROJ
OQ = OG + 2 * GW
PAGE, NPAGE = 128, 8
NE, DE, NGR = 16, 256, 4
ET = (2 * TOK + NE * (P - 1)) // P
C = 64
NC = SEQ // C
RMS_EPS, GN_EPS, LN_EPS = 1e-6, 64e-5, 1e-5
DECAY = float(np.exp(-0.5))


def each(eng, n, body, unroll=2):
    full = n // unroll
    if full > 1:
        with eng.Fori(0, full) as i:
            for u in range(unroll):
                body(i * unroll + u, u, i)
    else:
        for t in range(full * unroll):
            body(t, t % unroll, t // unroll)
    for t in range(full * unroll, n):
        body(t, t % unroll, t // unroll)


def ahead(eng, n, front, back, lead=1, back_first=False):
    looped = (n - 1 - lead) // 2 * 2
    for t in range(lead):
        front(t, t % 2, t // 2)

    def both(t, u, r):
        if back_first:
            back(t, u, r)
        front(t + lead, (u + lead) % 2, r + (u + lead) // 2)
        if not back_first:
            back(t, u, r)

    each(eng, looped, both)
    for t in range(looped, n - lead):
        both(t, t % 2, t // 2)
    for t in range(n - lead, n):
        back(t, t % 2, t // 2)


def wait_apart(eng, sem, value, passed):
    eng.wait_ge(sem, value)
    eng.sem_inc(passed, 1)


class Phase:

    def __init__(self, nc, name):
        self.nc, self.name, self.ctx = nc, name, ExitStack()
        self.semaphores = []

    def __enter__(self):
        return self

    def __exit__(self, *_):
        if self.semaphores:
            self.nc.clear_and_free_semaphores(self.semaphores)
            self.nc.all_engine_barrier()
        self.ctx.close()

    def sb(self, name, shape, dt=F32):
        return self.ctx.enter_context(self.nc.sbuf_tensor(f"{self.name}_{name}", shape, dt))

    def ps(self, name, shape, dt=F32):
        return self.ctx.enter_context(self.nc.psum_tensor(f"{self.name}_{name}", shape, dt))

    def sem(self, name):
        self.semaphores.append(self.nc.alloc_semaphore(name=f"{self.name}_{name}"))
        return self.semaphores[-1]


def bc(ap, axis, n):
    return ap.unsqueeze(axis).to_broadcast([*ap.shape[:axis], n, *ap.shape[axis:]])


def constants(nc, ph, keep):
    ident, head_ones, neg_from, neg_ones = (keep[k] for k in ("ident", "head_ones", "neg_from", "neg_ones"))
    built = ph.sem("const_built")

    def build(pool):
        def fill(ap, value):
            nc.gpsimd.memset(ap, value).then_inc(built, 1)

        for at, half in enumerate((0, HD)):
            fill(head_ones[half:half + HD, half:half + HD], 1.0)
            pool.wait_ge(built, 2 * at + 1)
            fill(head_ones[half:half + HD, HD - half:P - half], 0.0)
            pool.wait_ge(built, 2 * at + 2)
        fill(ident[:, :], 0.0)
        fill(neg_from[:, :], -1.0)
        fill(neg_ones[:, :], -1.0)
        pool.wait_ge(built, 7)
        nc.gpsimd.affine_select(out=ident[:, :], in_=ident[:, :], compare_op=ALU.not_equal, fill=1.0,
                                base=0, pattern=[[-1, P]], channel_multiplier=1).then_inc(built, 1)
        nc.gpsimd.affine_select(out=neg_from[:, :], in_=neg_from[:, :], compare_op=ALU.is_ge, fill=0.0,
                                base=0, pattern=[[-1, P]], channel_multiplier=1).then_inc(built, 1)
        pool.wait_ge(built, 9)

    return build, built


MOD_COLS = 512
MOD_LATE = range(3 * D // MOD_COLS, 6 * D // MOD_COLS)


def early_places(keep):
    return keep["mT"][:, :, 0:GW + SBW], keep["R"][:, 2:4, 0:D]


def modulation(nc, T, keep, mod_rows):
    W, NM, WC = 3, 3 * D, MOD_COLS
    R = SB + 1
    w_view = T["w_mod"].rearrange("(k p) n -> p k n", p=P)
    with Phase(nc, "mod") as ph:
        c_in, c_act = ph.sb("c_in", [R, D]), ph.sb("c_act", [R, D])
        c_T = keep["c_T"]
        w = ph.sb("w", [P, W, KT, WC])
        bias, rows = ph.sb("bias", [R, NM]), ph.sb("sums", [R, NM])
        ps_T = ph.ps("ps_T", [P, KT, R])
        ps = ph.ps("ps", [P, W, WC])
        build, built = constants(nc, ph, keep)
        c_loaded, b_loaded, silu_done, cT_ready = (ph.sem(x) for x in ("c_loaded", "b_loaded", "silu_done", "cT_ready"))
        c_turned = ph.sem("c_turned")
        w_loaded = [ph.sem(f"w_loaded{u}") for u in range(W)]
        prod_done, row_done, stored = ph.sem("prod_done"), ph.sem("row_done"), ph.sem("stored")
        with nc.Block() as block:
            @block.gpsimd
            def _(pool):
                build(pool)

            @block.sync
            def _(sp):
                sp.dma_start(c_in[0:SB, :], T["c_sample"]).then_inc(c_loaded, 16)
                sp.dma_start(c_in[SB:R, :], T["c_prompt"]).then_inc(c_loaded, 16)
                sp.dma_start(bias[:, :], T["b_mod"][:, 0:NM].to_broadcast([R, NM])).then_inc(b_loaded, 16)

                def load(n, u, r):
                    sp.wait_ge(prod_done, n + 1)
                    sp.dma_start(w[:, u, :, :], w_view[:, :, bass.ds(n * WC, WC)]).then_inc(w_loaded[u], 16)

                each(sp, NM // WC, load, W)
                wv, x = early_places(keep)
                columns = T["w_in"].rearrange("(k p) n -> p k n", p=P)
                for lo, hi, at in ((0, GW, OG + GW), (GW, GW + SBW, OQ + 2 * SBW)):
                    sp.dma_start(wv[:, :, lo:hi], columns[:, :, at:at + hi - lo]).then_inc(keep["wv_loaded"], 16)
                for n in range(2):
                    sp.dma_start(x[:, n, :], T["x_prompt"][n * P:(n + 1) * P, :]).then_inc(keep["x_loaded"][n], 16)
                sp.wait_ge(row_done, NM // WC + W)
                sp.dma_start(mod_rows[:, 0:NM], rows[:, :]).then_inc(stored, 16)
                sp.wait_ge(stored, 16)

            @block.scalar
            def _(act):
                act.wait_ge(c_loaded, 32)
                nc.scalar.activation(c_act[:, :], c_in[:, :], ACT.Silu).then_inc(silu_done, 1)

            @block.tensor
            def _(pe):
                pe.sem_inc(prod_done, W)
                pe.wait_ge(built, 9)
                pe.wait_ge(silu_done, 1)
                for k in range(KT):
                    last = nc.tensor.transpose(ps_T[:, k, :], c_act[:, k * P:(k + 1) * P], keep["ident"][0:R, 0:R])
                last.then_inc(c_turned, 1)
                pe.wait_ge(cT_ready, 1)

                def product(n, u, r):
                    pe.wait_ge(w_loaded[u], r * 16 + 16)
                    pe.wait_ge(row_done, n + 1)
                    for k in range(KT):
                        last = nc.tensor.matmul(ps[0:R, u, :], c_T[:, k, :], w[:, u, k, :],
                                                start=(k == 0), stop=(k == KT - 1))
                    last.then_inc(prod_done, 1)

                each(pe, NM // WC, product, W)

            @block.vector
            def _(dve):
                dve.sem_inc(row_done, W)
                dve.wait_ge(c_turned, 1)
                nc.vector.tensor_copy(c_T[:, :, :], ps_T[:, :, :]).then_inc(cT_ready, 1)
                dve.wait_ge(b_loaded, 16)

                def add_bias(n, u, r):
                    dve.wait_ge(prod_done, W + n + 1)
                    nc.vector.tensor_tensor(rows[:, bass.ds(n * WC, WC)], ps[0:R, u, :],
                                            bias[:, bass.ds(n * WC, WC)], ALU.add).then_inc(row_done, 1)

                each(dve, NM // WC, add_bias, W)


def rows_of(n):
    return NS if isinstance(n, int) and n == NT else P


def load_mod(eng, dst, mod_rows, what, loaded):
    eng.dma_start(dst[:, :], mod_rows[SB:SB + 1, what * D:(what + 1) * D].to_broadcast([P, D])).then_inc(loaded, 16)


def load_mod_sampled(eng, dst, mod_rows, what, loaded):
    for b in range(SB):
        eng.dma_start(dst[b * ST:(b + 1) * ST, :],
                      mod_rows[b:b + 1, what * D:(what + 1) * D].to_broadcast([ST, D])).then_inc(loaded, 16)


def norm1(nc, T, keep, mod_rows):
    hT, v_sb, v_g = keep["hT"], keep["v_sb"], keep["v_g"]
    w_view = T["w_in"].rearrange("(k p) n -> p k n", p=P)
    x_tiles = T["x_prompt"].rearrange("(n p) d -> n p d", p=P)
    with Phase(nc, "n1") as ph:
        wv, x = early_places(keep)
        wv_loaded, x_loaded = keep["wv_loaded"], keep["x_loaded"]
        h = ph.sb("h", [P, 2, D])
        squares = ph.sb("squares", [P, 2, D])
        ht = ph.sb("ht", [P, 2, KT, P])
        gain = {"p": ph.sb("gain_p", [P, D]), "s": ph.sb("gain_s", [NS, D])}
        shift = {"p": ph.sb("shift_p", [P, D]), "s": ph.sb("shift_s", [NS, D])}
        g = ph.sb("g", [P, D])
        ss, ms, rt, rstd = (ph.sb(x_, [P, 2]) for x_ in ("ss", "ms", "rt", "rstd"))
        ps_h = ph.ps("ps_h", [P, 2, KT, P])
        ps_v = ph.ps("ps_v", [P, 2, 1024])
        (mod_loaded, x_free, sq_done, ms_done, rt_done, rstd_done, h_done, turned, ht_ready,
         copied, v_done, v_kept, gains, mod_s_loaded) = (ph.sem(x_) for x_ in (
             "mod_loaded", "x_free", "sq_done", "ms_done", "rt_done", "rstd_done", "h_done",
             "turned", "ht_ready", "copied", "v_done", "v_kept", "gains", "mod_s_loaded"))
        with nc.Block() as block:
            @block.sync
            def _(sp):
                sp.dma_start(g[:, :], T["norm1_g"].to_broadcast([P, D])).then_inc(mod_loaded, 16)
                load_mod(sp, gain["p"], mod_rows, 1, mod_loaded)
                load_mod(sp, shift["p"], mod_rows, 0, mod_loaded)

                def load(n, u, r):
                    sp.wait_ge(x_free, n + 1)
                    src = T["x_sample"] if rows_of(n) == NS else x_tiles[bass.ds(n, 1), :, :].squeeze(0)
                    sp.dma_start(x[0:rows_of(n), u, :], src).then_inc(x_loaded[u], 16)

                with sp.Fori(1, NT // 2) as i:
                    for u in range(2):
                        load(i * 2 + u, u, i)
                load(NT, 0, NT // 2)
                for x_ in range(2):
                    sp.dma_start(keep["R"][:, x_, 0:KT // 2 * GW].rearrange("p (k c) -> p k c", c=GW),
                                 w_view[:, x_ * KT // 2:(x_ + 1) * KT // 2, OG:OG + GW]).then_inc(keep["w_u_loaded"], 16)
                sp.wait_ge(v_kept, 2 * (NT + 1) + 4)
                sp.dma_start(T["v_prompt"].rearrange("(n p) c -> p n c", p=P), v_sb[:, 0:NT, :]).then_inc(keep["v_stored"], 16)
                sp.dma_start(T["v_sample"], v_sb[0:NS, NT, :]).then_inc(keep["v_stored"], 16)

            @block.scalar
            def _(act):
                act.sem_inc(ht_ready, 2)

                def stats(n, u, r):
                    m = rows_of(n)
                    act.wait_ge(x_loaded[u], r * 16 + 16)
                    nc.scalar.activation(squares[0:m, u, :], x[0:m, u, :], ACT.Square,
                                         accum_out=ss[0:m, u:u + 1]).then_inc(sq_done, 1)
                    act.wait_ge(ms_done, n + 1)
                    nc.scalar.activation(rt[0:m, u:u + 1], ms[0:m, u:u + 1], ACT.Sqrt).then_inc(rt_done, 1)

                def evacuate(n, u, r):
                    m = rows_of(n)
                    act.wait_ge(turned, n + 3)
                    act.wait_ge(copied, n + 1)
                    act.wait_ge(v_done, n + 1)
                    nc.scalar.activation(ht[:, u, :, 0:m], ps_h[:, u, :, 0:m], ACT.Copy).then_inc(ht_ready, 1)

                ahead(act, NT + 1, stats, evacuate)

            @block.gpsimd
            def _(pool):
                load_mod_sampled(pool, gain["s"], mod_rows, 1, mod_s_loaded)
                load_mod_sampled(pool, shift["s"], mod_rows, 0, mod_s_loaded)
                pool.sem_inc(copied, 2)

                def copy(n, u, r):
                    m = rows_of(n)
                    pool.wait_ge(ht_ready, n + 3)
                    nc.gpsimd.tensor_copy(hT[:, :, bass.ds(n * P, m)], ht[:, u, :, 0:m]).then_inc(copied, 1)

                each(pool, NT + 1, copy)

            @block.vector
            def _(dve):
                dve.sem_inc(x_free, 2)
                dve.sem_inc(v_kept, 4)
                dve.wait_ge(mod_loaded, 16 * 3)
                nc.vector.scalar_tensor_tensor(gain["p"][:, :], gain["p"][:, :], 1.0, g[:, :],
                                               ALU.add, ALU.mult).then_inc(gains, 1)
                dve.wait_ge(gains, 1)

                def norm(n, u, r):
                    m = rows_of(n)
                    group = "s" if m == NS else "p"
                    if group == "s":
                        dve.wait_ge(mod_s_loaded, 2 * SB * 16)
                        nc.vector.scalar_tensor_tensor(gain["s"][:, :], gain["s"][:, :], 1.0, g[0:NS, :],
                                                       ALU.add, ALU.mult).then_inc(gains, 1)
                        dve.wait_ge(gains, 2)
                    dve.wait_ge(sq_done, n + 1)
                    nc.vector.tensor_scalar(ms[0:m, u:u + 1], ss[0:m, u:u + 1], 1.0 / D, RMS_EPS,
                                            ALU.mult, ALU.add).then_inc(ms_done, 1)
                    dve.wait_ge(rt_done, n + 1)
                    nc.vector.reciprocal(rstd[0:m, u:u + 1], rt[0:m, u:u + 1]).then_inc(rstd_done, 1)
                    dve.wait_ge(rstd_done, n + 1)
                    dve.wait_ge(turned, n + 1)
                    nc.vector.scalar_tensor_tensor(h[0:m, u, :], x[0:m, u, :], rstd[0:m, u:u + 1], gain[group][0:m, :],
                                                   ALU.mult, ALU.mult).then_inc(x_free, 1)
                    dve.wait_ge(x_free, n + 3)
                    nc.vector.tensor_tensor(h[0:m, u, :], h[0:m, u, :], shift[group][0:m, :],
                                            ALU.add).then_inc(h_done, 1)

                def keep_v(n, u, r):
                    m = rows_of(n)
                    dve.wait_ge(v_done, n + 3)
                    nc.vector.tensor_copy(v_g[0:m, bass.ds(n, 1), :].squeeze(1), ps_v[0:m, u, 0:GW]).then_inc(v_kept, 1)
                    nc.vector.tensor_copy(v_sb[0:m, bass.ds(n, 1), :].squeeze(1),
                                          ps_v[0:m, u, 512:1024]).then_inc(v_kept, 1)

                ahead(dve, NT + 1, norm, keep_v, lead=2)

            @block.tensor
            def _(pe):
                pe.sem_inc(turned, 2)
                pe.sem_inc(v_done, 2)

                def turn(n, u, r):
                    m = rows_of(n)
                    pe.wait_ge(h_done, n + 1)
                    pe.wait_ge(ht_ready, n + 1)
                    for k in range(KT):
                        last = nc.tensor.transpose(ps_h[:, u, k, 0:m], h[0:m, u, k * P:(k + 1) * P],
                                                   keep["ident"][0:m, 0:m])
                    last.then_inc(turned, 1)

                def project(n, u, r):
                    m = rows_of(n)
                    pe.wait_ge(wv_loaded, 32)
                    pe.wait_ge(ht_ready, n + 3)
                    pe.wait_ge(v_kept, 2 * n + 2)
                    for col, lo, hi in ((0, 0, GW), (512, GW, GW + SBW)):
                        for k in range(KT):
                            last = nc.tensor.matmul(ps_v[0:m, u, col:col + hi - lo], ht[:, u, k, 0:m], wv[:, k, lo:hi],
                                                    start=(k == 0), stop=(k == KT - 1))
                    last.then_inc(v_done, 1)

                ahead(pe, NT + 1, turn, project)


BUILT = 2 * (2 * 4 + 1 + 4 + 1 + 4)
NORM_STEPS = 9
STAGED = 10
LN_STEPS = 20
CLIP = 20.0
STEPS = 21


def rwkv_project(nc, T, keep):
    hT, R = keep["hT"], keep["R"]
    w_view = T["w_in"].rearrange("(k p) n -> p k n", p=P)
    with Phase(nc, "rp") as ph:
        w = ph.sb("w", [P, 2, KT, P])
        p_at = ph.sb("p_at", [P, 2, 1 + TOK])
        diff = ph.sb("diff", [P, 2, TOK])
        mu = ph.sb("mu", [P, RF])
        carried, carried_T = ph.sb("carried", [SB, RPROJ]), ph.sb("carried_T", [P, RF, SB])
        lasts, last_rows = ph.sb("lasts", [P, RF, SB + 1]), ph.sb("last_rows", [SB + 1, RF, P])
        ps = ph.ps("ps", [P, 2, 1536])
        ps_c, ps_l = ph.ps("ps_c", [P, RF, SB]), ps[0:SB + 1, 1, :]
        (small_loaded, zeroed, carried_turned, carried_kept, projected, p_kept, diffed, fixed, mixed, lasts_kept,
         lasts_turned, rows_kept, stored) = (ph.sem(x_) for x_ in (
             "small_loaded", "zeroed", "carried_turned", "carried_kept", "projected", "p_kept", "diffed", "fixed",
             "mixed", "lasts_kept", "lasts_turned", "rows_kept", "stored"))
        w_loaded = [ph.sem(f"w_loaded{u}") for u in range(2)]
        with nc.Block() as block:
            @block.sync
            def _(sp):
                sp.dma_start(carried[:, :], T["state_rwkv_shift"]).then_inc(small_loaded, 16)
                with nc.allow_non_contiguous_dma(reason="one scalar per feature"):
                    sp.dma_start(mu[:, :], T["rwkv_mu"].rearrange("a (f p) -> p (a f)", p=P)).then_inc(small_loaded, 16)

                def load(n, u, r):
                    sp.wait_ge(projected, n + 1)
                    sp.dma_start(w[:, u, :, :], w_view[:, :, bass.ds(n * P, P)]).then_inc(w_loaded[u], 16)

                each(sp, RF, load)
                sp.wait_ge(rows_kept, 1)
                rows = last_rows[:, :, :].rearrange("b f p -> b (f p)")
                sp.dma_start(T["shift_prompt"], rows[0:1, :]).then_inc(stored, 16)
                sp.dma_start(T["shift_sample"], rows[1:SB + 1, :]).then_inc(stored, 16)
                sp.wait_ge(stored, 32)

            @block.tensor
            def _(pe):
                pe.sem_inc(projected, 2)
                pe.wait_ge(small_loaded, 32)
                for f in range(RF):
                    last = nc.tensor.transpose(ps_c[:, f, :], carried[:, f * P:(f + 1) * P], keep["ident"][0:SB, 0:SB])
                last.then_inc(carried_turned, 1)

                def project(n, u, r):
                    pe.wait_ge(w_loaded[u], r * 16 + 16)
                    pe.wait_ge(p_kept, n + 1)
                    for lo, hi in COLS:
                        for k in range(KT):
                            last = nc.tensor.matmul(ps[:, u, lo:hi], w[:, u, k, :], hT[:, k, lo:hi],
                                                    start=(k == 0), stop=(k == KT - 1))
                    last.then_inc(projected, 1)

                each(pe, RF, project)
                pe.wait_ge(lasts_kept, RF + 2)
                for f in range(RF):
                    last = nc.tensor.transpose(ps_l[:, f * P:(f + 1) * P], lasts[:, f, :], keep["ident"][:, :])
                last.then_inc(lasts_turned, 1)

            @block.scalar
            def _(act):
                act.sem_inc(p_kept, 2)
                act.wait_ge(carried_turned, 1)
                nc.scalar.activation(carried_T[:, :, :], ps_c[:, :, :], ACT.Copy).then_inc(carried_kept, 1)
                act.wait_ge(zeroed, 1)

                def evacuate(n, u, r):
                    act.wait_ge(projected, n + 3)
                    act.wait_ge(mixed, n + 1)
                    act.wait_ge(lasts_kept, n + 1)
                    nc.scalar.activation(p_at[:, u, 1:], ps[:, u, 0:TOK], ACT.Copy).then_inc(p_kept, 1)

                each(act, RF, evacuate)
                act.wait_ge(lasts_turned, 1)
                nc.scalar.activation(last_rows[:, :, :].rearrange("b f p -> b (f p)"), ps_l[:, 0:RPROJ],
                                     ACT.Copy).then_inc(rows_kept, 1)

            @block.gpsimd
            def _(pool):
                pool.sem_inc(lasts_kept, 2)

                def keep_last(n, u, r):
                    pool.wait_ge(p_kept, n + 3)
                    nc.gpsimd.tensor_copy(lasts[:, bass.ds(n, 1), :].squeeze(1),
                                          p_at[:, u, SEQ:1 + TOK:ST]).then_inc(lasts_kept, 1)

                each(pool, RF, keep_last)

            @block.vector
            def _(dve):
                dve.sem_inc(mixed, 2)
                nc.vector.memset(p_at[:, :, 0:1], 0.0).then_inc(zeroed, 1)
                dve.wait_ge(carried_kept, 1)

                def mix(n, u, r):
                    dve.wait_ge(p_kept, n + 3)
                    nc.vector.tensor_tensor(diff[:, u, :], p_at[:, u, 0:TOK], p_at[:, u, 1:],
                                            ALU.subtract).then_inc(diffed, 1)
                    dve.wait_ge(diffed, n + 1)
                    nc.vector.tensor_tensor(diff[:, u, SEQ::ST], carried_T[:, bass.ds(n, 1), :].squeeze(1),
                                            p_at[:, u, 1 + SEQ::ST], ALU.subtract).then_inc(fixed, 1)
                    dve.wait_ge(fixed, n + 1)
                    nc.vector.scalar_tensor_tensor(R[:, bass.ds(n, 1), :].squeeze(1), diff[:, u, :],
                                                   mu[:, bass.ds(n, 1)], p_at[:, u, 1:],
                                                   ALU.mult, ALU.add).then_inc(mixed, 1)

                each(dve, RF, mix)


def chunk_masks(nc, pool, keep, built):
    masks, blocks, own, I2, ident = (keep[x_] for x_ in ("masks", "blocks", "own", "I2", "ident"))
    count = [0]

    def step(ins):
        count[0] += 1
        ins.then_inc(built, 1)
        pool.wait_ge(built, count[0])

    def select(ap, op, base, pattern, mult):
        step(nc.gpsimd.affine_select(out=ap, in_=ap, compare_op=op, fill=0.0, base=base, pattern=pattern,
                                     channel_multiplier=mult))

    for h in range(2):
        rows = slice(h * HD, h * HD + HD)
        for m in masks.values():
            step(nc.gpsimd.memset(m[rows, :, :], 1.0))
            select(m[rows, 0, :], ALU.is_gt, 0, [[-1, C]], 1)
            select(m[rows, 1, :], ALU.is_gt, 0, [[1, C]], -1)
            select(m[rows, 2, :], ALU.is_ge, 0, [[1, C]], -1)
        step(nc.gpsimd.memset(own[rows, :], 1.0))
        for ap, pattern in ((masks["s"][rows, :, :], [[0, 3], [-ST, SB], [0, ST]]), (own[rows, :], [[-ST, SB]])):
            select(ap, ALU.is_ge, 0, pattern, 1)
            select(ap, ALU.is_ge, ST - 1, [[-x_, n_] for x_, n_ in pattern], -1)
        step(nc.gpsimd.tensor_copy(I2[rows, :], ident[rows, rows]))
        for x_ in "ps":
            step(nc.gpsimd.memset(blocks[x_][rows, :, :, :], 0.0))
            step(nc.gpsimd.tensor_copy(blocks[x_][rows, :, h, :], masks[x_][rows, 0:2, :]))
    assert count[0] == BUILT


def rwkv_prepare(nc, T, keep, mod_rows):
    c_T = keep["c_T"]
    MR = SB + 1
    w_view = T["w_mod"].rearrange("(k p) n -> p k n", p=P)
    mod_cols = lambda i: slice(MOD_LATE[i] * MOD_COLS, (MOD_LATE[i] + 1) * MOD_COLS)
    R, B, ends, head_ones, gates, bonus = (keep[x_] for x_ in ("R", "B", "ends", "head_ones", "rwkv_g", "bonus"))
    with Phase(nc, "rq") as ph:
        t_w, t_a, t_l, t_k, t_e, t_x, t_y = (ph.sb(x_, [P, TOK])[:, :] for x_ in ("t_w", "t_a", "t_l", "t_k", "t_e", "t_x", "t_y"))
        inside = ph.sb("inside", [P, TOK])
        up = ph.sb("up", [P, RW])
        gd = ph.sb("gd", [P, TOK])
        cols = {x_: ph.sb(x_, [P, 2]) for x_ in ("w0", "a0", "k_k", "k_a", "r_k", "k_0")}
        w_mod, b_mod = ph.sb("w_mod", [P, 2, KT, MOD_COLS]), ph.sb("b_mod", [MR, 2, MOD_COLS])
        mod_sum = ph.sb("mod_sum", [MR, 2, MOD_COLS])
        ps_mod = ph.ps("ps_mod", [P, 2, MOD_COLS])
        masks_built, mod_done, mod_kept, mod_added = (ph.sem(x_) for x_ in ("masks_built", "mod_done", "mod_kept", "mod_added"))
        mod_loaded, mod_stored = ([ph.sem(f"{x_}{u}") for u in range(2)] for x_ in ("mod_loaded", "mod_stored"))
        ps_w, ps_a = ph.ps("ps_w", [P, 1536]), ph.ps("ps_a", [P, 1536])
        (loaded, lora_in, w_up, a_up, g_up, w_sig, a_sig, g_kept, squared, sums, did) = (ph.sem(x_) for x_ in (
            "loaded", "lora_in", "w_up", "a_up", "g_up", "w_sig", "a_sig", "g_kept", "squared", "sums", "did"))
        rooted, exp_l, exp_nl, exp_p, bonus_sum, const = (ph.sem(x_) for x_ in (
            "rooted", "exp_l", "exp_nl", "exp_p", "bonus_sum", "const"))
        with nc.Block() as block:
            @block.sync
            def _(sp):
                with nc.allow_non_contiguous_dma(reason="one scalar per feature"):
                    for x_, name in (("w0", "rwkv_w0"), ("a0", "rwkv_a0"), ("k_k", "rwkv_k_k"), ("k_a", "rwkv_k_a"),
                                     ("r_k", "rwkv_r_k")):
                        sp.dma_start(cols[x_][:, :], T[name].rearrange("a (f p) -> p (a f)", p=P)).then_inc(loaded, 16)
                sp.dma_start(up[0:32, :], T["rwkv_w_up"]).then_inc(loaded, 16)
                sp.dma_start(up[32:64, :], T["rwkv_a_up"]).then_inc(loaded, 16)
                sp.dma_start(up[64:P, :], T["rwkv_g_up"]).then_inc(loaded, 16)

                def store(i):
                    sp.wait_ge(mod_added, i + 1)
                    sp.dma_start(mod_rows[:, mod_cols(i)], mod_sum[:, i % 2, :]).then_inc(mod_stored[i % 2], 16)

                for i in range(len(MOD_LATE)):
                    if i >= 2:
                        sp.wait_ge(mod_done, i - 1)
                        store(i - 2)
                    sp.dma_start(w_mod[:, i % 2, :, :], w_view[:, :, mod_cols(i)]).then_inc(mod_loaded[i % 2], 16)
                    sp.dma_start(b_mod[:, i % 2, :], T["b_mod"][:, mod_cols(i)].to_broadcast([MR, MOD_COLS])
                                 ).then_inc(mod_loaded[i % 2], 16)
                for i in range(len(MOD_LATE) - 2, len(MOD_LATE)):
                    store(i)
                for u in range(2):
                    sp.wait_ge(mod_stored[u], len(MOD_LATE) // 2 * 16)

            @block.gpsimd
            def _(pool):
                chunk_masks(nc, pool, keep, masks_built)
                for i in range(len(MOD_LATE)):
                    pool.wait_ge(mod_kept, i + 1)
                    nc.gpsimd.tensor_tensor(mod_sum[:, i % 2, :], mod_sum[:, i % 2, :], b_mod[:, i % 2, :], ALU.add).then_inc(mod_added, 1)

            @block.tensor
            def _(pe):
                def up_project(ps, rows, f, done):
                    for lo, hi in COLS:
                        last = nc.tensor.matmul(ps[:, lo:hi], up[rows, f * P:(f + 1) * P], gd[rows, lo:hi],
                                                start=True, stop=True)
                    last.then_inc(done, 1)

                def modulate(i):
                    pe.wait_ge(mod_loaded[i % 2], i // 2 * 32 + 32)
                    if i >= 2:
                        pe.wait_ge(mod_kept, i - 1)
                    for k in range(KT):
                        last = nc.tensor.matmul(ps_mod[0:MR, i % 2, :], c_T[:, k, :], w_mod[:, i % 2, k, :],
                                                start=(k == 0), stop=(k == KT - 1))
                    last.then_inc(mod_done, 1)

                def head_sum(ps, of, done):
                    for lo, hi in COLS:
                        last = nc.tensor.matmul(ps[:, lo:hi], head_ones[:, :], of[:, lo:hi], start=True, stop=True)
                    last.then_inc(done, 1)

                pe.wait_ge(loaded, 16 * 8)
                pe.wait_ge(lora_in, 3)
                for f in range(2):
                    if f:
                        pe.wait_ge(did, STEPS)
                        pe.wait_ge(g_kept, 1)
                    up_project(ps_w, slice(0, 32), f, w_up)
                    up_project(ps_a, slice(32, 64), f, a_up)
                    modulate(3 * f)
                    pe.wait_ge(w_sig, f + 1)
                    pe.wait_ge(squared, f + 1)
                    head_sum(ps_w, t_k, sums)
                    pe.wait_ge(did, f * STEPS + 4)
                    pe.wait_ge(rooted, f + 1)
                    up_project(ps_w, slice(64, P), f, g_up)
                    modulate(3 * f + 1)
                    modulate(3 * f + 2)
                    pe.wait_ge(a_sig, f + 1)
                    pe.wait_ge(did, f * STEPS + 12)
                    head_sum(ps_a, t_x, bonus_sum)

            @block.scalar
            def _(act):
                act.wait_ge(loaded, 16 * 8)
                nc.scalar.activation(gd[0:32, :], R[0:32, 6, :], ACT.Tanh).then_inc(lora_in, 1)
                nc.scalar.activation(gd[64:P, :], R[64:P, 6, :], ACT.Sigmoid).then_inc(lora_in, 1)
                nc.scalar.activation(gd[32:64, :], R[32:64, 6, :], ACT.Copy).then_inc(lora_in, 1)

                def keep_modulation(i):
                    act.wait_ge(mod_done, i + 1)
                    if i >= 2:
                        act.wait_ge(mod_stored[i % 2], i // 2 * 16)
                    nc.scalar.activation(mod_sum[:, i % 2, :], ps_mod[0:MR, i % 2, :], ACT.Copy).then_inc(mod_kept, 1)

                for f in range(2):
                    if f:
                        act.wait_ge(did, STEPS)
                    act.wait_ge(w_up, f + 1)
                    nc.scalar.activation(t_w, ps_w[:, 0:TOK], ACT.Sigmoid, bias=cols["w0"][:, f:f + 1]).then_inc(w_sig, 1)
                    act.wait_ge(a_up, f + 1)
                    nc.scalar.activation(t_a, ps_a[:, 0:TOK], ACT.Sigmoid, bias=cols["a0"][:, f:f + 1]).then_inc(a_sig, 1)
                    nc.scalar.activation(t_k, R[:, 2 + f, :], ACT.Square, scale=cols["k_k"][:, f:f + 1]).then_inc(squared, 1)
                    keep_modulation(3 * f)
                    act.wait_ge(did, f * STEPS + 4)
                    nc.scalar.activation(t_k, t_y, ACT.Sqrt).then_inc(rooted, 1)
                    act.wait_ge(did, f * STEPS + 6)
                    nc.scalar.activation(t_e, t_e, ACT.Exp, scale=-DECAY).then_inc(exp_p, 1)
                    nc.scalar.activation(t_w, t_l, ACT.Exp, scale=DECAY).then_inc(exp_nl, 1)
                    act.wait_ge(exp_nl, f + 1)
                    nc.scalar.activation(t_l, t_l, ACT.Exp, scale=-DECAY).then_inc(exp_l, 1)
                    act.wait_ge(g_up, f + 1)
                    nc.scalar.activation(gates[:, f, :], ps_w[:, 0:TOK], ACT.Copy).then_inc(g_kept, 1)
                    keep_modulation(3 * f + 1)
                    keep_modulation(3 * f + 2)

            @block.vector
            def _(dve):
                def of_ends(f):
                    return ((slice(0, SEQ), C, bc(ends[:, f, 0:NC], 2, C)),
                            (slice(SEQ, TOK), ST, bc(ends[:, f, NC:], 2, ST)))

                def step(ins):
                    count[0] += 1
                    ins.then_inc(did, 1)
                    dve.wait_ge(did, count[0])

                count = [0]
                nc.vector.memset(inside[:, :], 1.0).then_inc(const, 1)
                dve.wait_ge(const, 1)
                nc.vector.memset(inside[:, 0:SEQ:C], 0.0).then_inc(const, 1)
                nc.vector.memset(inside[:, SEQ::ST], 0.0).then_inc(const, 1)
                dve.wait_ge(loaded, 16 * 8)
                nc.vector.tensor_scalar(cols["k_0"][:, :], cols["k_a"][:, :], -1.0, 1.0, ALU.mult, ALU.add).then_inc(const, 1)
                dve.wait_ge(const, 4)
                for f in range(2):
                    r, k, v = R[:, f, :], R[:, 2 + f, :], R[:, 4 + f, :]
                    sc = {x_: c[:, f:f + 1] for x_, c in cols.items()}
                    if f:
                        dve.wait_ge(bonus_sum, 1)
                        dve.wait_ge(exp_l, 1)
                    dve.wait_ge(w_sig, f + 1)
                    step(nc.vector.tensor_tensor_scan(t_l, inside[:, :], t_w, 0.0, ALU.mult, ALU.add))
                    step(nc.vector.tensor_scalar(t_x, k, sc["k_k"], None, ALU.mult))
                    step(nc.vector.tensor_tensor(t_e, t_l, t_w, ALU.subtract))
                    dve.wait_ge(sums, f + 1)
                    step(nc.vector.tensor_scalar(t_y, ps_w[:, 0:TOK], 1e-24, None, ALU.max))
                    dve.wait_ge(rooted, f + 1)
                    step(nc.vector.reciprocal(t_y, t_k))
                    step(nc.vector.tensor_tensor(t_x, t_x, t_y, ALU.mult))
                    dve.wait_ge(exp_p, f + 1)
                    nc.vector.scalar_tensor_tensor(B[:, 0, f, :], t_x, -1.0, t_e, ALU.mult, ALU.mult).then_inc(did, 1)
                    dve.wait_ge(a_sig, f + 1)
                    nc.vector.tensor_scalar(t_y, t_a, sc["k_a"], sc["k_0"], ALU.mult, ALU.add).then_inc(did, 1)
                    count[0] += 2
                    dve.wait_ge(did, count[0])
                    step(nc.vector.tensor_tensor(k, k, t_y, ALU.mult))
                    step(nc.vector.tensor_tensor(t_a, t_x, t_a, ALU.mult))
                    dve.wait_ge(exp_nl, f + 1)
                    step(nc.vector.tensor_tensor(B[:, 1, f, :], t_a, t_w, ALU.mult))
                    step(nc.vector.scalar_tensor_tensor(t_x, r, sc["r_k"], k, ALU.mult, ALU.mult))
                    dve.wait_ge(exp_l, f + 1)
                    step(nc.vector.tensor_copy(ends[:, f, 0:NC], t_l[:, C - 1:SEQ:C]))
                    step(nc.vector.tensor_copy(ends[:, f, NC:], t_l[:, SEQ + ST - 1::ST]))
                    step(nc.vector.tensor_tensor(r, r, t_l, ALU.mult))
                    step(nc.vector.tensor_tensor(k, k, t_w, ALU.mult))
                    for at, size, end in of_ends(f):
                        for dst, src in ((B[:, 2, f, at], B[:, 1, f, at]), (B[:, 3, f, at], k[:, at])):
                            step(nc.vector.tensor_tensor(dst.rearrange("p (c t) -> p c t", t=size),
                                                         src.rearrange("p (c t) -> p c t", t=size), end, ALU.mult))
                    dve.wait_ge(bonus_sum, f + 1)
                    step(nc.vector.tensor_tensor(bonus[:, f, :], ps_a[:, 0:TOK], v, ALU.mult))
                assert count[0] == 2 * STEPS


def rwkv_chunks(nc, T, keep):
    gates, bonus = keep["rwkv_g"], keep["bonus"]
    R, B, mT, ends = keep["R"], keep["B"], keep["mT"], keep["ends"]
    ident, head_ones = keep["ident"], keep["head_ones"]
    LEVELS = 5
    TURNS = NT
    HALF = [slice(0, HD), slice(HD, P)]
    L_, N_ = 0, 1
    with Phase(nc, "rc") as ph:
        a_, b_, bt_, kt_, k_, v_ = range(6)
        st = ph.sb("st", [P, 6, 4, P])
        mv = ph.sb("mv", [P, 2, 2, 7, C])
        RING = 3
        pw = ph.sb("pw", [P, RING, 2, 4, P])
        inv = ph.sb("inv", [P, 4, P])
        M = ph.sb("M", [P, 2, 4, C])
        LkT = ph.sb("LkT", [P, 4, P])
        tok = ph.sb("tok", [P, 4, 4, P])
        X, W = ph.sb("X", [P, 4, P]), ph.sb("W", [P, 4, P])
        U, U_s = ph.sb("U", [P, 2, P]), ph.sb("U_s", [P, 2, C])
        S = ph.sb("S", [P, 2, 2, P])
        masks, blocks, own, I2 = keep["masks"], keep["blocks"], keep["own"], keep["I2"]
        Ss = ph.sb("Ss", [P, 2, SB, HD])
        UVm = ph.sb("UVm", [P, 2, SB, C])
        ln_g, ln_b = ph.sb("ln_g", [P, 2]), ph.sb("ln_b", [P, 2])
        sq, root = ph.sb("sq", [P, 2, P]), ph.sb("root", [P, 2, P])
        S_out, S_out_prompt = UVm, U_s
        bank = [ph.ps(f"bank{x_}", [P, 512]) for x_ in range(8)]

        def q4(b, half=0):
            return bank[b][:, half * 256:half * 256 + 256].rearrange("p (q c) -> p q c", c=C)

        def q2(b):
            return bank[b][:, :].rearrange("p (q x c) -> p q x c", x=2, c=C)

        def bd(b, n=4):
            return bank[b][:, 0:n * P].rearrange("p (q c) -> p q c", c=P)

        names = ("staged a_done b_done bk_done v_done k_done l_power n_power inverses x_done w_done u_done s_done y_done "
                 "l_kept n_kept inv_kept tok_kept lk_kept m_kept x_kept w_kept u_kept s_kept y_kept built loaded S_turned "
                 "S_ready parts masked_uv passed out_turned out_kept stored zeroed stage_passed "
                 "ln_loaded means sums squared rooted normed norm_passed")
        g = {x_: ph.sem(x_) for x_ in names.split()}

        def turns(eng, body):
            body(0, 0, 0, False)
            with eng.Fori(0, TURNS // 2 - 1) as i:
                body(i * 2 + 1, 1, i, True)
                body(i * 2 + 2, 0, i + 1, True)
            body(TURNS - 1, 1, TURNS // 2 - 1, True)

        def y_of(n, f=slice(0, 2)):
            return mT[:, f, bass.ds(n * P, rows_of(n))]

        with nc.Block() as block:
            @block.sync
            def _(sp):
                with nc.allow_non_contiguous_dma(reason="one scalar per feature"):
                    sp.dma_start(ln_g[:, :], T["rwkv_ln_g"].rearrange("a (f p) -> p (a f)", p=P)).then_inc(g["ln_loaded"], 16)
                    sp.dma_start(ln_b[:, :], T["rwkv_ln_b"].rearrange("a (f p) -> p (a f)", p=P)).then_inc(g["ln_loaded"], 16)
                for h in range(2):
                    for f in range(2):
                        sp.dma_start(Ss[HALF[h], f, :, :],
                                     T["state_rwkv"][:, 2 * f + h, :, :].rearrange("b i j -> i b j")).then_inc(g["loaded"], 16)
                sp.wait_ge(g["out_kept"], 2)
                for h in range(2):
                    for f in range(2):
                        sp.dma_start(T["S_prompt"][2 * f + h, :, :], S_out_prompt[HALF[h], f, :]).then_inc(g["stored"], 16)
                        sp.dma_start(T["S_sample"][:, 2 * f + h, :, :].rearrange("b i j -> i b j"),
                                     S_out[HALF[h], f, :, :]).then_inc(g["stored"], 16)
                sp.wait_ge(g["stored"], 8 * 16)

            @block.gpsimd
            def _(pool):
                for u in range(2):
                    for ch in range(2):
                        nc.gpsimd.tensor_copy(mv[:, u, ch, 6, :], I2[:, :]).then_inc(g["built"], 1)
                nc.gpsimd.memset(st[:, :, :, :], 0.0).then_inc(g["built"], 1)
                pool.wait_ge(g["built"], 5)

                def stage(n, u, r):
                    chunks = rows_of(n) // C
                    wait_apart(pool, g["staged"], STAGED * n + STAGED, g["stage_passed"])
                    wait_apart(pool, g["y_done"], 2 * n + 2, g["stage_passed"])
                    for dst, src in ((mv[:, u, 0:chunks, 0:2, :], R[:, 0:2, bass.ds(n * P, rows_of(n))]),
                                     (mv[:, u, 0:chunks, 2:6, :], B[:, 0:2, :, :].rearrange("p m f t -> p (m f) t")[
                                         :, :, bass.ds(n * P, rows_of(n))])):
                        nc.gpsimd.tensor_copy(dst, src.rearrange("p x (c t) -> p c x t", t=C)).then_inc(g["staged"], 1)
                    wait_apart(pool, g["k_done"], n + 1, g["stage_passed"])
                    for h in range(2):
                        rows = HALF[h]
                        for ch in range(2):
                            if ch >= chunks:
                                pool.sem_inc(g["staged"], 2)
                                continue
                            at = bass.ds(n * P + ch * C, C)
                            nc.gpsimd.tensor_copy(st[rows, 0:4, 2 * ch:2 * ch + 2, rows], B[rows, :, :, at]).then_inc(g["staged"], 1)
                            nc.gpsimd.tensor_copy(st[rows, 4:6, 2 * ch:2 * ch + 2, rows],
                                                  R[rows, 2:6, at].rearrange("p (x f) t -> p x f t", f=2)).then_inc(g["staged"], 1)
                        if h == 0:
                            wait_apart(pool, g["staged"], STAGED * n + STAGED + 6, g["stage_passed"])

                pool.sem_inc(g["staged"], STAGED)
                pool.sem_inc(g["k_done"], 1)
                pool.sem_inc(g["y_done"], 4)
                each(pool, NT + 1, stage)

            @block.tensor
            def _(pe):
                def ready(sem, value):
                    wait_apart(pe, sem, value, g["passed"])

                def mm(out, lhsT, rhs, start=True, stop=True):
                    return nc.tensor.matmul(out, lhsT, rhs, start=start, stop=stop, skip_group_check=True)

                def head_sums(n, half, of, done):
                    m = rows_of(n)
                    for f in range(2):
                        at = half * 256 + f * P
                        last = mm(bank[7][:, at:at + m], head_ones[:, :], of(f))
                    last.then_inc(done, 1)

                def mean_of(n):
                    ready(g["y_kept"], n + 2)
                    head_sums(n, 0, lambda f: y_of(n, f), g["means"])

                def square_sum_of(n):
                    ready(g["squared"], n + 1)
                    head_sums(n, 1, lambda f: sq[:, f, 0:rows_of(n)], g["sums"])

                def before_state(n, u, chunks, before):
                    Q = [(2 * ch + f, ch, f) for ch in range(chunks) for f in range(2)]
                    b_and_I = lambda ch, f: mv[:, u, ch, 4 + f:7:2 - f, :]
                    r_and_a = lambda ch, f: mv[:, u, ch, f:f + 3:2, :]
                    I = lambda ch: mv[:, u, ch, 6, :]
                    ready(g["staged"], STAGED * n + 2 * STAGED)
                    for q, ch, f in Q:
                        last = mm(q2(0)[:, q, :, :], st[:, a_, q, :], b_and_I(ch, f))
                    last.then_inc(g["a_done"], 1)
                    for q, ch, f in Q:
                        last = mm(q2(1)[:, q, :, :], st[:, b_, q, :], r_and_a(ch, f))
                    last.then_inc(g["b_done"], 1)
                    if before:
                        mean_of(n - 1)
                    for q, ch, f in Q:
                        mm(q2(3)[:, q, 0, :], st[:, bt_, q, :], I(ch))
                        last = mm(q2(3)[:, q, 1, :], st[:, kt_, q, :], I(ch))
                    last.then_inc(g["bk_done"], 1)
                    ready(g["y_kept"], n + 1)
                    for q, ch, f in Q:
                        last = mm(q4(4)[:, q, :], st[:, v_, q, :], I(ch))
                    last.then_inc(g["v_done"], 1)
                    ready(g["s_kept"], 2 * n + 1)
                    for q, ch, f in Q:
                        last = mm(q2(2)[:, q, :, :], st[:, k_, q, :], r_and_a(ch, f))
                    last.then_inc(g["k_done"], 1)
                    if before:
                        square_sum_of(n - 1)

                    def square(k):
                        L, N = pw[:, (k - 1) % RING, L_, :, :], pw[:, (k - 1) % RING, N_, :, :]
                        ready(g["l_kept"], (LEVELS + 1) * n + k)
                        ready(g["n_kept"], LEVELS * n + k)
                        for q, _, _ in Q:
                            last = mm(bd(5)[:, q, :], N[:, q, :], L[:, q, :])
                        last.then_inc(g["l_power"], 1)
                        if k < LEVELS:
                            for q, _, _ in Q:
                                last = mm(bd(6)[:, q, :], L[:, q, :], N[:, q, :])
                            last.then_inc(g["n_power"], 1)

                    def times(k):
                        ready(g["l_kept"], (LEVELS + 1) * n + k + 1)
                        ready(g["inv_kept"], (LEVELS + 1) * n + k)
                        if k == 1 and before:
                            ready(g["normed"], NORM_STEPS * (n - 1) + 2)
                        for q, _, _ in Q:
                            last = mm(bd(7)[:, q, :], pw[:, k % RING, L_, q, :], inv[:, q, :])
                        last.then_inc(g["inverses"], 1)

                    square(1)
                    for k in range(1, LEVELS):
                        square(k + 1)
                        times(k)
                    ready(g["tok_kept"], n + 1)
                    ready(g["lk_kept"], n + 1)
                    ready(g["m_kept"], n + 1)
                    for q, _, _ in Q:
                        last = mm(bd(1)[:, q, :], LkT[:, q, :], tok[:, 3, q, :])
                    last.then_inc(g["x_done"], 1)
                    times(LEVELS)
                    ready(g["inv_kept"], (LEVELS + 1) * n + LEVELS + 1)
                    for q, _, _ in Q:
                        last = mm(bd(0)[:, q, :], tok[:, 0, q, :], inv[:, q, :])
                    last.then_inc(g["w_done"], 1)
                    ready(g["x_kept"], n + 1)

                def turn_of_prompt(n, u, r, before):
                    before_state(n, u, 2, before)
                    for ch in range(2):
                        for f in range(2):
                            mm(bd(3)[:, f, :], inv[:, 2 * ch + f, :], X[:, 2 * ch + f, :], start=(f == 0), stop=False)
                        if ch == 0:
                            ready(g["w_kept"], n + 1)
                        ready(g["s_kept"], 2 * n + ch + 1)
                        for f in range(2):
                            last = mm(bd(3)[:, f, :], W[:, 2 * ch + f, :], S[:, ch, f, :], start=False)
                        last.then_inc(g["u_done"], 1)
                        for f in range(2):
                            q = 2 * ch + f
                            y, s_new = q4(4, 1)[:, q, :], bd(2)[:, f, :]
                            mm(y, S[:, ch, f, :], mv[:, u, ch, f, :], start=(f == 0), stop=False)
                            mm(y, tok[:, 3, q, :], M[:, 1, q, :], start=False, stop=False)
                            mm(s_new, tok[:, 2, q, :], tok[:, 3, q, :], start=(f == 0), stop=False)
                        ready(g["u_kept"], 2 * n + ch + 1)
                        for f in range(2):
                            q = 2 * ch + f
                            mm(bd(2)[:, f, :], tok[:, 1, q, :], U[:, f, :], start=False)
                            last = mm(q4(4, 1)[:, q, :], U[:, f, :], M[:, 0, q, :], start=False)
                        last.then_inc(g["y_done"], 1)

                pe.wait_ge(g["built"], 5)
                pe.wait_ge(g["loaded"], 64)
                for f in range(2):
                    for b in range(SB):
                        for rows in HALF:
                            last = mm(bank[f][rows, b * HD:(b + 1) * HD], Ss[rows, f, b, :], I2[rows, :])
                last.then_inc(g["S_turned"], 1)
                pe.wait_ge(g["S_ready"], 2)
                turns(pe, turn_of_prompt)

                u = TURNS % 2
                before_state(TURNS, u, 1, True)
                ready(g["w_kept"], TURNS + 1)
                for f in range(2):
                    mm(bank[3 + f][:, :], W[:, f, :], Ss[:, f, :, :].rearrange("p b i -> p (b i)"))
                    for rows in HALF:
                        last = mm(q4(7)[rows, f, :], inv[rows, f, rows], X[rows, f, rows])
                last.then_inc(g["u_done"], 1)
                pe.wait_ge(g["u_kept"], 2 * TURNS + 1)
                for f in range(2):
                    for rows in HALF:
                        y = q4(6)[rows, f, :]
                        mm(y, U_s[rows, f, :], M[rows, 0, f, :], stop=False)
                        mm(y, tok[rows, 3, f, rows], M[rows, 1, f, :], start=False, stop=False)
                        for b in range(SB):
                            at = slice(b * ST, b * ST + ST)
                            last = mm(y[:, at], Ss[rows, f, b, :], mv[rows, u, 0, f, at], start=False)
                last.then_inc(g["y_done"], 2)
                for f in range(2):
                    pe.wait_ge(g["masked_uv"], 3 * f + 3)
                    mm(bank[f][:, :], tok[:, 1, f, :], UVm[:, 0, :, :].rearrange("p b i -> p (b i)"), stop=False)
                    last = mm(bank[f][:, :], tok[:, 2, f, :], UVm[:, 1, :, :].rearrange("p b i -> p (b i)"), start=False)
                    last.then_inc(g["s_done"], 1)
                pe.wait_ge(g["s_kept"], 2 * TURNS + 1 + 2)
                for f in range(2):
                    for rows in HALF:
                        mm(q4(2)[rows, f, :], S[rows, 0, f, rows], I2[rows, :])
                        for b in range(SB):
                            last = mm(bank[3 + f][rows, b * HD:(b + 1) * HD], Ss[rows, f, b, :], I2[rows, :])
                last.then_inc(g["out_turned"], 1)
                mean_of(TURNS)
                square_sum_of(TURNS)

            @block.scalar
            def _(act):
                act.sem_inc(g["y_kept"], 1)
                nc.scalar.preload_act_table(ACT.Sqrt)
                act.wait_ge(g["zeroed"], 1)
                act.wait_ge(g["S_turned"], 1)
                for f in range(2):
                    nc.scalar.activation(Ss[:, f, :, :].rearrange("p b i -> p (b i)"), bank[f][:, :], ACT.Copy).then_inc(g["S_ready"], 1)

                def copy(out, in_):
                    return nc.scalar.activation(out, in_, ACT.Copy)

                def keep_power(n, k, Q):
                    act.wait_ge(g["n_power"], (LEVELS - 1) * n + k)
                    copy(pw[:, k % RING, N_, 0:Q, :], bd(6)[:, 0:Q, :]).then_inc(g["n_kept"], 1)

                def square_of(n):
                    wait_apart(act, g["normed"], NORM_STEPS * n + 1, g["norm_passed"])
                    nc.scalar.activation(sq[:, :, 0:rows_of(n)], y_of(n), ACT.Square).then_inc(g["squared"], 1)

                def root_of(n):
                    m = rows_of(n)
                    act.wait_ge(g["normed"], NORM_STEPS * n + 2)
                    nc.scalar.activation(root[:, :, 0:m], root[:, :, 0:m], ACT.Sqrt).then_inc(g["rooted"], 1)

                def keep_turn(n, u, Q, before):
                    act.wait_ge(g["a_done"], n + 1)
                    act.wait_ge(g["l_kept"], (LEVELS + 1) * n + 1)
                    for rows in HALF:
                        copy(tok[rows, 0, 0:Q, rows], q2(0)[rows, 0:Q, 1, :])
                    act.wait_ge(g["bk_done"], n + 1)
                    for rows in HALF:
                        copy(tok[rows, 1:3, 0:Q, rows].rearrange("p x q c -> p q x c"), q2(3)[rows, 0:Q, :, :])
                    if before:
                        square_of(n - 1)
                    keep_power(n, 1, Q)
                    act.wait_ge(g["v_done"], n + 1)
                    for rows in HALF:
                        last = copy(tok[rows, 3, 0:Q, rows], q4(4)[rows, 0:Q, :])
                    last.then_inc(g["tok_kept"], 1)
                    for k in range(2, LEVELS):
                        keep_power(n, k, Q)
                        if k == 2 and before:
                            root_of(n - 1)
                    act.wait_ge(g["x_done"], n + 1)
                    copy(X[:, 0:Q, :], bd(1)[:, 0:Q, :]).then_inc(g["x_kept"], 1)
                    act.wait_ge(g["w_done"], n + 1)
                    copy(W[:, 0:Q, :], bd(0)[:, 0:Q, :]).then_inc(g["w_kept"], 1)
                    act.wait_ge(g["y_done"], 2 * n + 2 + 4)

                def prompt(n, u, r, before):
                    keep_turn(n, u, 4, before)
                    nc.scalar.activation(mT[:, 0:2, bass.ds(n * P, P)].rearrange("p f (c t) -> p c f t", c=2),
                                         q4(4, 1).rearrange("p (c f) t -> p c f t", c=2), ACT.Copy).then_inc(g["y_kept"], 1)

                turns(act, prompt)
                keep_turn(TURNS, 0, 2, True)
                nc.scalar.activation(mT[:, 0:2, SEQ:TOK], q4(6)[:, 0:2, :], ACT.Copy).then_inc(g["y_kept"], 1)
                act.wait_ge(g["out_turned"], 1)
                for f in range(2):
                    nc.scalar.activation(S_out_prompt[:, f, :], q4(2)[:, f, :], ACT.Copy)
                    last = nc.scalar.activation(S_out[:, f, :, :], bank[3 + f][:, :].rearrange("p (b i) -> p b i", b=SB),
                                                ACT.Copy)
                    last.then_inc(g["out_kept"], 1)
                square_of(TURNS)
                root_of(TURNS)

            @block.vector
            def _(dve):
                def norm_steps(n):
                    m, y = rows_of(n), y_of(n)
                    half = lambda x_: bank[7][:, x_ * 256:x_ * 256 + 256].rearrange("p (f t) -> p f t", f=2)[:, :, 0:m]
                    r = root[:, :, 0:m]

                    def step(i, ins):
                        ins.then_inc(g["normed"], 1)
                        dve.wait_ge(g["normed"], NORM_STEPS * n + i)

                    def center():
                        dve.wait_ge(g["means"], n + 1)
                        step(1, nc.vector.scalar_tensor_tensor(y, half(0), -1.0 / HD, y, ALU.mult, ALU.add))

                    def mean_square():
                        dve.wait_ge(g["sums"], n + 1)
                        step(2, nc.vector.tensor_scalar(r, half(1), 1.0 / HD, GN_EPS, ALU.mult, ALU.add))

                    def invert(f):
                        dve.wait_ge(g["rooted"], n + 1)
                        step(3 + f, nc.vector.reciprocal(root[:, f, 0:m], root[:, f, 0:m]))

                    def affine():
                        step(5, nc.vector.tensor_tensor(y, y, r, ALU.mult))
                        for f in range(2):
                            step(6 + f, nc.vector.tensor_scalar(y_of(n, f), y_of(n, f), ln_g[:, f:f + 1], ln_b[:, f:f + 1],
                                                                ALU.mult, ALU.add))

                    def gate():
                        at = bass.ds(n * P, m)
                        step(8, nc.vector.tensor_tensor(y, y, bonus[:, :, at], ALU.add))
                        step(9, nc.vector.tensor_tensor(y, y, gates[:, :, at], ALU.mult))

                    return center, mean_square, lambda: invert(0), lambda: invert(1), affine, gate

                def keep_turn(n, u, Q, mask, block_mask, before):
                    norm = iter(norm_steps(n - 1) if before else [lambda: None] * 6)
                    def blocks_of(ps, x_):
                        return bc(ps, 2, 2), bc(block_mask[:, x_, :, :], 1, Q)

                    def by_block(ap):
                        return ap.rearrange("p q (h c) -> p q h c", h=2)

                    dve.wait_ge(g["a_done"], n + 1)
                    nc.vector.tensor_tensor(by_block(pw[:, 0, L_, 0:Q, :]), *blocks_of(q2(0)[:, 0:Q, 0, :], 0), ALU.mult).then_inc(g["l_kept"], 1)
                    dve.wait_ge(g["b_done"], n + 1)
                    nc.vector.tensor_tensor(by_block(pw[:, 0, N_, 0:Q, :]), *blocks_of(q2(1)[:, 0:Q, 1, :], 1), ALU.mult).then_inc(g["n_kept"], 1)
                    nc.vector.tensor_tensor(M[:, 0, 0:Q, :], q2(1)[:, 0:Q, 0, :], bc(mask[:, 2, :], 1, Q), ALU.mult).then_inc(g["m_kept"], 1)
                    dve.wait_ge(g["n_kept"], LEVELS * n + 1)
                    nc.vector.tensor_tensor(inv[:, 0:Q, :], pw[:, 0, N_, 0:Q, :], bc(ident[:, :], 1, Q), ALU.add).then_inc(g["inv_kept"], 1)

                    def keep_power(k):
                        dve.wait_ge(g["l_power"], LEVELS * n + k)
                        nc.vector.tensor_copy(pw[:, k % RING, L_, 0:Q, :], bd(5)[:, 0:Q, :]).then_inc(g["l_kept"], 1)

                    def keep_inverse(k):
                        dve.wait_ge(g["inverses"], LEVELS * n + k)
                        nc.vector.tensor_tensor(inv[:, 0:Q, :], inv[:, 0:Q, :], bd(7)[:, 0:Q, :], ALU.add).then_inc(g["inv_kept"], 1)

                    next(norm)()
                    keep_power(1)
                    dve.wait_ge(g["k_done"], n + 2)
                    nc.vector.tensor_tensor(by_block(LkT[:, 0:Q, :]), *blocks_of(q2(2)[:, 0:Q, 1, :], 1), ALU.mult).then_inc(g["lk_kept"], 1)
                    nc.vector.tensor_tensor(M[:, 1, 0:Q, :], q2(2)[:, 0:Q, 0, :], bc(mask[:, 2, :], 1, Q), ALU.mult).then_inc(g["m_kept"], 1)
                    next(norm)()
                    for k in range(1, LEVELS):
                        keep_power(k + 1)
                        keep_inverse(k)
                        next(norm)()
                    keep_inverse(LEVELS)

                def prompt(n, u, r, before):
                    keep_turn(n, u, 4, masks["p"], blocks["p"], before)
                    for c in range(2):
                        dve.wait_ge(g["u_done"], 2 * n + c + 1)
                        nc.vector.tensor_copy(U[:, :, :], bd(3, 2)).then_inc(g["u_kept"], 1)
                        dve.wait_ge(g["y_done"], 2 * n + c + 1 + 4)
                        for f in range(2):
                            last = nc.vector.scalar_tensor_tensor(S[:, 1 - c, f, :], S[:, c, f, :],
                                                                  ends[:, f, bass.ds(n * 2 + c, 1)], bd(2)[:, f, :],
                                                                  ALU.mult, ALU.add)
                        last.then_inc(g["s_kept"], 1)

                nc.vector.memset(tok[:, :, :, :], 0.0).then_inc(g["zeroed"], 1)
                nc.vector.memset(S[:, 0, :, :], 0.0).then_inc(g["s_kept"], 1)
                dve.wait_ge(g["ln_loaded"], 32)
                turns(dve, prompt)
                keep_turn(TURNS, 0, 2, masks["s"], blocks["s"], True)
                dve.wait_ge(g["u_done"], 2 * TURNS + 1)
                for f in range(2):
                    nc.vector.tensor_tensor(UVm[:, f, :, :], bank[3 + f][:, :].rearrange("p (b i) -> p b i", b=SB),
                                            bc(own[:, :], 2, C), ALU.mult).then_inc(g["parts"], 1)
                dve.wait_ge(g["parts"], 2)
                for f in range(2):
                    nc.vector.tensor_reduce(U_s[:, f, :], UVm[:, f, :, :].rearrange("p b i -> p i b"), axis=AXX, op=ALU.add).then_inc(g["parts"], 1)
                dve.wait_ge(g["parts"], 4)
                nc.vector.tensor_tensor(U_s[:, :, :], U_s[:, :, :], q4(7)[:, 0:2, :], ALU.add).then_inc(g["u_kept"], 1)
                dve.wait_ge(g["u_kept"], 2 * TURNS + 1)
                for f in range(2):
                    if f:
                        dve.wait_ge(g["s_done"], 1)
                    for rows, x_, src in ((slice(0, P), 0, U_s[:, f, :]), *((rows, 1, tok[rows, 3, f, rows]) for rows in HALF)):
                        nc.vector.tensor_tensor(UVm[rows, x_, :, :], bc(src, 1, SB), bc(own[rows, :], 2, C), ALU.mult).then_inc(g["masked_uv"], 1)
                dve.wait_ge(g["y_done"], 2 * TURNS + 2 + 4)
                dve.wait_ge(g["s_done"], 2)
                for f in range(2):
                    nc.vector.tensor_tensor(Ss[:, f, :, :], Ss[:, f, :, :], bc(ends[:, f, NC:], 2, HD), ALU.mult).then_inc(g["parts"], 1)
                dve.wait_ge(g["parts"], 6)
                for f in range(2):
                    nc.vector.tensor_tensor(Ss[:, f, :, :], Ss[:, f, :, :], bank[f][:, :].rearrange("p (b i) -> p b i", b=SB),
                                            ALU.add).then_inc(g["s_kept"], 1)
                for step_of_norm in norm_steps(TURNS):
                    step_of_norm()


def gated_mlp(nc, T, keep):
    hT, mT, v_g, ident = keep["hT"], keep["mT"], keep["v_g"], keep["ident"]
    G = GG * NT
    parts = [(slice(0, P), slice(0, NT), G, 0), (slice(0, NS), slice(NT, NT + 1), GG, 1)]
    with Phase(nc, "gm") as ph:
        w_u = lambda k, f: keep["R"][:, k // (KT // 2), k % (KT // 2) * GW + f * P:k % (KT // 2) * GW + (f + 1) * P]
        ws, wsT = ph.sb("ws", [P, GG, P]), ph.sb("wsT", [P, GG, P])
        ws_s, ws_sT = ph.sb("ws_s", [NS, GG, NS]), ph.sb("ws_sT", [NS, GG, NS])
        bs, bs_s = ph.sb("bs", [P, 2, P]), ph.sb("bs_s", [P, 2, ST])
        g, b = ph.sb("g", [P, GW]), ph.sb("b", [P, GW])
        sq = ph.sb("sq", [P, NT + 1, GW])
        st = [ph.sb(f"st{x_}", [P, 2, G]) for x_ in range(3)]
        mixed = ph.sb("mixed", [P, 2, TOK])
        ps_u, ps_m, ps_s = ph.ps("ps_u", [P, 1536]), ph.ps("ps_m", [P, 2, SEQ]), ph.ps("ps_s", [P, 512])
        ps_u1 = ps_m[:, :, :].rearrange("p f t -> p (f t)")
        (loaded, zeroed, masked, u_done, u_kept, gelus, rooted, turned, turned_kept, did, mixes,
         stored) = (ph.sem(x_) for x_ in (
             "loaded", "zeroed", "masked", "u_done", "u_kept", "gelus", "rooted", "turned",
             "turned_kept", "did", "mixes", "stored"))

        def groups(t, part):
            rows, tiles, n, _ = part
            return t[rows, tiles, :].rearrange("p t (g c) -> p (t g) c", c=HD)

        with nc.Block() as block:
            @block.sync
            def _(sp):
                sp.dma_start(ws[:, :, :], T["gmlp_ws"].rearrange("g t s -> t g s")).then_inc(loaded, 16)
                sp.dma_start(g[:, :], T["gmlp_ln_g"].to_broadcast([P, GW])).then_inc(loaded, 16)
                sp.dma_start(b[:, :], T["gmlp_ln_b"].to_broadcast([P, GW])).then_inc(loaded, 16)
                for x_ in range(GG):
                    rows = slice(x_ % 2 * HD, x_ % 2 * HD + HD)
                    sp.dma_start(bs[rows, x_ // 2, :], T["gmlp_bs"][x_:x_ + 1, :].to_broadcast([HD, P])).then_inc(loaded, 16)
                    sp.dma_start(bs_s[rows, x_ // 2, :], T["gmlp_bs"][x_:x_ + 1, 0:ST].to_broadcast([HD, ST])).then_inc(loaded, 16)
                sp.wait_ge(zeroed, 1)
                for x_ in range(SB):
                    at = slice(x_ * ST, x_ * ST + ST)
                    sp.dma_start(ws_s[at, :, at], T["gmlp_ws"][:, 0:ST, 0:ST].rearrange("g t s -> t g s")).then_inc(loaded, 16)
                sp.wait_ge(did, LN_STEPS)
                sp.dma_start(T["g_v_sample"], v_g[0:NS, NT, :]).then_inc(stored, 16)
                sp.wait_ge(stored, 16)

            @block.gpsimd
            def _(pool):
                nc.gpsimd.memset(ws_s[:, :, :], 0.0).then_inc(zeroed, 1)
                pool.wait_ge(loaded, 16 * (3 + 2 * GG + SB))
                nc.gpsimd.affine_select(out=ws[:, :, :], in_=ws[:, :, :], compare_op=ALU.is_ge, fill=0.0, base=0,
                                        pattern=[[0, GG], [-1, P]], channel_multiplier=1).then_inc(masked, 1)
                nc.gpsimd.affine_select(out=ws_s[:, :, :], in_=ws_s[:, :, :], compare_op=ALU.is_ge, fill=0.0, base=0,
                                        pattern=[[0, GG], [-1, NS]], channel_multiplier=1).then_inc(masked, 1)

            @block.tensor
            def _(pe):
                pe.wait_ge(keep["w_u_loaded"], 32)
                for f, ps in enumerate((ps_u, ps_u1)):
                    for lo, hi in COLS:
                        for k in range(KT):
                            last = nc.tensor.matmul(ps[:, lo:hi], w_u(k, f), hT[:, k, lo:hi],
                                                    start=(k == 0), stop=(k == KT - 1))
                    last.then_inc(u_done, 1)
                pe.wait_ge(masked, 2)
                pe.wait_ge(u_kept, 1)
                for x_ in range(GG):
                    nc.tensor.transpose(ps_s[:, x_ * P:(x_ + 1) * P], ws[:, x_, :], ident[:, :])
                    last = nc.tensor.transpose(ps_u[0:NS, x_ * NS:(x_ + 1) * NS], ws_s[:, x_, :], ident[0:NS, 0:NS])
                last.then_inc(turned, 1)
                pe.wait_ge(turned_kept, 2)
                pe.wait_ge(u_kept, 2)
                pe.wait_ge(did, LN_STEPS)
                at = lambda x_: (slice(x_ % 2 * HD, x_ % 2 * HD + HD), slice(x_ * HD, x_ * HD + HD))
                for x_ in range(GG):
                    rows, cols = at(x_)
                    nc.tensor.matmul(ps_s[rows, x_ // 2 * NS:(x_ // 2 + 1) * NS], v_g[0:NS, NT, cols], ws_sT[:, x_, :],
                                     start=True, stop=True)
                for x_ in range(GG):
                    rows, cols = at(x_)
                    for n in range(NT):
                        last = nc.tensor.matmul(ps_m[rows, x_ // 2, n * P:(n + 1) * P], v_g[:, n, cols], wsT[:, x_, :],
                                                start=True, stop=True)
                    if x_ % 2:
                        last.then_inc(mixes, 1)

            @block.scalar
            def _(act):
                for rows, tiles, _, _ in parts:
                    nc.scalar.activation(v_g[rows, tiles, :], v_g[rows, tiles, :], ACT.Gelu_apprx_tanh).then_inc(gelus, 1)
                for i, (rows, _, n, _) in enumerate(parts):
                    act.wait_ge(did, LN_STEPS // 2 * i + 6)
                    nc.scalar.activation(st[2][rows, i, 0:n], st[1][rows, i, 0:n], ACT.Sqrt).then_inc(rooted, 1)
                for f, ps in enumerate((ps_u, ps_u1)):
                    act.wait_ge(u_done, f + 1)
                    nc.scalar.activation(mT[:, 2 + f, :], ps[:, 0:TOK], ACT.Gelu_apprx_tanh).then_inc(u_kept, 1)
                act.wait_ge(turned, 1)
                nc.scalar.activation(wsT[:, :, :].rearrange("p g t -> p (g t)"), ps_s[:, :], ACT.Copy).then_inc(turned_kept, 1)
                nc.scalar.activation(ws_sT[:, :, :].rearrange("p g t -> p (g t)"), ps_u[0:NS, 0:GG * NS],
                                     ACT.Copy).then_inc(turned_kept, 1)

            @block.vector
            def _(dve):
                count = [0]

                def step(ins):
                    count[0] += 1
                    ins.then_inc(did, 1)
                    dve.wait_ge(did, count[0])

                for i, part in enumerate(parts):
                    rows, tiles, n, _ = part
                    v, s = groups(v_g, part), groups(sq, part)
                    mean, ms, rt = (x_[rows, i, 0:n] for x_ in st)
                    m_tiles = NT if i == 0 else 1
                    dve.wait_ge(gelus, i + 1)
                    step(nc.vector.tensor_reduce(mean, v, axis=AXX, op=ALU.add))
                    step(nc.vector.tensor_scalar(mean, mean, 1.0 / HD, None, ALU.mult))
                    step(nc.vector.tensor_tensor(v, v, bc(mean, 2, HD), ALU.subtract))
                    step(nc.vector.tensor_tensor(s, v, v, ALU.mult))
                    step(nc.vector.tensor_reduce(ms, s, axis=AXX, op=ALU.add))
                    step(nc.vector.tensor_scalar(ms, ms, 1.0 / HD, LN_EPS, ALU.mult, ALU.add))
                    dve.wait_ge(rooted, i + 1)
                    step(nc.vector.reciprocal(rt, rt))
                    step(nc.vector.tensor_tensor(v, v, bc(rt, 2, HD), ALU.mult))
                    t = v_g[rows, tiles, :]
                    dve.wait_ge(loaded, 16 * (3 + 2 * GG + SB))
                    step(nc.vector.tensor_tensor(t, t, bc(g[rows, :], 1, m_tiles), ALU.mult))
                    step(nc.vector.tensor_tensor(t, t, bc(b[rows, :], 1, m_tiles), ALU.add))
                assert count[0] == LN_STEPS
                dve.wait_ge(u_kept, 2)
                for f in range(2):
                    dve.wait_ge(mixes, f + 1)
                    step(nc.vector.tensor_tensor(mixed[:, f, 0:SEQ].rearrange("p (n t) -> p n t", n=NT),
                                                 ps_m[:, f, :].rearrange("p (n t) -> p n t", n=NT), bc(bs[:, f, :], 1, NT), ALU.add))
                    step(nc.vector.tensor_tensor(mixed[:, f, SEQ:].rearrange("p (n t) -> p n t", n=SB),
                                                 ps_s[:, f * NS:(f + 1) * NS].rearrange("p (n t) -> p n t", n=SB),
                                                 bc(bs_s[:, f, :], 1, SB), ALU.add))
                    step(nc.vector.tensor_tensor(mT[:, 2 + f, :], mT[:, 2 + f, :], mixed[:, f, :], ALU.mult))


def attention(nc, T, keep):
    hT, mT, v_sb, v_new, qs, ks = (keep[x_] for x_ in ("hT", "mT", "v_sb", "v_new", "qs", "ks"))
    ident, neg_from, neg_ones = keep["ident"], keep["neg_from"], keep["neg_ones"]
    w_view = T["w_in"].rearrange("(k p) n -> p k n", p=P)
    WT, TT = 512, 512 // P
    blocks = []
    for half in range(2):
        for run in range(SEQ // WT):
            tiles = list(range(TT * run + TT - 1, -1, -1))
            for s in tiles:
                blocks.append((half, run, s, max(0, s - TT * run) * P, s == tiles[0], s == tiles[-1]))
    NB, NR = len(blocks), 4
    BANKS, BUF = 4, 3
    with Phase(nc, "at") as ph:
        w = ph.sb("w", [P, 2, KT, P])
        qk = ph.sb("qk", [P, 2, SEQ])
        k_tok = ph.sb("k_tok", [P, NT + 1, P])
        v_pair = ph.sb("v_pair", [P, NT, P])
        k_s = ph.sb("k_s", [P, NS])
        bias = ph.sb("bias", [P, SH])
        zc, sp_ = ph.sb("zc", [P, BUF, WT]), ph.sb("sp", [P, BUF, WT])
        acc, A = ph.sb("acc", [P, 2, WT]), ph.sb("A", [P, BUF, WT])
        ps_p, ps_z = ph.ps("ps_p", [P, 1536]), ph.ps("ps_z", [P, BANKS, 512])
        names = ("bias_loaded w_loaded proj_done qk_kept ks_kept k_turned k_tok_kept k_stored z_done z_clipped exp_done "
                 "ln_done sp_done sp_masked acc_zero acc_done cum_done a_done a_masked av_done run_kept v_staged passed")
        g = {x_: ph.sem(x_) for x_ in names.split()}

        def cols(b):
            return slice(blocks[b][3], WT)

        def diagonal(b):
            half, run, s, lo, _, _ = blocks[b]
            return s >= TT * run

        n_diag = sum(diagonal(b) for b in range(NB))
        diag_before = [sum(diagonal(x_) for x_ in range(b)) for b in range(NB + 1)]

        with nc.Block() as block:
            @block.sync
            def _(sp):
                sp.dma_start(bias[:, :], T["sb_bias"].to_broadcast([P, SH])).then_inc(g["bias_loaded"], 16)

                def load(j, u, r):
                    wait_apart(sp, g["proj_done"], 2 * j + 2, g["passed"])
                    for x_ in range(2):
                        sp.dma_start(w[:, x_, :, :], w_view[:, :, bass.ds(j * P + (OQ + x_ * SBW), P)]).then_inc(g["w_loaded"], 16)
                    wait_apart(sp, g["k_tok_kept"], j + 2, g["passed"])
                    sp.dma_start(T["k_prompt"].rearrange("(n p) c -> p n c", p=P)[:, :, bass.ds(j * P, P)],
                                 k_tok[:, 0:NT, :]).then_inc(g["k_stored"], 16)
                    sp.dma_start(T["k_sample"][:, bass.ds(j * P, P)], k_tok[0:NS, NT, :]).then_inc(g["k_stored"], 16)

                each(sp, SH // 2, load, 1)
                sp.wait_ge(g["k_stored"], 32 + SH // 2 * 32)
                sp.wait_ge(keep["v_stored"], 32)

            @block.gpsimd
            def _(pool):
                def turn(j, u, r):
                    pool.wait_ge(g["qk_kept"], 4 * j + 4)
                    nc.gpsimd.tensor_copy(ks[:, bass.ds(j, 1), :].squeeze(1), k_s[:, :]).then_inc(g["ks_kept"], 1)
                    pool.wait_ge(g["av_done"], j * NB + 1)
                    nc.gpsimd.tensor_copy(v_pair[:, :, :], v_sb[:, 0:NT, bass.ds(j * P, P)]).then_inc(g["v_staged"], 1)

                    def mask(t, b, done):
                        lo = blocks[b][3]
                        nc.gpsimd.affine_select(out=t[:, b % BUF, lo:lo + P], in_=t[:, b % BUF, lo:lo + P],
                                                compare_op=ALU.is_gt, fill=0.0, base=0, pattern=[[1, P]],
                                                channel_multiplier=-1).then_inc(done, 1)

                    for i in range(NB + 1):
                        if i < NB and diagonal(i):
                            wait_apart(pool, g["sp_done"], j * NB + i + 1, g["passed"])
                            mask(sp_, i, g["sp_masked"])
                        if i >= 1 and diagonal(i - 1):
                            wait_apart(pool, g["a_done"], j * NB + i + 1, g["passed"])
                            mask(A, i - 1, g["a_masked"])

                nc.gpsimd.tensor_copy(v_new[:, :], v_sb[0:NS, NT, :])
                pool.sem_inc(g["k_stored"], 32)
                pool.sem_inc(g["ks_kept"], 1)
                pool.sem_inc(g["av_done"], 1)
                each(pool, SH // 2, turn, 1)

            @block.tensor
            def _(pe):
                pe.sem_inc(g["proj_done"], 2)

                def turn(j, u, r):
                    pe.wait_ge(g["w_loaded"], j * 32 + 32)
                    pe.wait_ge(g["run_kept"], j * NR + 1)
                    for x_, ps in ((0, ps_p[:, :]), (1, ps_z[:, 0:3, :].rearrange("p b c -> p (b c)"))):
                        if x_:
                            pe.wait_ge(g["a_done"], j * NB + 1)
                        for lo, hi in COLS:
                            for k in range(KT):
                                last = nc.tensor.matmul(ps[:, lo:hi], w[:, x_, k, :], hT[:, k, lo:hi],
                                                        start=(k == 0), stop=(k == KT - 1))
                        last.then_inc(g["proj_done"], 1)
                    pe.wait_ge(g["qk_kept"], j * 4 + 4)
                    for n in range(NT):
                        nc.tensor.transpose(ps_p[:, n * P:(n + 1) * P], qk[:, 1, n * P:(n + 1) * P], ident[:, :])
                    nc.tensor.transpose(ps_p[0:NS, NT * P:(NT + 1) * P], k_s[:, :], ident[:, :]).then_inc(g["k_turned"], 1)

                    def scores(b):
                        half, run, s, lo, _, _ = blocks[b]
                        rows = slice(half * HD, half * HD + HD)
                        if b >= BANKS:
                            pe.wait_ge(g["a_done"], j * NB + b - BANKS + 2)
                        nc.tensor.matmul(ps_z[:, b % BANKS, cols(b)], qk[rows, 1, s * P:(s + 1) * P],
                                         qk[rows, 0, run * WT + lo:run * WT + WT], start=True, stop=False,
                                         skip_group_check=True).then_inc(g["z_done"], 1)

                    def sums(b):
                        first = blocks[b][4]
                        if diagonal(b):
                            pe.wait_ge(g["sp_masked"], j * n_diag + diag_before[b + 1])
                        pe.wait_ge(g["sp_done"], j * NB + b + 1)
                        out = ps_z[:, b % BANKS, cols(b)]
                        last = nc.tensor.matmul(out, neg_from[:, :], sp_[:, b % BUF, cols(b)], start=False, stop=first,
                                                skip_group_check=True)
                        if not first:
                            pe.wait_ge(g["acc_done"], j * NB + b)
                            last = nc.tensor.matmul(out, neg_ones[:, :], acc[:, b % 2, cols(b)], start=False, stop=True,
                                                    skip_group_check=True)
                        last.then_inc(g["cum_done"], 1)

                    def values(b):
                        half, run, s, lo, first, final = blocks[b]
                        x_ = half * 2 + run
                        if diagonal(b):
                            pe.wait_ge(g["a_masked"], j * n_diag + diag_before[b + 1])
                        pe.wait_ge(g["a_done"], j * NB + b + 2)
                        if first:
                            pe.wait_ge(g["k_tok_kept"], j + 2)
                            if x_ >= 3:
                                pe.wait_ge(g["run_kept"], j * NR + x_ - 1)
                            pe.wait_ge(g["v_staged"], j + 1)
                        rows = slice(half * HD, half * HD + HD)
                        nc.tensor.matmul(ps_p[rows, x_ % 3 * 512 + lo:x_ % 3 * 512 + WT], v_pair[:, s, rows],
                                         A[:, b % BUF, cols(b)], start=first, stop=final,
                                         skip_group_check=True).then_inc(g["av_done"], 1)

                    for i in range(NB + 3):
                        if i < NB:
                            scores(i)
                        if 2 <= i < NB + 2:
                            sums(i - 2)
                        if i >= 3:
                            values(i - 3)

                each(pe, SH // 2, turn, 1)

            @block.scalar
            def _(act):
                act.sem_inc(g["a_done"], 1)
                act.sem_inc(g["k_tok_kept"], 1)
                act.wait_ge(g["bias_loaded"], 16)
                nc.scalar.preload_act_table_set("natural_log_exp_and_others")

                def turn(j, u, r):
                    act.wait_ge(g["proj_done"], 2 * j + 3)
                    nc.scalar.activation(qk[:, 0, :], ps_p[:, 0:SEQ], ACT.Copy, scale=HD ** -0.5).then_inc(g["qk_kept"], 1)
                    nc.scalar.activation(qs[:, bass.ds(j, 1), :].squeeze(1), ps_p[:, SEQ:TOK], ACT.Copy,
                                         scale=HD ** -0.5).then_inc(g["qk_kept"], 1)
                    act.wait_ge(g["proj_done"], 2 * j + 4)
                    ps_k = ps_z[:, 0:3, :].rearrange("p b c -> p (b c)")
                    nc.scalar.activation(qk[:, 1, :], ps_k[:, 0:SEQ], ACT.Copy).then_inc(g["qk_kept"], 1)
                    act.wait_ge(g["ks_kept"], j + 1)
                    nc.scalar.activation(k_s[:, :], ps_k[:, SEQ:TOK], ACT.Copy).then_inc(g["qk_kept"], 1)
                    act.wait_ge(g["k_turned"], j + 1)
                    act.wait_ge(g["k_stored"], j * 32 + 32)
                    nc.scalar.activation(k_tok[:, 0:NT, :].rearrange("p n c -> p (n c)"), ps_p[:, 0:SEQ], ACT.Copy)
                    nc.scalar.activation(k_tok[0:NS, NT, :], ps_p[0:NS, SEQ:SEQ + P], ACT.Copy).then_inc(g["k_tok_kept"], 1)
                    head = lambda b: bias[:, bass.ds(j * 2 + blocks[b][0], 1)]

                    def logs(b):
                        act.wait_ge(g["z_clipped"], j * NB + b + 1)
                        z = zc[:, b % BUF, cols(b)]
                        nc.scalar.activation(z, z, ACT.Exp).then_inc(g["exp_done"], 1)
                        act.wait_ge(g["exp_done"], j * NB + b + 1)
                        nc.scalar.activation(z, z, ACT.Ln, bias=1.0).then_inc(g["ln_done"], 1)

                    def weights(b):
                        if b >= BUF:
                            act.wait_ge(g["av_done"], j * NB + b - BUF + 2)
                        wait_apart(act, g["cum_done"], j * NB + b + 1, g["passed"])
                        nc.scalar.activation(A[:, b % BUF, cols(b)], ps_z[:, b % BANKS, cols(b)], ACT.Exp,
                                             bias=head(b)).then_inc(g["a_done"], 1)

                    for i in range(NB + 2):
                        if i < NB:
                            logs(i)
                        if i >= 2:
                            weights(i - 2)

                each(act, SH // 2, turn, 1)

            @block.vector
            def _(dve):
                dve.sem_inc(g["run_kept"], 1)
                dve.wait_ge(g["bias_loaded"], 16)

                def turn(j, u, r):
                    head = lambda b: bias[:, bass.ds(j * 2 + blocks[b][0], 1)]

                    def clip(b):
                        dve.wait_ge(g["z_done"], j * NB + b + 1)
                        nc.vector.tensor_scalar(zc[:, b % BUF, cols(b)], ps_z[:, b % BANKS, cols(b)], head(b), CLIP,
                                                ALU.add, ALU.min).then_inc(g["z_clipped"], 1)

                    def softplus(b):
                        half, run, s, lo, first, final = blocks[b]
                        dve.wait_ge(g["ln_done"], j * NB + b + 1)
                        if b >= BUF:
                            dve.wait_ge(g["cum_done"], j * NB + b - BUF + 1)
                        nc.vector.scalar_tensor_tensor(sp_[:, b % BUF, cols(b)], ps_z[:, b % BANKS, cols(b)], head(b),
                                                       zc[:, b % BUF, cols(b)], ALU.add, ALU.max).then_inc(g["sp_done"], 1)
                        if first:
                            if b:
                                dve.wait_ge(g["cum_done"], j * NB + b)
                            nc.vector.memset(acc[:, :, :], 0.0).then_inc(g["acc_zero"], 1)
                            dve.wait_ge(g["acc_zero"], j * NR + half * 2 + run + 1)
                        if diagonal(b):
                            dve.wait_ge(g["sp_masked"], j * n_diag + diag_before[b + 1])
                        else:
                            dve.wait_ge(g["sp_done"], j * NB + b + 1)
                        if b:
                            dve.wait_ge(g["acc_done"], j * NB + b)
                            dve.wait_ge(g["cum_done"], j * NB + b)
                        if not final:
                            nc.vector.tensor_tensor(acc[:, (b + 1) % 2, cols(b)], acc[:, b % 2, cols(b)],
                                                    sp_[:, b % BUF, cols(b)], ALU.add).then_inc(g["acc_done"], 1)
                        else:
                            dve.sem_inc(g["acc_done"], 1)

                    def keep_run(x_):
                        half, run = x_ // 2, x_ % 2
                        end = max(b for b in range(NB) if blocks[b][0:2] == (half, run))
                        rows = slice(half * HD, half * HD + HD)
                        dve.wait_ge(g["av_done"], j * NB + end + 2)
                        nc.vector.tensor_copy(mT[rows, bass.ds(j + KT - SBW // P, 1), run * WT:(run + 1) * WT].squeeze(1),
                                              ps_p[rows, x_ % 3 * 512:x_ % 3 * 512 + WT]).then_inc(g["run_kept"], 1)

                    ends = {b: blocks[b][0] * 2 + blocks[b][1] for b in range(NB) if blocks[b][5]}
                    for i in range(NB + 3):
                        if i < NB:
                            clip(i)
                        if 1 <= i < NB + 1:
                            softplus(i - 1)
                        if i >= 3 and i - 3 in ends:
                            keep_run(ends[i - 3])

                each(dve, SH // 2, turn, 1)


def sampled_attention(nc, T, keep):
    mT, v_new, qs, ks = keep["mT"], keep["v_new"], keep["qs"], keep["ks"]
    ident, neg_from, neg_ones = keep["ident"], keep["neg_from"], keep["neg_ones"]
    FT, HC = SBW // P, SH * ST
    TWO = 2 * ST
    HALF = NPAGE // 2
    with Phase(nc, "sa") as ph:
        k, v = ph.sb("k", [P, 2, NPAGE, SBW]), ph.sb("v", [P, 2, NPAGE, SBW])
        table = ph.sb("table", [1, SB * NPAGE], I32)
        kt = ph.sb("kt", [P, 2, FT, HALF * P])
        q_all, q_seq = ph.sb("q_all", [P, SB, FT, HC]), ph.sb("q_seq", [P, 2, FT, HC])
        z_rows = ph.sb("z_rows", [HC, 2, HALF * P])
        q2 = ph.sb("q2", [P, FT, SB, TWO])
        bias = ph.sb("bias", [P, SH])
        head_bias = ph.sb("head_bias", [P, SH, ST])
        bias2 = ph.sb("bias2", [P, SB, HC])
        mask, mask_n = ph.sb("mask", [NS, SB, ST]), ph.sb("mask_n", [NS, FT, SB, TWO])
        zn, cn = ph.sb("zn", [NS, FT, SB, TWO]), ph.sb("cn", [NS, FT, SB, TWO])
        an = ph.sb("an", [NS, FT, SB, TWO])
        y_new = ph.sb("y_new", [P, FT, SB, TWO])
        y_rows = ph.sb("y_rows", [HC, SBW])
        zb, zc, sp_, suf, a_in, A = (ph.sb(x_, [P, 2, NPAGE, HC]) for x_ in ("zb", "zc", "sp", "suf", "a_in", "A"))
        ps_t, ps_z = ph.ps("ps_t", [P, 2, 512]), ph.ps("ps_z", [P, 2, NPAGE, HC])
        ps_y, ps_o = ph.ps("ps_y", [P, 512]), ph.ps("ps_o", [P, FT, TWO])
        ps_n, ps_c = ph.ps("ps_n", [P, FT, SB, TWO]), ph.ps("ps_c", [P, FT, SB, TWO])
        ps_r = [ps[0:HC].rearrange("p f b c -> p (f b c)") for ps in (ps_n, ps_c)]
        names = ("bias_loaded did masked new_z new_clipped new_logs new_cum new_a q_ready turned kt_kept "
                 "rows_done z_rows_kept q_staged z_done z_read clipped logged sp_done suf_done cum_done a_in_done a_done values_done rows_kept y_new_done y_new_kept y_turned y_kept table_loaded passed stage_passed")
        g = {x_: ph.sem(x_) for x_ in names.split()}
        k_loaded, v_loaded = ([ph.sem(f"{x_}_loaded{u}") for u in range(2)] for x_ in "kv")
        flat = lambda ap: ap.rearrange("p f b c -> p (f b c)")
        row = lambda ap: ap.rearrange("p n c -> p (n c)")
        with nc.Block() as block:
            @block.sync
            def _(sp):
                sp.dma_start(table[:, :], T["page_table"]).then_inc(g["table_loaded"], 16)
                sp.dma_start(bias[:, :], T["sb_bias"].to_broadcast([P, SH])).then_inc(g["bias_loaded"], 16)
                sp.wait_ge(g["table_loaded"], 16)

                def load(b, u, r):
                    wait_apart(sp, g["turned"], b * NPAGE + NPAGE, g["passed"])
                    pages = [sp.value_load(table[0:1, bass.ds(b * NPAGE + n, 1)], min_val=0, max_val=79) for n in range(NPAGE)]
                    for n, page in enumerate(pages):
                        sp.dma_start(k[:, u, n, :], T["cache_k"][bass.ds(page, 1), :, :].squeeze(0)).then_inc(k_loaded[u], 16)
                    wait_apart(sp, g["values_done"], b + 1, g["passed"])
                    for n, page in enumerate(pages):
                        sp.dma_start(v[:, u, n, :], T["cache_v"][bass.ds(page, 1), :, :].squeeze(0)).then_inc(v_loaded[u], 16)

                each(sp, SB, load)

            @block.gpsimd
            def _(pool):
                nc.gpsimd.memset(mask[:, :, :], 1.0).then_inc(g["masked"], 1)
                pool.wait_ge(g["masked"], 1)
                nc.gpsimd.affine_select(out=mask[:, :, :], in_=mask[:, :, :], compare_op=ALU.is_gt, fill=0.0, base=0,
                                        pattern=[[ST, SB], [1, ST]], channel_multiplier=-1).then_inc(g["masked"], 1)
                pool.wait_ge(g["masked"], 2)
                nc.gpsimd.affine_select(out=mask[:, :, :], in_=mask[:, :, :], compare_op=ALU.is_ge, fill=0.0, base=0,
                                        pattern=[[-ST, SB], [0, ST]], channel_multiplier=1).then_inc(g["masked"], 1)

                def stage(b, u, r):
                    wait_apart(pool, g["rows_done"], 2 * b + 2, g["stage_passed"])
                    nc.gpsimd.tensor_copy(q_seq[:, u, :, :], q_all[:, bass.ds(b, 1), :, :].squeeze(1)).then_inc(g["q_staged"], 1)

                pool.wait_ge(g["masked"], 3)
                pool.wait_ge(g["q_ready"], 3)
                each(pool, SB, stage)

            @block.tensor
            def _(pe):
                pe.sem_inc(g["turned"], 2 * NPAGE)
                pe.sem_inc(g["rows_done"], 4)
                pe.sem_inc(g["cum_done"], 2)
                pe.sem_inc(g["values_done"], 2)
                pe.wait_ge(g["q_ready"], 3)
                for f in range(FT):
                    last = nc.tensor.matmul(ps_n[0:NS, f, :, :], ks[:, f, :], q2[:, f, :, :], start=(f == 0), stop=False,
                                            skip_group_check=True)
                last.then_inc(g["new_z"], 1)
                pe.wait_ge(g["new_logs"], 2)
                nc.tensor.matmul(flat(ps_n[0:NS]), neg_from[0:NS, 0:NS], flat(zn), start=False, stop=True,
                                 skip_group_check=True)
                nc.tensor.matmul(flat(ps_c), neg_ones[0:NS, :], flat(zn), start=True, stop=True).then_inc(g["new_cum"], 1)

                pe.wait_ge(g["new_a"], 3)
                for f in range(FT):
                    last = nc.tensor.matmul(ps_y[:, f * P:(f + 1) * P], v_new[:, f * P:(f + 1) * P],
                                            an[:, f, :, :].rearrange("p b c -> p (b c)"), start=True, stop=True)
                last.then_inc(g["y_new_done"], 1)
                pe.wait_ge(g["y_new_kept"], 1)

                def turn(b, u, r, half):
                    if half == 0:
                        pe.wait_ge(k_loaded[u], r * (16 * NPAGE) + 16 * NPAGE)
                    for n in range(half * HALF, (half + 1) * HALF):
                        pe.wait_ge(g["kt_kept"], b * NPAGE + n + 1)
                        for f in range(FT):
                            last = nc.tensor.transpose(ps_t[:, n % 2, f * P:(f + 1) * P], k[:, u, n, f * P:(f + 1) * P], ident[:, :])
                        last.then_inc(g["turned"], 1)

                def score(b, u, half):
                    pe.wait_ge(g["q_staged"], b + 1)
                    pe.wait_ge(g["kt_kept"], b * NPAGE + (half + 1) * HALF + 2)
                    for f in range(FT):
                        last = nc.tensor.matmul(ps_r[half], q_seq[:, u, f, :], kt[:, half, f, :], start=(f == 0), stop=(f == FT - 1))
                    last.then_inc(g["rows_done"], 1)

                def turn_scores(b, u, half):
                    if half == 0:
                        pe.wait_ge(g["a_in_done"], b + 1)
                    pe.wait_ge(g["z_rows_kept"], 2 * b + half + 1)
                    for n in range(half * HALF, (half + 1) * HALF):
                        at = n % HALF * P
                        last = nc.tensor.matmul(ps_z[:, u, n, :], z_rows[:, half, at:at + P], ident[0:HC, 0:HC],
                                                start=(n == 0), stop=False, skip_group_check=True)
                    if half:
                        last.then_inc(g["z_done"], 1)

                def sums(b, u, r):
                    pe.wait_ge(g["sp_done"], b + 1)
                    nc.tensor.matmul(row(ps_z[:, u]), neg_from[:, :], row(sp_[:, u]), start=False, stop=False, skip_group_check=True)
                    pe.wait_ge(g["suf_done"], b * (NPAGE - 1) + NPAGE - 1 + 2)
                    nc.tensor.matmul(row(ps_z[:, u]), neg_ones[:, :], row(suf[:, u]), start=False, stop=True,
                                     skip_group_check=True).then_inc(g["cum_done"], 1)

                def values(b, u, r):
                    pe.wait_ge(v_loaded[u], r * (16 * NPAGE) + 16 * NPAGE)
                    pe.wait_ge(g["rows_kept"], b + 1)
                    pe.wait_ge(g["a_done"], b + 3)
                    for n in range(NPAGE):
                        last = nc.tensor.matmul(ps_y[0:HC, :], A[:, u, n, :], v[:, u, n, :], start=(n == 0), stop=(n == NPAGE - 1))
                    last.then_inc(g["values_done"], 1)

                def turn_rows(b):
                    pe.wait_ge(g["rows_kept"], b + 2)
                    pe.wait_ge(g["y_kept"], b * 2 + 1)
                    for f in range(FT):
                        last = nc.tensor.matmul(ps_o[:, f, :], y_rows[:, f * P:(f + 1) * P], ident[0:HC, f * TWO:(f + 1) * TWO],
                                                start=True, stop=True)
                    last.then_inc(g["y_turned"], 1)

                def both(b, u, r, last=False, first=False):
                    v, q = (u + 1) % 2, r + u
                    if not last:
                        turn(b + 1, v, q, 0)
                    if not first:
                        turn_rows(b - 1)
                    if not last:
                        score(b + 1, v, 0)
                        turn(b + 1, v, q, 1)
                    sums(b, u, r)
                    if not last:
                        score(b + 1, v, 1)
                        turn_scores(b + 1, v, 0)
                        turn_scores(b + 1, v, 1)
                    values(b, u, r)

                for half in range(2):
                    turn(0, 0, 0, half)
                    score(0, 0, half)
                turn_scores(0, 0, 0)
                turn_scores(0, 0, 1)
                both(0, 0, 0, first=True)
                with pe.Fori(0, (SB - 2) // 2) as i:
                    both(i * 2 + 1, 1, i)
                    both(i * 2 + 2, 0, i + 1)
                both(SB - 1, 1, SB // 2 - 1, last=True)
                turn_rows(SB - 1)

            @block.scalar
            def _(act):
                act.sem_inc(g["kt_kept"], 2)
                act.sem_inc(g["a_done"], 2)
                nc.scalar.preload_act_table_set("natural_log_exp_and_others")
                act.wait_ge(g["new_clipped"], 1)
                nc.scalar.activation(flat(cn), flat(cn), ACT.Exp).then_inc(g["new_clipped"], 1)
                act.wait_ge(g["new_clipped"], 2)
                nc.scalar.activation(flat(cn), flat(cn), ACT.Ln, bias=1.0).then_inc(g["new_clipped"], 1)
                act.wait_ge(g["new_a"], 1)
                nc.scalar.activation(flat(an), flat(an), ACT.Exp).then_inc(g["new_a"], 1)

                def keep_keys(b):
                    for n in range(NPAGE):
                        act.wait_ge(g["turned"], b * NPAGE + n + 1 + 2 * NPAGE)
                        half, at = n // HALF, n % HALF * P
                        if n % HALF == 0:
                            act.wait_ge(g["rows_done"], 2 * b + half + 3)
                        nc.scalar.activation(kt[:, half, :, at:at + P], ps_t[:, n % 2, :].rearrange("p (f s) -> p f s", f=FT),
                                             ACT.Copy).then_inc(g["kt_kept"], 1)

                def logs(b, u):
                    act.wait_ge(g["clipped"], b + 1)
                    z = row(zc[:, u])
                    nc.scalar.activation(z, z, ACT.Exp).then_inc(g["logged"], 1)
                    act.wait_ge(g["logged"], 2 * b + 1)
                    nc.scalar.activation(z, z, ACT.Ln, bias=1.0).then_inc(g["logged"], 1)

                def weights(b, u):
                    act.wait_ge(g["values_done"], b + 1)
                    act.wait_ge(g["a_in_done"], b + 3)
                    nc.scalar.activation(row(A[:, u]), row(a_in[:, u]), ACT.Exp).then_inc(g["a_done"], 1)

                def both(b, u, r):
                    keep_keys(b + 1)
                    weights(b, u)
                    logs(b + 1, (u + 1) % 2)

                keep_keys(0)
                logs(0, 0)
                each(act, SB - 2, both)
                both(SB - 2, 0, 0)
                weights(SB - 1, 1)

            @block.vector
            def _(dve):
                count = [0]

                def step(ins, sem="did"):
                    if sem == "did":
                        count[0] += 1
                    ins.then_inc(g[sem], 1)
                    if sem == "did":
                        dve.wait_ge(g["did"], count[0])

                dve.sem_inc(g["a_in_done"], 2)
                dve.sem_inc(g["y_kept"], 2)
                dve.sem_inc(g["rows_kept"], 1)
                dve.sem_inc(g["y_turned"], 1)
                step(nc.vector.memset(q_all[:, :, :, :], 0.0))
                step(nc.vector.memset(flat(q2), 0.0))
                nc.vector.tensor_copy(q2[0:HD, :, :, 0:ST], qs[0:HD, :, :].rearrange("p f (b t) -> p f b t", b=SB)).then_inc(g["q_ready"], 1)
                nc.vector.tensor_copy(q2[HD:P, :, :, ST:TWO], qs[HD:P, :, :].rearrange("p f (b t) -> p f b t", b=SB)).then_inc(g["q_ready"], 1)
                dve.wait_ge(g["did"], count[0])
                for f in range(FT):
                    for x_ in range(2):
                        rows, at = slice(x_ * HD, x_ * HD + HD), (2 * f + x_) * ST
                        step(nc.vector.tensor_copy(q_all[rows, :, f, at:at + ST], qs[rows, f, :].rearrange("p (b t) -> p b t", b=SB)))
                dve.wait_ge(g["q_ready"], 2)
                dve.sem_inc(g["q_ready"], 1)
                nc.vector.memset(suf[:, 0, NPAGE - 1, :], 0.0).then_inc(g["suf_done"], 1)
                nc.vector.memset(suf[:, 1, NPAGE - 1, :], 0.0).then_inc(g["suf_done"], 1)
                dve.wait_ge(g["bias_loaded"], 16)
                step(nc.vector.tensor_copy(head_bias[:, :, :], bc(bias[:, :], 2, ST)))
                dve.wait_ge(g["masked"], 3)
                for f in range(FT):
                    for x_ in range(2):
                        step(nc.vector.tensor_copy(mask_n[:, f, :, x_ * ST:(x_ + 1) * ST], mask[:, :, :]))
                dve.wait_ge(g["new_z"], 1)
                hb = lambda rows, f: bc(head_bias[rows, 2 * f:2 * f + 2, :].rearrange("p h t -> p (h t)"), 1, SB)
                for f in range(FT):
                    step(nc.vector.tensor_tensor(zn[:, f, :, :], ps_n[0:NS, f, :, :], hb(slice(0, NS), f), ALU.add))
                nc.vector.tensor_scalar(flat(cn), flat(zn), CLIP, None, ALU.min).then_inc(g["new_clipped"], 1)
                dve.wait_ge(g["new_clipped"], 3)
                nc.vector.tensor_tensor(flat(zn), flat(zn), flat(cn), ALU.max).then_inc(g["new_logs"], 1)
                dve.wait_ge(g["new_logs"], 1)
                nc.vector.tensor_tensor(flat(zn), flat(zn), flat(mask_n), ALU.mult).then_inc(g["new_logs"], 1)
                dve.wait_ge(g["new_cum"], 1)
                for f in range(FT):
                    step(nc.vector.tensor_tensor(an[:, f, :, :], ps_n[0:NS, f, :, :], hb(slice(0, NS), f), ALU.add))
                    step(nc.vector.tensor_tensor(bias2[:, :, f * TWO:(f + 1) * TWO], ps_c[:, f, :, :], hb(slice(0, P), f), ALU.add))
                nc.vector.tensor_tensor(flat(an), flat(an), flat(mask_n), ALU.mult).then_inc(g["new_a"], 1)
                dve.wait_ge(g["new_a"], 2)
                nc.vector.tensor_tensor(flat(an), flat(an), flat(mask_n), ALU.mult).then_inc(g["new_a"], 1)
                dve.wait_ge(g["y_new_done"], 1)
                nc.vector.tensor_copy(flat(y_new), ps_y[:, :]).then_inc(g["y_new_kept"], 1)

                def softplus(b, u):
                    dve.wait_ge(g["z_done"], b + 1)
                    page_bias = bc(head_bias[:, :, :].rearrange("p h t -> p (h t)"), 1, NPAGE)
                    nc.vector.tensor_tensor(zb[:, u], ps_z[:, u], page_bias, ALU.add).then_inc(g["z_read"], 1)
                    dve.wait_ge(g["z_read"], b + 1)
                    nc.vector.tensor_scalar(row(zc[:, u]), row(zb[:, u]), CLIP, None, ALU.min).then_inc(g["clipped"], 1)
                    dve.wait_ge(g["logged"], 2 * b + 2)
                    dve.wait_ge(g["cum_done"], b + 1)
                    nc.vector.tensor_tensor(row(sp_[:, u]), row(zb[:, u]), row(zc[:, u]), ALU.max).then_inc(g["sp_done"], 1)
                    dve.wait_ge(g["sp_done"], b + 1)
                    for n in range(NPAGE - 2, -1, -1):
                        dve.wait_ge(g["suf_done"], b * (NPAGE - 1) + NPAGE - n)
                        nc.vector.tensor_tensor(suf[:, u, n, :], suf[:, u, n + 1, :], sp_[:, u, n + 1, :], ALU.add).then_inc(g["suf_done"], 1)

                def weights_in(b, u):
                    dve.wait_ge(g["cum_done"], b + 3)
                    dve.wait_ge(g["a_done"], b + 1)
                    nc.vector.tensor_tensor(a_in[:, u], ps_z[:, u], bc(bias2[:, bass.ds(b, 1), :].squeeze(1), 1, NPAGE),
                                            ALU.add).then_inc(g["a_in_done"], 1)

                def keep_rows(b):
                    dve.wait_ge(g["values_done"], b + 3)
                    dve.wait_ge(g["y_turned"], b + 1)
                    nc.vector.tensor_copy(y_rows[:, :], ps_y[0:HC, :]).then_inc(g["rows_kept"], 1)

                def keep_output(b):
                    dve.wait_ge(g["y_turned"], b + 2)
                    for x_ in range(2):
                        rows, at = slice(x_ * HD, x_ * HD + HD), slice(x_ * ST, (x_ + 1) * ST)
                        nc.vector.tensor_tensor(mT[rows, KT - FT:KT, bass.ds(b * ST + SEQ, ST)], ps_o[rows, :, at],
                                                y_new[rows, :, bass.ds(b, 1), at].squeeze(2), ALU.add).then_inc(g["y_kept"], 1)

                def keep_scores(b, half):
                    dve.wait_ge(g["rows_done"], 2 * b + half + 1 + 4)
                    nc.vector.tensor_copy(z_rows[:, half, :], ps_r[half]).then_inc(g["z_rows_kept"], 1)

                def both(b, u, r, first=False):
                    if not first:
                        keep_output(b - 1)
                    keep_scores(b + 1, 0)
                    weights_in(b, u)
                    keep_scores(b + 1, 1)
                    softplus(b + 1, (u + 1) % 2)
                    keep_rows(b)

                keep_scores(0, 0)
                keep_scores(0, 1)
                softplus(0, 0)
                both(0, 0, 0, first=True)
                with dve.Fori(0, (SB - 2) // 2) as i:
                    both(i * 2 + 1, 1, i)
                    both(i * 2 + 2, 0, i + 1)
                keep_output(SB - 2)
                weights_in(SB - 1, 1)
                keep_rows(SB - 1)
                keep_output(SB - 1)


def out_project(nc, T, keep, mod_rows, h2_rows):
    mT, x1, logits, ident = keep["mT"], keep["x1"], keep["logits"], keep["ident"]
    NL = NGR + NE
    with Phase(nc, "op") as ph:
        w = ph.sb("w", [P, KT, D])
        wr, br = ph.sb("wr", [P, KT, NL]), ph.sb("br", [P, NL])
        g = ph.sb("g", [P, D])
        gate = {"p": ph.sb("gate_p", [P, D]), "s": ph.sb("gate_s", [NS, D])}
        gain = {"p": ph.sb("gain_p", [P, D]), "s": ph.sb("gain_s", [NS, D])}
        shift = {"p": ph.sb("shift_p", [P, D]), "s": ph.sb("shift_s", [NS, D])}
        m_t = ph.sb("m_t", [P, 2, KT, P])
        gated, squares, h2 = (ph.sb(x_, [P, 2, D]) for x_ in ("gated", "squares", "h2"))
        ht = ph.sb("ht", [P, KT, P])
        ss, ms, rt, rstd = (ph.sb(x_, [P, 2]) for x_ in ("ss", "ms", "rt", "rstd"))
        ps_o, ps_h, ps_l = ph.ps("ps_o", [P, 2, D]), ph.ps("ps_h", [P, KT, P]), ph.ps("ps_l", [P, NL])
        names = ("x_loaded mod_s_loaded r_loaded mod_loaded gains staged product_done gated_done x1_done sq_done ms_done rt_done rstd_done "
                 "scaled h2_done turned ht_kept routed logits_kept")
        s = {x_: ph.sem(x_) for x_ in names.split()}
        stored = keep["h2_stored"]
        w_loaded = [ph.sem(f"w_loaded{x_}") for x_ in range(2)]
        with nc.Block() as block:
            @block.sync
            def _(sp):
                for x_ in range(2):
                    cols = slice(x_ * 512, x_ * 512 + 512)
                    sp.dma_start(w[:, :, cols], T["w_out"].rearrange("(k p) n -> p k n", p=P)[:, :, cols]).then_inc(w_loaded[x_], 16)
                sp.dma_start(x1[:, 0:NT, :], T["x_prompt"].rearrange("(n p) d -> p n d", p=P)).then_inc(s["x_loaded"], 16)
                sp.dma_start(x1[0:NS, NT, :], T["x_sample"]).then_inc(s["x_loaded"], 16)
                load_mod(sp, gate["p"], mod_rows, 2, s["mod_loaded"])
                load_mod(sp, gain["p"], mod_rows, 4, s["mod_loaded"])
                load_mod(sp, shift["p"], mod_rows, 3, s["mod_loaded"])
                sp.dma_start(wr[:, :, 0:NGR], T["router_g_w"].rearrange("(k p) n -> p k n", p=P)).then_inc(s["r_loaded"], 16)
                sp.dma_start(wr[:, :, NGR:], T["router_e_w"].rearrange("(k p) n -> p k n", p=P)).then_inc(s["r_loaded"], 16)

                def store(n, u, r):
                    m = rows_of(n)
                    sp.wait_ge(s["h2_done"], n + 1)
                    sp.dma_start(h2_rows[bass.ds(n * P, m), :], h2[0:m, u, :]).then_inc(stored[u], 16)

                each(sp, NT + 1, store)

            @block.gpsimd
            def _(pool):
                pool.sem_inc(s["product_done"], 2)

                def stage(n, u, r):
                    m = rows_of(n)
                    pool.wait_ge(s["product_done"], n + 1)
                    nc.gpsimd.tensor_copy(m_t[:, u, :, 0:m], mT[:, :, bass.ds(n * P, m)]).then_inc(s["staged"], 1)

                each(pool, 2, stage)
                for what, dst in ((2, gate), (4, gain), (3, shift)):
                    load_mod_sampled(pool, dst["s"], mod_rows, what, s["mod_s_loaded"])
                with pool.Fori(1, NT // 2) as i:
                    for u in range(2):
                        stage(i * 2 + u, u, i)
                stage(NT, NT % 2, NT // 2)

            @block.tensor
            def _(pe):

                def product(n, u, half):
                    m, lo = rows_of(n), half * 512
                    if half == 0:
                        pe.wait_ge(s["staged"], n + 1)
                        pe.wait_ge(s["gated_done"], n + 1)
                    pe.wait_ge(w_loaded[half], 16)
                    for k in range(KT):
                        last = nc.tensor.matmul(ps_o[0:m, u, lo:lo + 512], m_t[:, u, k, 0:m], w[:, k, lo:lo + 512],
                                                start=(k == 0), stop=(k == KT - 1))
                    if half:
                        last.then_inc(s["product_done"], 1)

                def turn(n, u):
                    m = rows_of(n)
                    pe.wait_ge(s["h2_done"], n + 1)
                    pe.wait_ge(s["ht_kept"], n + 1)
                    for k in range(KT):
                        last = nc.tensor.transpose(ps_h[:, k, 0:m], h2[0:m, u, k * P:(k + 1) * P], ident[0:m, 0:m])
                    last.then_inc(s["turned"], 1)

                def route(n, u):
                    m = rows_of(n)
                    pe.wait_ge(s["ht_kept"], n + 2)
                    pe.wait_ge(s["logits_kept"], n + 1)
                    pe.wait_ge(s["r_loaded"], 48)
                    for k in range(KT):
                        last = nc.tensor.matmul(ps_l[0:m, :], ht[:, k, 0:m], wr[:, k, :], start=(k == 0), stop=(k == KT - 1))
                    last.then_inc(s["routed"], 1)

                def both(n, u, r):
                    turn(n, u)
                    product(n + 2, u, 0)
                    route(n, u)
                    product(n + 2, u, 1)

                for n in range(2):
                    product(n, n, 0)
                    product(n, n, 1)
                each(pe, NT - 2, both)
                both(NT - 2, 0, 0)
                for n in (NT - 1, NT):
                    turn(n, n % 2)
                    route(n, n % 2)

            @block.scalar
            def _(act):
                act.dma_start(g[:, :], T["norm2_g"].to_broadcast([P, D])).then_inc(s["r_loaded"], 16)
                act.dma_start(br[:, 0:NGR], T["router_g_b"].to_broadcast([P, NGR])).then_inc(s["mod_loaded"], 16)
                act.dma_start(br[:, NGR:], T["router_e_b"].to_broadcast([P, NE])).then_inc(s["mod_loaded"], 16)
                act.sem_inc(s["ht_kept"], 1)

                def stats(n, u, r):
                    m = rows_of(n)
                    act.wait_ge(s["x1_done"], n + 1)
                    nc.scalar.activation(squares[0:m, u, :], x1[0:m, bass.ds(n, 1), :].squeeze(1), ACT.Square,
                                         accum_out=ss[0:m, u:u + 1]).then_inc(s["sq_done"], 1)
                    act.wait_ge(s["ms_done"], n + 1)
                    nc.scalar.activation(rt[0:m, u:u + 1], ms[0:m, u:u + 1], ACT.Sqrt).then_inc(s["rt_done"], 1)

                def evacuate(n, u, r):
                    m = rows_of(n)
                    act.wait_ge(s["turned"], n + 1)
                    act.wait_ge(s["routed"], n + 1)
                    nc.scalar.activation(ht[:, :, 0:m], ps_h[:, :, 0:m], ACT.Copy).then_inc(s["ht_kept"], 1)

                ahead(act, NT + 1, stats, evacuate, back_first=True)

            @block.vector
            def _(dve):
                dve.sem_inc(s["gated_done"], 2)
                for u in range(2):
                    dve.sem_inc(stored[u], 16)
                dve.sem_inc(s["logits_kept"], 1)
                dve.sem_inc(s["routed"], 1)
                nc.vector.memset(logits[:, NT, :], 0.0).then_inc(s["gains"], 1)
                dve.wait_ge(s["r_loaded"], 48)
                dve.wait_ge(s["mod_loaded"], 16 * 5)
                nc.vector.scalar_tensor_tensor(gain["p"][:, :], gain["p"][:, :], 1.0, g[:, :],
                                               ALU.add, ALU.mult).then_inc(s["gains"], 1)
                dve.wait_ge(s["gains"], 2)
                dve.wait_ge(s["x_loaded"], 32)

                def norm(n, u, r):
                    m = rows_of(n)
                    group = "s" if m == NS else "p"
                    if group == "s":
                        dve.wait_ge(s["mod_s_loaded"], 3 * SB * 16)
                        nc.vector.scalar_tensor_tensor(gain["s"][:, :], gain["s"][:, :], 1.0, g[0:NS, :],
                                                       ALU.add, ALU.mult).then_inc(s["gains"], 1)
                        dve.wait_ge(s["gains"], 3)
                    x = x1[0:m, bass.ds(n, 1), :].squeeze(1)
                    dve.wait_ge(s["product_done"], n + 3)
                    nc.vector.tensor_tensor(gated[0:m, u, :], ps_o[0:m, u, :], gate[group][0:m, :], ALU.mult).then_inc(s["gated_done"], 1)
                    dve.wait_ge(s["gated_done"], n + 3)
                    nc.vector.tensor_tensor(x, x, gated[0:m, u, :], ALU.add).then_inc(s["x1_done"], 1)
                    dve.wait_ge(s["sq_done"], n + 1)
                    nc.vector.tensor_scalar(ms[0:m, u:u + 1], ss[0:m, u:u + 1], 1.0 / D, RMS_EPS,
                                            ALU.mult, ALU.add).then_inc(s["ms_done"], 1)
                    dve.wait_ge(s["rt_done"], n + 1)
                    nc.vector.reciprocal(rstd[0:m, u:u + 1], rt[0:m, u:u + 1]).then_inc(s["rstd_done"], 1)
                    dve.wait_ge(s["rstd_done"], n + 1)
                    dve.wait_ge(stored[u], r * 16 + 16)
                    nc.vector.scalar_tensor_tensor(h2[0:m, u, :], x, rstd[0:m, u:u + 1], gain[group][0:m, :],
                                                   ALU.mult, ALU.mult).then_inc(s["scaled"], 1)
                    dve.wait_ge(s["scaled"], n + 1)
                    nc.vector.tensor_tensor(h2[0:m, u, :], h2[0:m, u, :], shift[group][0:m, :], ALU.add).then_inc(s["h2_done"], 1)

                def keep_logits(n, u, r):
                    m = rows_of(n)
                    dve.wait_ge(s["routed"], n + 2)
                    nc.vector.tensor_tensor(logits[0:m, bass.ds(n, 1), :].squeeze(1), ps_l[0:m, :], br[0:m, :],
                                            ALU.add).then_inc(s["logits_kept"], 1)

                ahead(dve, NT + 1, norm, keep_logits)


def route(nc, T, keep, slot_token, tile_expert):
    logits, slots, gates, neg_ones = keep["logits"], keep["slots"], keep["gates"], keep["neg_ones"]
    N, EG = NT + 1, NE // NGR
    MAX_TILES = -(-TOK // P)
    with Phase(nc, "rt") as ph:
        low_first = ph.sb("low_first", [P, EG])
        before = ph.sb("before", [P, P])
        experts_before = ph.sb("experts_before", [P, NE, NE])
        starts, tiles_at = ph.sb("starts", [P, MAX_TILES]), ph.sb("tiles_at", [P, ET])
        token = ph.sb("token", [P, N], I32)
        zeros = ph.sb("zeros", [P, ET], I32)
        gl, el = ph.sb("gl", [P, N, EG]), ph.sb("el", [P, N, EG])
        top, total, pg, two = (ph.sb(x_, [P, N]) for x_ in ("top", "total", "pg", "two"))
        key, pick_g = ph.sb("key", [P, N, EG]), ph.sb("pick_g", [P, N, EG])
        picks = ph.sb("picks", [P, N, 2, EG])
        tmp = ph.sb("tmp", [P, N, NGR, EG])
        chosen, place = ph.sb("chosen", [P, N * 2, NE]), ph.sb("place", [P, N * 2, NE])
        run = ph.sb("run", [P, N * 2 + 1, NE])
        tiles, first = ph.sb("tiles", [P, NE]), ph.sb("first", [P, NE])
        cmp1, cmp2, cmp3 = ph.sb("cmp1", [P, NE, MAX_TILES]), ph.sb("cmp2", [P, NE, NE]), ph.sb("cmp3", [P, ET, NE])
        slot_f, expert_f = ph.sb("slot_f", [P, N * 2]), ph.sb("expert_f", [P, ET + 1])
        used, cmp4 = ph.sb("used", [P, 1]), ph.sb("cmp4", [P, ET // 2 - 1])
        expert = ph.sb("expert", [P, ET + 1], I32)
        iota_i, iota_j = ph.sb("iota_i", [P, ET], I32), ph.sb("iota_j", [P, MAX_TILES], I32)
        ps_before, ps_total = ph.ps("ps_before", [P, N * 2, NE]), ph.ps("ps_total", [P, N * 2, NE])
        built, did, exped, counted, zeroed, stored, scattered = (ph.sem(x_) for x_ in (
            "built", "did", "exped", "counted", "zeroed", "stored", "scattered"))
        PICKED, PLACED, EXPERT = 34, 68, 75
        with nc.Block() as block:
            @block.gpsimd
            def _(pool):
                nc.gpsimd.memset(before[:, :], -1.0).then_inc(built, 1)
                nc.gpsimd.memset(experts_before[:, :, :], 1.0).then_inc(built, 1)
                nc.gpsimd.memset(zeros[:, :], 0).then_inc(built, 1)
                nc.gpsimd.iota(token[:, :], pattern=[[P, N]], base=0, channel_multiplier=1).then_inc(built, 1)
                nc.gpsimd.iota(iota_i[:, :], pattern=[[1, ET]], base=0, channel_multiplier=0).then_inc(built, 1)
                nc.gpsimd.iota(iota_j[:, :], pattern=[[P, MAX_TILES]], base=0, channel_multiplier=0).then_inc(built, 1)
                pool.wait_ge(built, 6)
                nc.gpsimd.affine_select(out=before[:, :], in_=before[:, :], compare_op=ALU.is_gt, fill=0.0, base=0,
                                        pattern=[[1, P]], channel_multiplier=-1).then_inc(built, 1)
                nc.gpsimd.affine_select(out=experts_before[:, :, :], in_=experts_before[:, :, :], compare_op=ALU.is_gt,
                                        fill=0.0, base=0, pattern=[[1, NE], [-1, NE]], channel_multiplier=0).then_inc(built, 1)
                pool.wait_ge(zeroed, 16)
                pool.wait_ge(did, PLACED)
                for n in range(N):
                    for c in range(2):
                        m = rows_of(n)
                        nc.gpsimd.indirect_dma_start(
                            slot_token, bass.IndirectOffsetOnAxis(ap=slots[0:m, n * 2 + c:n * 2 + c + 1], axis=0),
                            token[0:m, n:n + 1].bitcast(U32), None).then_inc(scattered, 16)
                pool.wait_ge(scattered, 16 * 2 * N)

            @block.sync
            def _(sp):
                sp.wait_ge(built, 6)
                sp.dma_start(slot_token.rearrange("(p t) a -> p (t a)", p=P), zeros[:, :].bitcast(U32)).then_inc(zeroed, 16)
                sp.wait_ge(did, EXPERT)
                sp.dma_start(tile_expert, expert[0:1, :]).then_inc(stored, 16)
                sp.wait_ge(stored, 16)

            @block.tensor
            def _(pe):
                pe.wait_ge(built, 8)
                pe.wait_ge(did, PICKED)
                for out, w in ((ps_before, before), (ps_total, neg_ones)):
                    nc.tensor.matmul(out[:, :, :].rearrange("p n e -> p (n e)"), w[:, :],
                                     chosen[:, :, :].rearrange("p n e -> p (n e)"), start=True, stop=True).then_inc(counted, 1)

            @block.scalar
            def _(act):
                for i, (t, after) in enumerate(((gl, 6), (el, 16))):
                    act.wait_ge(did, after)
                    nc.scalar.activation(t[:, :, :], t[:, :, :], ACT.Exp).then_inc(exped, 1)

            @block.vector
            def _(dve):
                count = [0]

                def step(ins):
                    count[0] += 1
                    ins.then_inc(did, 1)
                    dve.wait_ge(did, count[0])

                V = nc.vector

                def pick(out, values, best):
                    step(V.tensor_tensor(key[:, :, :], values, bc(best, 2, EG), ALU.is_equal))
                    step(V.tensor_tensor(key[:, :, :], key[:, :, :], bc(low_first[:, :], 1, N), ALU.mult))
                    step(V.tensor_reduce(two[:, :], key[:, :, :], axis=AXX, op=ALU.max))
                    step(V.tensor_tensor(out, key[:, :, :], bc(two[:, :], 2, EG), ALU.is_equal))

                for e in range(EG):
                    step(V.memset(low_first[:, e:e + 1], float(EG - e)))
                step(V.tensor_reduce(top[:, :], logits[:, :, 0:NGR], axis=AXX, op=ALU.max))
                step(V.tensor_tensor(gl[:, :, :], logits[:, :, 0:NGR], bc(top[:, :], 2, NGR), ALU.subtract))
                dve.wait_ge(exped, 1)
                step(V.tensor_reduce(total[:, :], gl[:, :, :], axis=AXX, op=ALU.add))
                step(V.tensor_reduce(top[:, :], gl[:, :, :], axis=AXX, op=ALU.max))
                pick(pick_g[:, :, :], gl[:, :, :], top[:, :])
                el4 = logits[:, :, NGR:].rearrange("p n (g e) -> p n g e", e=EG)
                step(V.tensor_tensor(tmp[:, :, :, :], el4, bc(pick_g[:, :, :], 3, EG), ALU.mult))
                step(V.tensor_reduce(el[:, :, :], tmp[:, :, :, :].rearrange("p n g e -> p n e g"), axis=AXX, op=ALU.add))
                step(V.tensor_reduce(top[:, :], el[:, :, :], axis=AXX, op=ALU.max))
                step(V.tensor_tensor(el[:, :, :], el[:, :, :], bc(top[:, :], 2, EG), ALU.subtract))
                dve.wait_ge(exped, 2)
                step(V.tensor_reduce(gates[:, :, 0], el[:, :, :], axis=AXX, op=ALU.max))
                pick(picks[:, :, 0, :], el[:, :, :], gates[:, :, 0])
                step(V.tensor_tensor(tmp[:, :, 0, :], el[:, :, :], picks[:, :, 0, :], ALU.mult))
                step(V.tensor_tensor(el[:, :, :], el[:, :, :], tmp[:, :, 0, :], ALU.subtract))
                step(V.tensor_tensor(el[:, :, :], el[:, :, :], picks[:, :, 0, :], ALU.subtract))
                step(V.tensor_reduce(gates[:, :, 1], el[:, :, :], axis=AXX, op=ALU.max))
                pick(picks[:, :, 1, :], el[:, :, :], gates[:, :, 1])
                for c in range(2):
                    step(V.tensor_tensor(tmp[:, :, :, :], bc(pick_g[:, :, :], 3, EG), bc(picks[:, :, c, :], 2, NGR), ALU.mult))
                    step(V.tensor_copy(chosen[:, :, :].rearrange("p (n c) e -> p n c e", c=2)[:, :, c, :],
                                       tmp[:, :, :, :].rearrange("p n g e -> p n (g e)")))
                step(V.memset(chosen[NS:P, 2 * NT:, :], 0.0))
                assert count[0] == PICKED, count[0]
                step(V.tensor_tensor(two[:, :], gates[:, :, 0], gates[:, :, 1], ALU.add))
                step(V.tensor_tensor(two[:, :], two[:, :], total[:, :], ALU.mult))
                step(V.reciprocal(pg[:, :], two[:, :]))
                step(V.tensor_tensor(gates[:, :, :], gates[:, :, :], bc(pg[:, :], 2, 2), ALU.mult))
                dve.wait_ge(built, 8)
                step(V.tensor_copy(starts[:, :], iota_j[:, :]))
                step(V.tensor_copy(tiles_at[:, :], iota_i[:, :]))
                step(V.memset(run[:, 0, :], 0.0))
                dve.wait_ge(counted, 2)
                for n in range(2 * N):
                    step(V.tensor_tensor(run[:, n + 1, :], run[:, n, :], ps_total[:, n, :], ALU.subtract))
                step(V.tensor_tensor(cmp1[:, :, :], bc(run[:, 2 * N, :], 2, MAX_TILES), bc(starts[:, :], 1, NE), ALU.is_gt))
                step(V.tensor_reduce(tiles[:, :], cmp1[:, :, :], axis=AXX, op=ALU.add))
                step(V.tensor_tensor(cmp2[:, :, :], bc(tiles[:, :], 1, NE), experts_before[:, :, :], ALU.mult))
                step(V.tensor_reduce(first[:, :], cmp2[:, :, :], axis=AXX, op=ALU.add))
                step(V.tensor_tensor(place[:, :, :], run[:, 0:2 * N, :], ps_before[:, :, :], ALU.subtract))
                step(V.scalar_tensor_tensor(place[:, :, :], bc(first[:, :], 1, 2 * N), float(P), place[:, :, :], ALU.mult, ALU.add))
                step(V.tensor_tensor(place[:, :, :], place[:, :, :], chosen[:, :, :], ALU.mult))
                step(V.tensor_reduce(slot_f[:, :], place[:, :, :], axis=AXX, op=ALU.add))
                step(V.tensor_copy(slots[:, :], slot_f[:, :]))
                assert count[0] == PLACED, count[0]
                step(V.tensor_tensor(cmp3[:, :, :], bc(tiles_at[:, :], 2, NE), bc(first[:, :], 1, ET), ALU.is_ge))
                step(V.tensor_reduce(expert_f[:, 0:ET], cmp3[:, :, :], axis=AXX, op=ALU.add))
                step(V.tensor_scalar(expert_f[:, 0:ET], expert_f[:, 0:ET], -1.0, None, ALU.add))
                step(V.tensor_reduce(used[:, :], tiles[:, :], axis=AXX, op=ALU.add))
                step(V.tensor_tensor(cmp4[:, :], used[:, :].to_broadcast([P, ET // 2 - 1]),
                                     tiles_at[:, :].rearrange("p (t u) -> p t u", u=2)[:, 1:, 0], ALU.is_gt))
                step(V.tensor_reduce(expert_f[:, ET:ET + 1], cmp4[:, :], axis=AXX, op=ALU.add))
                step(V.tensor_copy(expert[:, :], expert_f[:, :]))
                assert count[0] == EXPERT, count[0]


def experts(nc, T, keep, h2_rows, slot_token, tile_expert, slot_rows):
    ident = keep["ident"]
    FK, HALF = DE // P, ET // 2

    def last_round(eng):
        return eng.value_load(tile_expert[0:1, ET:ET + 1], min_val=(2 * TOK // P + 1) // 2 - 1, max_val=HALF - 1)

    def tile_of(u, r, last):
        return r + last + 1 if u else r

    def rounds(eng, last, first, body):
        with eng.Fori(first, HALF - 1) as r:
            with eng.If(last > r):
                body(r)

    with Phase(nc, "ex") as ph:
        w1, wd = ph.sb("w1", [P, 2, KT, 2 * DE]), ph.sb("wd", [P, 2, FK, D])
        token = ph.sb("token", [P, 2], U32)
        x, xt = ph.sb("x", [P, 2, D]), ph.sb("xt", [P, KT, P])
        hid, hid_T = ph.sb("hid", [P, 2, DE]), ph.sb("hid_T", [P, FK, P])
        y, zeros = ph.sb("y", [P, 2, D]), ph.sb("zeros", [P, D])
        zeros_ready, zeros_stored = ph.sem("zeros_ready"), ph.sem("zeros_stored")
        ps_x, ps_g = ph.ps("ps_x", [P, KT, P]), ph.ps("ps_g", [P, 2, 2 * DE])
        ps_h, ps_y = ph.ps("ps_h", [P, FK, P]), ph.ps("ps_y", [P, D])
        names = ("turned x_kept gu_done gated hid_done hid_turned hid_kept down_done y_kept passed gather_passed all_stored")
        s = {x_: ph.sem(x_) for x_ in names.split()}
        w1_loaded, wd_loaded, token_loaded, gathered, stored = ([ph.sem(f"{x_}{u}") for u in range(2)] for x_ in (
            "w1_loaded", "wd_loaded", "token_loaded", "gathered", "stored"))
        with nc.Block() as block:
            @block.sync
            def _(sp):
                last = last_round(sp)

                def load_tokens(u, r):
                    wait_apart(sp, s["turned"], r * 2 + u + 1, s["passed"])
                    sp.dma_start(token[:, u:u + 1], slot_token[bass.ds(tile_of(u, r, last) * P, P), :]).then_inc(token_loaded[u], 16)

                def expert_of(tile):
                    return sp.value_load(tile_expert[0:1, bass.ds(tile, 1)], min_val=0, max_val=NE - 1)

                def unless_held(u, r, load, skip):
                    e = expert_of(tile_of(u, r, last))
                    if isinstance(r, int) and r == 0:
                        load(e)
                        return
                    with sp.If(e != expert_of(tile_of(u, r, last) - 1)):
                        load(e)
                    with sp.Else():
                        skip()

                def load_w1(u, r):
                    def load(e):
                        for x_, name in enumerate(("exp_wg", "exp_wu")):
                            sp.dma_start(w1[:, u, :, x_ * DE:(x_ + 1) * DE],
                                         T[name][bass.ds(e, 1), :, :].squeeze(0).rearrange("(p k) f -> p k f", k=KT)).then_inc(w1_loaded[u], 16)

                    wait_apart(sp, s["gu_done"], r * 2 + u + 1, s["passed"])
                    unless_held(u, r, load, lambda: sp.sem_inc(w1_loaded[u], 32))

                def load_wd(u, r):
                    def load(e):
                        sp.dma_start(wd[:, u, :, :], T["exp_wd"][bass.ds(e, 1), :, :].squeeze(0).rearrange("(p k) d -> p k d", k=FK)
                                     ).then_inc(wd_loaded[u], 16)

                    wait_apart(sp, s["down_done"], r * 2 + u + 1, s["passed"])
                    unless_held(u, r, load, lambda: sp.sem_inc(wd_loaded[u], 16))

                def both(r):
                    load_w1(1, r)
                    load_tokens(0, r + 1)
                    load_wd(0, r)
                    load_w1(0, r + 1)
                    load_tokens(1, r + 1)
                    load_wd(1, r)

                load_tokens(0, 0)
                load_w1(0, 0)
                load_tokens(1, 0)
                both(0)
                rounds(sp, last, 1, both)
                load_w1(1, last)
                load_wd(0, last)
                load_wd(1, last)
                sp.wait_ge(zeros_ready, 1)
                with sp.Fori(1, HALF) as r:
                    with sp.If(r > last):
                        for u in range(2):
                            sp.dma_start(slot_rows[bass.ds((r * 2 + u) * P, P), :], zeros[:, :]).then_inc(zeros_stored, 16)
                    with sp.Else():
                        sp.sem_inc(zeros_stored, 32)
                sp.wait_ge(zeros_stored, (HALF - 1) * 32)

            @block.gpsimd
            def _(pool):
                nc.gpsimd.memset(zeros[:, :], 0.0).then_inc(zeros_ready, 1)
                pool.wait_ge(keep["h2_stored"][0], 16 + 16 * (NT // 2 + 1))
                pool.wait_ge(keep["h2_stored"][1], 16 + 16 * (NT // 2))
                last = last_round(pool)

                def gather(u, r):
                    wait_apart(pool, token_loaded[u], r * 16 + 16, s["gather_passed"])
                    nc.gpsimd.indirect_dma_start(x[:, u, :], None, h2_rows,
                                                 bass.IndirectOffsetOnAxis(ap=token[:, u:u + 1], axis=0)).then_inc(gathered[u], 16)

                def both(r):
                    gather(0, r)
                    gather(1, r)

                rounds(pool, last, 0, both)
                both(last)

            @block.tensor
            def _(pe):
                last = last_round(pe)
                pe.sem_inc(s["turned"], 2)
                pe.sem_inc(s["gu_done"], 2)
                pe.sem_inc(s["down_done"], 2)

                def turn(i, u, r):
                    pe.wait_ge(gathered[u], r * 16 + 16)
                    pe.wait_ge(s["x_kept"], i + 1)
                    for k in range(KT):
                        final = nc.tensor.transpose(ps_x[:, k, :], x[:, u, :].rearrange("t (p k) -> t k p", k=KT)[:, k, :], ident[:, :])
                    final.then_inc(s["turned"], 1)

                def gate_up(i, u, r):
                    pe.wait_ge(w1_loaded[u], r * 32 + 32)
                    pe.wait_ge(s["x_kept"], i + 2)
                    pe.wait_ge(s["hid_done"], i + 1)
                    for k in range(KT):
                        final = nc.tensor.matmul(ps_g[:, u, :], xt[:, k, :], w1[:, u, k, :], start=(k == 0), stop=(k == KT - 1))
                    final.then_inc(s["gu_done"], 1)

                def turn_hidden(i, u, r):
                    pe.wait_ge(s["hid_done"], i + 3)
                    pe.wait_ge(s["hid_kept"], i + 1)
                    for k in range(FK):
                        final = nc.tensor.transpose(ps_h[:, k, :], hid[:, u, :].rearrange("t (p k) -> t k p", k=FK)[:, k, :], ident[:, :])
                    final.then_inc(s["hid_turned"], 1)

                def down(i, u, r):
                    pe.wait_ge(wd_loaded[u], r * 16 + 16)
                    pe.wait_ge(s["hid_kept"], i + 2)
                    pe.wait_ge(s["y_kept"], i + 1)
                    for lo in range(0, D, 512):
                        for k in range(FK):
                            final = nc.tensor.matmul(ps_y[:, lo:lo + 512], hid_T[:, k, :], wd[:, u, k, lo:lo + 512],
                                                    start=(k == 0), stop=(k == FK - 1))
                    final.then_inc(s["down_done"], 1)

                turn(0, 0, 0)
                gate_up(0, 0, 0)
                turn(1, 1, 0)
                turn_hidden(0, 0, 0)
                gate_up(1, 1, 0)

                def both(r):
                    for u in range(2):
                        i = r * 2 + u
                        turn(i + 2, u, r + 1)
                        down(i, u, r)
                        turn_hidden(i + 1, (u + 1) % 2, r + u)
                        gate_up(i + 2, u, r + 1)

                rounds(pe, last, 0, both)
                down(last * 2, 0, last)
                turn_hidden(last * 2 + 1, 1, last)
                down(last * 2 + 1, 1, last)

            @block.scalar
            def _(act):
                last = last_round(act)
                act.sem_inc(s["y_kept"], 1)
                for u in range(2):
                    act.sem_inc(stored[u], 16)

                def front(i, u, r):
                    act.wait_ge(s["gu_done"], i + 3)
                    act.wait_ge(s["hid_turned"], i + 1)
                    nc.scalar.activation(hid[:, u, :], ps_g[:, u, 0:DE], ACT.Silu).then_inc(s["gated"], 1)

                def back(i, u, r):
                    act.wait_ge(s["down_done"], i + 3)
                    act.wait_ge(stored[u], r * 16 + 16)
                    nc.scalar.activation(y[:, u, :], ps_y[:, :], ACT.Copy).then_inc(s["y_kept"], 1)
                    act.wait_ge(s["y_kept"], i + 2)
                    act.dma_start(slot_rows[bass.ds(tile_of(u, r, last) * P, P), :], y[:, u, :]).then_inc(stored[u], 16)

                def both(r):
                    for u in range(2):
                        back(r * 2 + u, u, r)
                        front(r * 2 + u + 2, u, r + 1)

                front(0, 0, 0)
                front(1, 1, 0)
                rounds(act, last, 0, both)
                back(last * 2, 0, last)
                back(last * 2 + 1, 1, last)
                for u in range(2):
                    wait_apart(act, stored[u], last * 16 + 32, s["all_stored"])

            @block.vector
            def _(dve):
                last = last_round(dve)
                dve.sem_inc(s["x_kept"], 1)
                dve.sem_inc(s["hid_done"], 2)
                dve.sem_inc(s["hid_kept"], 1)
                dve.sem_inc(s["hid_turned"], 2)

                def keep_x(i):
                    dve.wait_ge(s["turned"], i + 3)
                    dve.wait_ge(s["gu_done"], i + 2)
                    nc.vector.tensor_copy(xt[:, :, :], ps_x[:, :, :]).then_inc(s["x_kept"], 1)

                def up(i, u):
                    dve.wait_ge(s["gated"], i + 1)
                    nc.vector.tensor_tensor(hid[:, u, :], hid[:, u, :], ps_g[:, u, DE:], ALU.mult).then_inc(s["hid_done"], 1)

                def keep_hidden(i):
                    dve.wait_ge(s["hid_turned"], i + 3)
                    dve.wait_ge(s["down_done"], i + 2)
                    nc.vector.tensor_copy(hid_T[:, :, :], ps_h[:, :, :]).then_inc(s["hid_kept"], 1)

                keep_x(0)
                up(0, 0)

                def step(i, u):
                    keep_x(i + 1)
                    keep_hidden(i)
                    up(i + 1, (u + 1) % 2)

                def both(r):
                    step(r * 2, 0)
                    step(r * 2 + 1, 1)

                rounds(dve, last, 0, both)
                step(last * 2, 0)
                keep_hidden(last * 2 + 1)


def combine(nc, T, keep, mod_rows, slot_rows):
    x1, slots, gates = keep["x1"], keep["slots"], keep["gates"]
    with Phase(nc, "cb") as ph:
        rows0, rows1 = ph.sb("rows0", [P, 2, D]), ph.sb("rows1", [P, 2, D])
        gate = {"p": ph.sb("gate_p", [P, D]), "s": ph.sb("gate_s", [NS, D])}
        final = ph.sb("final", [P, D])
        squares, y, mixed = (ph.sb(x_, [P, 2, D]) for x_ in ("squares", "y", "mixed"))
        ss, ms, rt, rstd = (ph.sb(x_, [P, 2]) for x_ in ("ss", "ms", "rt", "rstd"))
        names = "loaded sampled_loaded weighted added mixed summed sq_done ms_done rt_done rstd_done y_done"
        s = {x_: ph.sem(x_) for x_ in names.split()}
        gathered, stored = ([ph.sem(f"{x_}{u}") for u in range(2)] for x_ in ("gathered", "stored"))
        y_tiles = T["y_prompt"].rearrange("(n p) d -> n p d", p=P)
        with nc.Block() as block:
            @block.gpsimd
            def _(pool):
                pool.sem_inc(s["summed"], 2)

                def gather(n):
                    m, u = rows_of(n), n % 2
                    for c, rows in enumerate((rows0, rows1)):
                        nc.gpsimd.indirect_dma_start(rows[0:m, u, :], None, slot_rows, bass.IndirectOffsetOnAxis(
                            ap=slots[0:m, n * 2 + c:n * 2 + c + 1], axis=0)).then_inc(gathered[u], 16)

                gather(0)
                gather(1)
                load_mod_sampled(pool, gate["s"], mod_rows, 5, s["sampled_loaded"])
                for n in range(NT + 1):
                    m, u = rows_of(n), n % 2
                    pool.wait_ge(s["mixed"], n + 1)
                    if n + 2 <= NT:
                        gather(n + 2)
                    nc.gpsimd.tensor_tensor(x1[0:m, n, :], x1[0:m, n, :], mixed[0:m, u, :], ALU.add).then_inc(s["summed"], 1)

            @block.sync
            def _(sp):
                load_mod(sp, gate["p"], mod_rows, 5, s["loaded"])
                sp.dma_start(final[:, :], T["final_g"].to_broadcast([P, D])).then_inc(s["loaded"], 16)
                for u in range(2):
                    sp.sem_inc(stored[u], 16)

                def store(n, u, r):
                    sp.wait_ge(s["y_done"], n + 1)
                    out = T["y_sample"] if rows_of(n) == NS else y_tiles[bass.ds(n, 1), :, :].squeeze(0)
                    sp.dma_start(out, y[0:rows_of(n), u, :]).then_inc(stored[u], 16)

                each(sp, NT + 1, store)
                sp.wait_ge(stored[0], 16 + 16 * (NT // 2 + 1))
                sp.wait_ge(stored[1], 16 + 16 * (NT // 2))

            @block.scalar
            def _(act):
                nc.scalar.preload_act_table(ACT.Sqrt)

                def weigh(n, u, r):
                    m = rows_of(n)
                    a = rows0[0:m, u, :]
                    act.wait_ge(gathered[u], r * 32 + 32)
                    nc.scalar.activation(a, a, ACT.Copy, scale=gates[0:m, bass.ds(n, 1), 0:1].squeeze(1)).then_inc(s["weighted"], 1)

                def stats(n, u, r):
                    m = rows_of(n)
                    act.wait_ge(s["summed"], n + 3)
                    nc.scalar.activation(squares[0:m, u, :], x1[0:m, bass.ds(n, 1), :].squeeze(1), ACT.Square,
                                         accum_out=ss[0:m, u:u + 1]).then_inc(s["sq_done"], 1)
                    act.wait_ge(s["ms_done"], n + 1)
                    nc.scalar.activation(rt[0:m, u:u + 1], ms[0:m, u:u + 1], ACT.Sqrt).then_inc(s["rt_done"], 1)

                ahead(act, NT + 1, weigh, stats)

            @block.vector
            def _(dve):
                dve.wait_ge(s["loaded"], 32)

                def add(n, u, r):
                    m = rows_of(n)
                    group = "s" if m == NS else "p"
                    if group == "s":
                        dve.wait_ge(s["sampled_loaded"], SB * 16)
                    a, b = rows0[0:m, u, :], rows1[0:m, u, :]
                    g1 = gates[0:m, bass.ds(n, 1), 1:2].squeeze(1)
                    dve.wait_ge(s["weighted"], n + 1)
                    nc.vector.scalar_tensor_tensor(a, b, g1, a, ALU.mult, ALU.add).then_inc(s["added"], 1)
                    dve.wait_ge(s["added"], n + 1)
                    dve.wait_ge(s["summed"], n + 1)
                    nc.vector.tensor_tensor(mixed[0:m, u, :], a, gate[group][0:m, :], ALU.mult).then_inc(s["mixed"], 1)

                def norm(n, u, r):
                    m = rows_of(n)
                    x = x1[0:m, bass.ds(n, 1), :].squeeze(1)
                    dve.wait_ge(s["sq_done"], n + 1)
                    nc.vector.tensor_scalar(ms[0:m, u:u + 1], ss[0:m, u:u + 1], 1.0 / D, RMS_EPS,
                                            ALU.mult, ALU.add).then_inc(s["ms_done"], 1)
                    dve.wait_ge(s["rt_done"], n + 1)
                    nc.vector.reciprocal(rstd[0:m, u:u + 1], rt[0:m, u:u + 1]).then_inc(s["rstd_done"], 1)
                    dve.wait_ge(s["rstd_done"], n + 1)
                    dve.wait_ge(stored[u], r * 16 + 16)
                    nc.vector.scalar_tensor_tensor(y[0:m, u, :], x, rstd[0:m, u:u + 1], final[0:m, :],
                                                   ALU.mult, ALU.mult).then_inc(s["y_done"], 1)

                ahead(dve, NT + 1, add, norm)


def build(nc, T, scratch):
    keep = {}
    mod_rows = scratch("mod_rows", [SB + 1, 6 * D])
    h2_rows, slot_rows = scratch("h2_rows", [TOK, D]), scratch("slot_rows", [ET * P, D])
    slot_token, tile_expert = scratch("slot_token", [ET * P, 1], U32), scratch("tile_expert", [1, ET + 1], I32)
    with Phase(nc, "all") as whole:
        for name in ("ident", "head_ones", "neg_from", "neg_ones"):
            keep[name] = whole.sb(name, [P, P])
        keep["mT"] = whole.sb("mT", [P, KT, TOK])
        keep["c_T"] = whole.sb("c_T", [P, KT, SB + 1])
        keep["v_stored"], keep["h2_stored"] = whole.sem("v_stored"), [whole.sem(f"h2_stored{u}") for u in range(2)]
        keep["wv_loaded"], keep["x_loaded"] = whole.sem("wv_loaded"), [whole.sem(f"x_loaded{u}") for u in range(2)]
        with Phase(nc, "rwkv") as rw:
            keep["R"] = rw.sb("R", [P, RF, TOK])
            modulation(nc, T, keep, mod_rows)
            with Phase(nc, "kv") as kv:
                keep["v_new"] = kv.sb("v_new", [NS, SBW])
                keep["qs"] = kv.sb("qs", [P, SH // 2, NS])
                keep["ks"] = kv.sb("ks", [P, SH // 2, NS])
                with Phase(nc, "mix") as mix:
                    keep["hT"] = mix.sb("hT", [P, KT, TOK])
                    keep["v_sb"] = mix.sb("v_sb", [P, NT + 1, SBW])
                    keep["v_g"] = mix.sb("v_g", [P, NT + 1, GW])
                    keep["w_u_loaded"] = mix.sem("w_u_loaded")
                    norm1(nc, T, keep, mod_rows)
                    gated_mlp(nc, T, keep)
                    rwkv_project(nc, T, keep)
                    attention(nc, T, keep)
                sampled_attention(nc, T, keep)
            keep["B"] = rw.sb("B", [P, 4, 2, TOK])
            keep["ends"] = rw.sb("ends", [P, 2, NC + SB])
            keep["rwkv_g"], keep["bonus"] = rw.sb("g", [P, 2, TOK]), rw.sb("bonus", [P, 2, TOK])
            keep["masks"] = {x_: rw.sb(f"mask_{x_}", [P, 3, C]) for x_ in "ps"}
            keep["blocks"] = {x_: rw.sb(f"blocks_{x_}", [P, 2, 2, C]) for x_ in "ps"}
            keep["own"] = rw.sb("own", [P, SB])
            keep["I2"] = rw.sb("I2", [P, C])
            rwkv_prepare(nc, T, keep, mod_rows)
            rwkv_chunks(nc, T, keep)
        keep["x1"] = whole.sb("x1", [P, NT + 1, D])
        keep["logits"] = whole.sb("logits", [P, NT + 1, NGR + NE])
        keep["slots"] = whole.sb("slots", [P, 2 * (NT + 1)], U32)
        keep["gates"] = whole.sb("gates", [P, NT + 1, 2])
        out_project(nc, T, keep, mod_rows, h2_rows)
        route(nc, T, keep, slot_token, tile_expert)
        experts(nc, T, keep, h2_rows, slot_token, tile_expert, slot_rows)
        combine(nc, T, keep, mod_rows, slot_rows)


INPUTS = ['x_prompt', 'x_sample', 'cache_k', 'cache_v', 'page_table', 'state_rwkv', 'state_rwkv_shift', 'c_prompt',
          'c_sample', 'norm1_g', 'norm2_g', 'w_mod', 'b_mod', 'w_in', 'rwkv_mu', 'rwkv_w0', 'rwkv_w_up', 'rwkv_a0',
          'rwkv_a_up', 'rwkv_g_up', 'rwkv_k_k', 'rwkv_k_a', 'rwkv_r_k', 'rwkv_ln_g', 'rwkv_ln_b', 'gmlp_ln_g',
          'gmlp_ln_b', 'gmlp_ws', 'gmlp_bs', 'sb_bias', 'w_out', 'router_g_w', 'router_g_b', 'router_e_w',
          'router_e_b', 'exp_wg', 'exp_wu', 'exp_wd', 'final_g']
SHAPES = {'x_prompt': (SEQ, D), 'x_sample': (NS, D), 'cache_k': (80, PAGE, SBW), 'cache_v': (80, PAGE, SBW),
          'page_table': (1, SB * NPAGE), 'state_rwkv': (SB, RH, HD, HD), 'state_rwkv_shift': (SB, RPROJ),
          'final_g': (1, D), 'w_mod': (D, 6 * D), 'w_in': (D, 2944), 'w_out': (D, D), 'rwkv_w_up': (32, RW),
          'rwkv_a_up': (32, RW), 'rwkv_g_up': (64, RW), 'rwkv_r_k': (1, RW), 'gmlp_ws': (GG, P, P),
          'gmlp_bs': (GG, P), 'router_g_w': (D, 4), 'router_e_w': (D, NE), 'exp_wg': (NE, D, DE),
          'exp_wu': (NE, D, DE), 'exp_wd': (NE, DE, D)}
OUTPUTS = [('y_prompt', (SEQ, D), (1, SEQ, D)), ('y_sample', (NS, D), (SB, ST, D)),
           ('k_prompt', (SEQ, SBW), (1, 1, SEQ, SH, HD)), ('v_prompt', (SEQ, SBW), (1, 1, SEQ, SH, HD)),
           ('k_sample', (NS, SBW), (1, SB, ST, SH, HD)), ('v_sample', (NS, SBW), (1, SB, ST, SH, HD)),
           ('S_prompt', (RH, HD, HD), (1, 1, RH, HD, HD)), ('shift_prompt', (1, RPROJ), (1, 1, RPROJ)),
           ('S_sample', (SB, RH, HD, HD), (1, SB, RH, HD, HD)), ('shift_sample', (SB, RPROJ), (1, SB, RPROJ)),
           ('g_v_sample', (NS, GW), (1, SB, ST, GW))]


def program(nc, inputs):
    arrays, T = {}, {}
    for name in INPUTS:
        a = np.ascontiguousarray(inputs[name])
        a = a.reshape(SHAPES.get(name, a.shape))
        arrays[f"in_{name}"] = a
        T[name] = nc.dram_tensor(f"in_{name}", a.shape, mybir.dt.from_np(a.dtype), kind="ExternalInput").ap()
    for name, shape, _ in OUTPUTS:
        T[name] = nc.dram_tensor(f"out_{name}", shape, F32, kind="ExternalOutput").ap()

    def scratch(name, shape, dt=F32):
        return nc.dram_tensor(name, tuple(shape), dt, kind="Internal").ap()

    build(nc, T, scratch)
    return arrays


def kernel(**inputs):
    import concourse.bacc as bacc
    from concourse.bass_utils import run_bass_kernel_spmd

    nc = bacc.Bacc("TRN2", target_bir_lowering=False, num_devices=1)
    arrays = program(nc, inputs)
    got = run_bass_kernel_spmd(nc, [arrays], core_ids=[0]).results[0]
    return tuple(got[f"out_{name}"].reshape(shape) for name, _, shape in OUTPUTS)
```
